# Optimizing a Trainium2 kernel written in Bass

```python
import math
import jax, jax.numpy as jnp
from jax import lax
import numpy as np

D_MODEL = 1024
BATCH = 1
SEQ = 256
DEPTH = 1

MEM_LEN = 256
EPS = 1e-6
DA_HEADS = 4
DA_QK_DIM = 64
DA_V_DIM = 2 * DA_QK_DIM
DA_WIDTH = DA_HEADS * DA_V_DIM
QK_WIDTH = DA_HEADS * 2 * DA_QK_DIM
POOL_WINDOWS = (2, 4, 8, 16)
POOL_GROUPS = len(POOL_WINDOWS)
POOL_WIDTH = D_MODEL - DA_WIDTH
POOL_GROUP_DIM = POOL_WIDTH // POOL_GROUPS
MIX_WIDTH = DA_WIDTH + POOL_WIDTH
IN_WIDTH = 2 * QK_WIDTH + DA_WIDTH + POOL_WIDTH
ROPE_THETA = 500000.0
ROPE_DIM = DA_QK_DIM // 4
BLOCK_Q = 128
X_HEADS = 4
X_HEAD_DIM = D_MODEL // X_HEADS
D_FF = -(-(8 * D_MODEL) // (3 * 256)) * 256
def _lambda_init(layer_idx):
    return 0.8 - 0.6 * math.exp(-0.3 * (layer_idx - 1))


def rmsnorm(x, g):
    xf = x.astype(jnp.float32)
    y = xf * lax.rsqrt(jnp.mean(xf * xf, axis=-1, keepdims=True) + EPS)
    return (y * g.astype(jnp.float32)).astype(x.dtype)

def rope_tables(positions, dtype):
    inv_freq = ROPE_THETA ** (-jnp.arange(0, ROPE_DIM, 2, dtype=jnp.float32) / ROPE_DIM)
    ang = positions.astype(jnp.float32)[..., None] * inv_freq
    return jnp.cos(ang).astype(dtype), jnp.sin(ang).astype(dtype)

def apply_partial_rope(t, cos, sin):
    cos = cos[:, :, None, None, :]
    sin = sin[:, :, None, None, :]
    half = ROPE_DIM // 2
    t1 = t[..., :half]
    t2 = t[..., half:ROPE_DIM]
    rest = t[..., ROPE_DIM:]
    return jnp.concatenate([t1 * cos - t2 * sin, t2 * cos + t1 * sin, rest], axis=-1)

def diff_attention(q, k, v, lam):
    seq = q.shape[3]
    scale = DA_QK_DIM ** -0.5
    outs = []
    for i in range(seq // BLOCK_Q):
        q0 = i * BLOCK_Q
        kend = q0 + BLOCK_Q
        qb = q[:, :, :, q0:kend]
        kb = k[:, :, :, :kend]
        vb = v[:, :, :kend]
        s = jnp.einsum('bhmqd,bhmkd->bhmqk', qb, kb).astype(jnp.float32) * scale
        mask = (q0 + jnp.arange(BLOCK_Q))[:, None] >= jnp.arange(kend)[None, :]
        s = jnp.where(mask, s, -jnp.inf)
        p = jax.nn.softmax(s, axis=-1)
        a = p[:, :, 0] - lam * p[:, :, 1]
        outs.append(jnp.einsum('bhqk,bhkd->bhqd', a.astype(v.dtype), vb))
    return jnp.concatenate(outs, axis=2)

def causal_multiscale_pool(u):
    b, s, _ = u.shape
    uf = u.astype(jnp.float32).reshape(b, s, POOL_GROUPS, POOL_GROUP_DIM)
    c = jnp.cumsum(uf, axis=1)
    t1 = jnp.arange(1, s + 1, dtype=jnp.float32)
    groups = []
    for g, w in enumerate(POOL_WINDOWS):
        cg = c[:, :, g]
        shifted = jnp.pad(cg, ((0, 0), (w, 0), (0, 0)))[:, :s]
        count = jnp.minimum(t1, float(w))[None, :, None]
        groups.append((cg - shifted) / count - uf[:, :, g])
    return jnp.stack(groups, axis=2).astype(u.dtype)

def first_inputs(seed: int = 0) -> dict:
    key = jax.random.key(seed)
    ks = jax.random.split(key, 32)
    f32 = jnp.float32

    def w(k, shape, fan_in):
        return jax.random.normal(k, shape, f32) * (fan_in ** -0.5)

    def gain(k, n):
        return 1.0 + 0.02 * jax.random.normal(k, (n,), f32)

    return {
        "x": jax.random.normal(ks[0], (BATCH, SEQ, D_MODEL), f32),
        "mem": jax.random.normal(ks[1], (BATCH, MEM_LEN, D_MODEL), f32),
        "positions": jnp.broadcast_to(jnp.arange(SEQ, dtype=jnp.int32), (BATCH, SEQ)),
        "g_mix_pre": gain(ks[2], D_MODEL),
        "w_in": w(ks[3], (D_MODEL, IN_WIDTH), D_MODEL),
        "lambda_q1": 0.1 * jax.random.normal(ks[4], (DA_QK_DIM,), f32),
        "lambda_k1": 0.1 * jax.random.normal(ks[5], (DA_QK_DIM,), f32),
        "lambda_q2": 0.1 * jax.random.normal(ks[6], (DA_QK_DIM,), f32),
        "lambda_k2": 0.1 * jax.random.normal(ks[7], (DA_QK_DIM,), f32),
        "g_subln": gain(ks[8], DA_V_DIM),
        "w_pool": w(ks[9], (POOL_GROUPS, POOL_GROUP_DIM, POOL_GROUP_DIM), POOL_GROUP_DIM),
        "pool_scale": 1.0 + 0.1 * jax.random.normal(ks[10], (POOL_WIDTH,), f32),
        "w_out": w(ks[11], (MIX_WIDTH, D_MODEL), MIX_WIDTH),
        "g_mix_post": gain(ks[12], D_MODEL),
        "g_x_pre": gain(ks[13], D_MODEL),
        "g_mem": gain(ks[14], D_MODEL),
        "w_xq": w(ks[15], (D_MODEL, X_HEADS * X_HEAD_DIM), D_MODEL),
        "w_xkv": w(ks[16], (D_MODEL, 2 * X_HEADS * X_HEAD_DIM), D_MODEL),
        "w_xo": w(ks[17], (X_HEADS * X_HEAD_DIM, D_MODEL), X_HEADS * X_HEAD_DIM),
        "g_x_post": gain(ks[18], D_MODEL),
        "g_ffn_pre": gain(ks[19], D_MODEL),
        "w_gate": w(ks[20], (D_MODEL, D_FF), D_MODEL),
        "w_up": w(ks[21], (D_MODEL, D_FF), D_MODEL),
        "w_down": w(ks[22], (D_FF, D_MODEL), D_FF),
        "g_ffn_post": gain(ks[23], D_MODEL),
    }

def first_block(x, mem, positions, g_mix_pre, w_in, lambda_q1, lambda_k1, lambda_q2,
              lambda_k2, g_subln, w_pool, pool_scale, w_out, g_mix_post, g_x_pre,
              g_mem, w_xq, w_xkv, w_xo, g_x_post, g_ffn_pre, w_gate, w_up, w_down,
              g_ffn_post):
    b, s, _ = x.shape
    cos, sin = rope_tables(positions, x.dtype)
    mem_n = rmsnorm(mem, g_mem)

    for layer in range(DEPTH):
        lam_init = _lambda_init(layer + 1)

        h = rmsnorm(x, g_mix_pre)
        proj = h @ w_in
        q = proj[..., :QK_WIDTH].reshape(b, s, DA_HEADS, 2, DA_QK_DIM)
        k = proj[..., QK_WIDTH:2 * QK_WIDTH].reshape(b, s, DA_HEADS, 2, DA_QK_DIM)
        v = proj[..., 2 * QK_WIDTH:2 * QK_WIDTH + DA_WIDTH].reshape(b, s, DA_HEADS, DA_V_DIM)
        u = proj[..., 2 * QK_WIDTH + DA_WIDTH:]

        q = apply_partial_rope(q, cos, sin).transpose(0, 2, 3, 1, 4)
        k = apply_partial_rope(k, cos, sin).transpose(0, 2, 3, 1, 4)
        v = v.transpose(0, 2, 1, 3)
        lam = (jnp.exp(jnp.sum(lambda_q1.astype(jnp.float32) * lambda_k1.astype(jnp.float32)))
               - jnp.exp(jnp.sum(lambda_q2.astype(jnp.float32) * lambda_k2.astype(jnp.float32)))
               + lam_init)
        da = diff_attention(q, k, v, lam)
        da = rmsnorm(da, g_subln) * (1.0 - lam_init)
        da = da.transpose(0, 2, 1, 3).reshape(b, s, DA_WIDTH)

        pooled = causal_multiscale_pool(u)
        po = jnp.einsum('bsgc,gcd->bsgd', pooled, w_pool).reshape(b, s, POOL_WIDTH)
        po = po * pool_scale

        mix = jnp.concatenate([da, po], axis=-1) @ w_out
        x = x + rmsnorm(mix, g_mix_post)

        hq = rmsnorm(x, g_x_pre)
        xq = (hq @ w_xq).reshape(b, s, X_HEADS, X_HEAD_DIM)
        kv = (mem_n @ w_xkv).reshape(b, MEM_LEN, 2, X_HEADS, X_HEAD_DIM)
        sc = jnp.einsum('bshd,bmhd->bhsm', xq, kv[:, :, 0]).astype(jnp.float32) * (X_HEAD_DIM ** -0.5)
        pm = jax.nn.softmax(sc, axis=-1).astype(x.dtype)
        xo = jnp.einsum('bhsm,bmhd->bshd', pm, kv[:, :, 1]).reshape(b, s, X_HEADS * X_HEAD_DIM)
        x = x + rmsnorm(xo @ w_xo, g_x_post)

        hf = rmsnorm(x, g_ffn_pre)
        ff = (jax.nn.silu(hf @ w_gate) * (hf @ w_up)) @ w_down
        x = x + rmsnorm(ff, g_ffn_post)

    return x


DEPTH_2 = 2

CHUNK = 64
N_MEM = 256
HEAD_DIM = 64
MIX_WIDTH_2 = (D_MODEL * 3) // 4
N_MIX_HEADS = MIX_WIDTH_2 // HEAD_DIM
MEM_WIDTH = D_MODEL - MIX_WIDTH_2
N_MEM_HEADS = MEM_WIDTH // HEAD_DIM
D_FF_2 = 2816
DECAY_LORA = 64
AAA_LORA = 64
GATE_LORA = 128
Q_BLOCK = 128
N_MIXERS = 2
N_RWKV = (DEPTH_2 + 1) // 2
N_SB = DEPTH_2 // 2
ALPHA = (2 * DEPTH_2) ** 0.25
BETA = (8 * DEPTH_2) ** -0.25
LN_EPS = 1e-5
LNX_EPS = 64e-5
RWKV_SHIFT = 3 * MIX_WIDTH_2 + DECAY_LORA + AAA_LORA + GATE_LORA
RWKV_IN = RWKV_SHIFT + MEM_WIDTH
SB_IN = 3 * MIX_WIDTH_2 + MEM_WIDTH


def layer_norm(x, g, b):
    xf = x.astype(jnp.float32)
    mu = jnp.mean(xf, axis=-1, keepdims=True)
    var = jnp.mean(jnp.square(xf - mu), axis=-1, keepdims=True)
    return ((xf - mu) * lax.rsqrt(var + LN_EPS) * g + b).astype(x.dtype)

def swiglu(x, w_gate, w_up, w_down):
    return (jax.nn.silu(x @ w_gate) * (x @ w_up)) @ w_down

def split_heads(t):
    b, s, _ = t.shape
    return t.reshape(b, s, -1, HEAD_DIM).transpose(0, 2, 1, 3)

def merge_heads(t):
    b, h, s, d = t.shape
    return t.transpose(0, 2, 1, 3).reshape(b, s, h * d)

def token_shift(p, mu):
    prev = jnp.pad(p, ((0, 0), (1, 0), (0, 0)))[:, :-1]
    return p + (prev - p) * mu

def memory_attention(mq, mem_k, mem_v):
    q = split_heads(mq)
    scores = jnp.einsum('bhsd,bhmd->bhsm', q, mem_k).astype(jnp.float32) / math.sqrt(HEAD_DIM)
    p = jax.nn.softmax(scores, axis=-1).astype(mq.dtype)
    return merge_heads(jnp.einsum('bhsm,bhmd->bhsd', p, mem_v))

def rwkv7_mix(z_in, mu, w0, w_up, a0, a_up, g_up, k_k, k_a, r_k, lnx_g, lnx_b):
    bsz, seq, _ = z_in.shape
    dt = z_in.dtype
    z = token_shift(z_in, mu)
    c = MIX_WIDTH_2
    r = z[..., :c]
    k = z[..., c:2 * c]
    v = z[..., 2 * c:3 * c]
    o = 3 * c
    dw = z[..., o:o + DECAY_LORA]
    o += DECAY_LORA
    da = z[..., o:o + AAA_LORA]
    o += AAA_LORA
    dg = z[..., o:o + GATE_LORA]
    w = -jax.nn.softplus(-(w0 + jnp.tanh(dw) @ w_up)) - 0.5
    a = jax.nn.sigmoid(a0 + da @ a_up)
    g = jax.nn.sigmoid(dg) @ g_up

    def hs(t):
        return t.astype(jnp.float32).reshape(bsz, seq, N_MIX_HEADS, HEAD_DIM)

    kk = hs(k * k_k)
    kk = kk * lax.rsqrt(jnp.maximum(jnp.sum(kk * kk, axis=-1, keepdims=True), 1e-24))
    k = hs(k * (1.0 + (a - 1.0) * k_a))
    r, v, a = hs(r), hs(v), hs(a)
    decay = jnp.exp(-jnp.exp(hs(w)))

    n_chunks = seq // CHUNK

    def to_chunks(t):
        return t.transpose(1, 0, 2, 3).reshape(n_chunks, CHUNK, bsz, N_MIX_HEADS, HEAD_DIM)

    xs = (to_chunks(r), to_chunks(decay), to_chunks(k), to_chunks(v), to_chunks(kk), to_chunks(kk * a))

    def step(state, inp):
        r_t, w_t, k_t, v_t, kk_t, b_t = inp
        sa = jnp.einsum('bhij,bhj->bhi', state, kk_t)
        state = (state * w_t[:, :, None, :] - sa[..., :, None] * b_t[..., None, :]
                 + v_t[..., :, None] * k_t[..., None, :])
        return state, jnp.einsum('bhij,bhj->bhi', state, r_t)

    def chunk_step(state, chunk_inp):
        return lax.scan(step, state, chunk_inp)

    state0 = jnp.zeros((bsz, N_MIX_HEADS, HEAD_DIM, HEAD_DIM), jnp.float32)
    _, out = lax.scan(chunk_step, state0, xs)
    out = out.reshape(seq, bsz, N_MIX_HEADS, HEAD_DIM).transpose(1, 0, 2, 3)
    m = jnp.mean(out, axis=-1, keepdims=True)
    var = jnp.mean(jnp.square(out - m), axis=-1, keepdims=True)
    out = ((out - m) * lax.rsqrt(var + LNX_EPS)).reshape(bsz, seq, c) * lnx_g + lnx_b
    bonus = jnp.sum(r * k * r_k, axis=-1, keepdims=True) * v
    y = (out + bonus.reshape(bsz, seq, c)) * g
    return y.astype(dt)

def stick_breaking_mix(q, k, v):
    q, k, v = split_heads(q), split_heads(k), split_heads(v)
    seq = q.shape[2]
    scale = 1.0 / math.sqrt(HEAD_DIM)
    outs = []
    for blk in range(seq // Q_BLOCK):
        start = blk * Q_BLOCK
        end = start + Q_BLOCK
        kb = k[:, :, :end]
        vb = v[:, :, :end]
        z = jnp.einsum('bhtd,bhsd->bhts', q[:, :, start:end], kb).astype(jnp.float32) * scale
        t_pos = start + jnp.arange(Q_BLOCK)[:, None]
        s_pos = jnp.arange(end)[None, :]
        before = s_pos < t_pos
        log_keep = jnp.where(before, -jax.nn.softplus(z), 0.0)
        later = lax.cumsum(log_keep, axis=3, reverse=True) - log_keep
        att = jnp.where(before, jnp.exp(jax.nn.log_sigmoid(z) + later), 0.0)
        outs.append(jnp.einsum('bhts,bhsd->bhtd', att.astype(v.dtype), vb))
    return merge_heads(jnp.concatenate(outs, axis=2))

def second_inputs(seed: int = 0) -> dict:
    key = jax.random.key(seed)
    ks = jax.random.split(key, 32)
    f32 = jnp.float32
    d, f, c = D_MODEL, D_FF_2, MIX_WIDTH_2

    def nrm(k, shape, scale):
        return jax.random.normal(k, shape, f32) * scale

    return {
        "x": nrm(ks[0], (BATCH, SEQ, d), 1.0),
        "mem": nrm(ks[1], (BATCH, N_MEM, d), 1.0),
        "ffn1_w_gate": nrm(ks[2], (DEPTH_2, d, f), d ** -0.5),
        "ffn1_w_up": nrm(ks[3], (DEPTH_2, d, f), d ** -0.5),
        "ffn1_w_down": nrm(ks[4], (DEPTH_2, f, d), BETA * f ** -0.5),
        "ffn2_w_gate": nrm(ks[5], (DEPTH_2, d, f), d ** -0.5),
        "ffn2_w_up": nrm(ks[6], (DEPTH_2, d, f), d ** -0.5),
        "ffn2_w_down": nrm(ks[7], (DEPTH_2, f, d), BETA * f ** -0.5),
        "ln_g": 1.0 + nrm(ks[8], (DEPTH_2, 3, d), 0.02),
        "ln_b": nrm(ks[9], (DEPTH_2, 3, d), 0.02),
        "w_out": nrm(ks[10], (DEPTH_2, d, d), BETA * d ** -0.5),
        "w_mem_kv": nrm(ks[11], (d, 2 * MEM_WIDTH), d ** -0.5),
        "rwkv_w_in": nrm(ks[12], (N_RWKV, d, RWKV_IN), d ** -0.5),
        "rwkv_mu": jax.random.uniform(ks[13], (N_RWKV, RWKV_SHIFT), f32),
        "rwkv_w0": jax.random.uniform(ks[14], (N_RWKV, c), f32, -6.0, -1.0),
        "rwkv_w_up": nrm(ks[15], (N_RWKV, DECAY_LORA, c), 0.1 * DECAY_LORA ** -0.5),
        "rwkv_a0": nrm(ks[16], (N_RWKV, c), 0.5),
        "rwkv_a_up": nrm(ks[17], (N_RWKV, AAA_LORA, c), 0.5 * AAA_LORA ** -0.5),
        "rwkv_g_up": nrm(ks[18], (N_RWKV, GATE_LORA, c), GATE_LORA ** -0.5),
        "rwkv_k_k": 1.0 + nrm(ks[19], (N_RWKV, c), 0.1),
        "rwkv_k_a": 1.0 + nrm(ks[20], (N_RWKV, c), 0.1),
        "rwkv_r_k": nrm(ks[21], (N_RWKV, N_MIX_HEADS, HEAD_DIM), 0.1),
        "rwkv_lnx_g": 1.0 + nrm(ks[22], (N_RWKV, c), 0.02),
        "rwkv_lnx_b": nrm(ks[23], (N_RWKV, c), 0.02),
        "sb_w_in": nrm(ks[24], (N_SB, d, SB_IN), d ** -0.5),
    }

def second_block(x, mem, ffn1_w_gate, ffn1_w_up, ffn1_w_down, ffn2_w_gate, ffn2_w_up, ffn2_w_down,
              ln_g, ln_b, w_out, w_mem_kv, rwkv_w_in, rwkv_mu, rwkv_w0, rwkv_w_up, rwkv_a0,
              rwkv_a_up, rwkv_g_up, rwkv_k_k, rwkv_k_a, rwkv_r_k, rwkv_lnx_g, rwkv_lnx_b, sb_w_in):
    mem_kv = mem @ w_mem_kv
    mem_k = split_heads(mem_kv[..., :MEM_WIDTH])
    mem_v = split_heads(mem_kv[..., MEM_WIDTH:])
    c = MIX_WIDTH_2
    for i in range(DEPTH_2):
        x = layer_norm(ALPHA * x + 0.5 * swiglu(x, ffn1_w_gate[i], ffn1_w_up[i], ffn1_w_down[i]),
                       ln_g[i, 0], ln_b[i, 0])
        j = i // N_MIXERS
        if i % N_MIXERS == 0:
            proj = x @ rwkv_w_in[j]
            mix = rwkv7_mix(proj[..., :RWKV_SHIFT], rwkv_mu[j], rwkv_w0[j], rwkv_w_up[j],
                            rwkv_a0[j], rwkv_a_up[j], rwkv_g_up[j], rwkv_k_k[j], rwkv_k_a[j],
                            rwkv_r_k[j], rwkv_lnx_g[j], rwkv_lnx_b[j])
            mq = proj[..., RWKV_SHIFT:]
        else:
            proj = x @ sb_w_in[j]
            mix = stick_breaking_mix(proj[..., :c], proj[..., c:2 * c], proj[..., 2 * c:3 * c])
            mq = proj[..., 3 * c:]
        heads = jnp.concatenate([mix, memory_attention(mq, mem_k, mem_v)], axis=-1)
        x = layer_norm(ALPHA * x + heads @ w_out[i], ln_g[i, 1], ln_b[i, 1])
        x = layer_norm(ALPHA * x + 0.5 * swiglu(x, ffn2_w_gate[i], ffn2_w_up[i], ffn2_w_down[i]),
                       ln_g[i, 2], ln_b[i, 2])
    return x


def setup_inputs(seed=0):
    out = dict(first_inputs(seed))
    for name, value in second_inputs(seed + 1).items():
        if name != "x":
            out[name + "_2"] = value
    return out


def reference(
    x, mem, positions, g_mix_pre, w_in, lambda_q1, lambda_k1, lambda_q2, lambda_k2, g_subln,
    w_pool, pool_scale, w_out, g_mix_post, g_x_pre, g_mem, w_xq, w_xkv, w_xo, g_x_post,
    g_ffn_pre, w_gate, w_up, w_down, g_ffn_post, mem_2, ffn1_w_gate_2, ffn1_w_up_2,
    ffn1_w_down_2, ffn2_w_gate_2, ffn2_w_up_2, ffn2_w_down_2, ln_g_2, ln_b_2, w_out_2,
    w_mem_kv_2, rwkv_w_in_2, rwkv_mu_2, rwkv_w0_2, rwkv_w_up_2, rwkv_a0_2, rwkv_a_up_2,
    rwkv_g_up_2, rwkv_k_k_2, rwkv_k_a_2, rwkv_r_k_2, rwkv_lnx_g_2, rwkv_lnx_b_2, sb_w_in_2,
):
    x = first_block(
        x, mem, positions, g_mix_pre, w_in, lambda_q1, lambda_k1, lambda_q2, lambda_k2, g_subln,
        w_pool, pool_scale, w_out, g_mix_post, g_x_pre, g_mem, w_xq, w_xkv, w_xo, g_x_post,
        g_ffn_pre, w_gate, w_up, w_down, g_ffn_post,
    )
    return second_block(
        x, mem_2, ffn1_w_gate_2, ffn1_w_up_2, ffn1_w_down_2, ffn2_w_gate_2, ffn2_w_up_2,
        ffn2_w_down_2, ln_g_2, ln_b_2, w_out_2, w_mem_kv_2, rwkv_w_in_2, rwkv_mu_2, rwkv_w0_2,
        rwkv_w_up_2, rwkv_a0_2, rwkv_a_up_2, rwkv_g_up_2, rwkv_k_k_2, rwkv_k_a_2, rwkv_r_k_2,
        rwkv_lnx_g_2, rwkv_lnx_b_2, sb_w_in_2,
    )


_drawn_inputs = setup_inputs


def setup_inputs(seed=0):
    import zlib

    import numpy as np

    out = dict(_drawn_inputs(seed))
    spreads = {}
    factors = {'lambda_k1': 3.031,
     'lambda_q2': 3.196,
     'g_subln': 4.406,
     'g_mix_post': 3.342,
     'g_x_pre': 3.855,
     'g_mem': 2.754,
     'g_x_post': 4.129,
     'g_ffn_pre': 3.661,
     'g_ffn_post': 5.366,
     'rwkv_w_up_2': 8.0,
     'rwkv_k_k_2': 2.899,
     'rwkv_lnx_g_2': 8.0,
     'rwkv_lnx_b_2': 8.0}
    for name, (base, spread) in spreads.items():
        noise = np.random.default_rng([zlib.crc32(name.encode()), seed]).standard_normal(out[name].shape)
        drawn = base * np.exp(spread * noise) if base else spread * noise
        out[name] = __import__('jax').numpy.asarray(drawn.astype(out[name].dtype))
    for name, factor in factors.items():
        out[name] = (out[name] * factor).astype(out[name].dtype)
    return out
```

```python
import math
from contextlib import ExitStack

import numpy as np
import concourse.bass as bass
from concourse import mybir

F32 = mybir.dt.float32
F32R = mybir.dt.float32r
I32 = mybir.dt.int32
ALU = mybir.AluOpType
ACT = mybir.ActivationFunctionType
AX = mybir.AxisListType

P = 128
T = 256
D = 1024
FF = 2816
NF = FF // P
LAM0 = 0.8 - 0.6 * math.exp(0.0)
EPS = 1e-6
LN_EPS = 1e-5
LNX_EPS = 64e-5
ALPHA = 4.0 ** 0.25
C7 = 768
HC = C7 // P
NEG = -3.0e38

NR, NH = 6, 4
UW = 1024

K_ID, K_AM, K_SU, K_IU, K_M1, K_SL, K_LV = 0, 128, 512, 640, 768, 896, 1024
K_ONE, K_SEL2, K_FREQ, K_HALF, K_BO, K_SELH = 1408, 1536, 1538, 1546, 1570, 1698
NCST = K_SELH + C7

VROWS = [("pool_scale", 4), ("g_subln", 1), ("rwkv_mu_2", 20), ("rwkv_w0_2", 6), ("rwkv_a0_2", 6),
         ("rwkv_k_k_2", 6), ("rwkv_k_a_2", 6), ("rwkv_r_k_2", 6), ("rwkv_lnx_g_2", 6), ("rwkv_lnx_b_2", 6)]
NV = sum(n for _, n in VROWS)


class Lane:

    def __init__(self, engine, sem):
        self.e, self.sem, self.n, self.seen = engine, sem, 0, {}

    def wait(self, *tokens):
        for t in tokens:
            if isinstance(t, list):
                self.wait(*t)
            elif t is not None and self.seen.get(t[0].name, 0) < t[1]:
                self.seen[t[0].name] = t[1]
                self.e.wait_ge(t[0], t[1])

    def go(self, fn, *after):
        self.wait(*after)
        fn(self.e)

    def do(self, fn, *after):
        self.wait(*after)
        self.n += 1
        fn(self.e).then_inc(self.sem, 1)
        return (self.sem, self.n)


class Dmas:

    def __init__(self, sem):
        self.sem, self.n = sem, 0

    def start(self, lane, out, in_, *after, **how):
        lane.wait(*after)
        self.n += 16
        lane.e.dma_start(out, in_, **how).then_inc(self.sem, 16)
        return (self.sem, self.n)


def cols(w, k0, nk, n0, n):
    return w[k0 * P:(k0 + nk) * P, n0:n0 + n].rearrange("(k p) n -> p k n", p=P)


def chunk(name, w, n0, n, nk=8):
    per = UW // n
    return [((name, n0), cols(w, k, per, n0, n), per, n) for k in range(0, nk, per)]


def build_program(nc, I, cst_in, band_in, out, dbg=None):
    es = ExitStack()
    with es:
        sem = lambda n: es.enter_context(nc.semaphore(n))
        sb = lambda n, s, d=F32: es.enter_context(nc.sbuf_tensor(n, s, d))
        pe, act, dve, pool, sp = (
            Lane(e, sem("s_" + n)) for e, n in ((nc.tensor, "pe"), (nc.scalar, "act"), (nc.vector, "dve"),
                                                (nc.gpsimd, "pool"), (nc.sync, "sp")))
        s_raw = [sem(f"s_raw{i}") for i in range(NR)]
        ps = [es.enter_context(nc.psum_tensor(f"ps{i}", [P, 512], F32)) for i in range(8)]
        bf = [[] for _ in range(8)]

        raw = sb("raw", [P, NR, UW])
        wh = sb("wh", [P, NH, UW], F32R)
        wl = sb("wl", [P, NH, UW], F32R)
        x = sb("xres", [P, 2, D])
        gb = sb("gb", [P, 3, D])
        cst = sb("cst", [P, NCST])
        vcol = sb("vcol", [P, NV])
        vrow = sb("vrow", [P, P])
        junk = sb("junk", [P, D])
        st = sb("st", [P, 256])
        mk2 = sb("mk2", [P, 2, T])
        mv2 = sb("mv2", [P, 2, T])
        pos_i = sb("pos_i", [P, 2], I32)

        ident = cst[:, K_ID:K_ID + P]
        C = lambda k, n, p=P: cst[0:p, k:k + n]

        W = {k: v for k, v in I.items()}
        ffn_list = lambda nm, g, u, d: sum(
            [chunk(nm + "g", g, n, min(512, FF - n)) + chunk(nm + "u", u, n, min(512, FF - n))
             for n in range(0, FF, 512)], []) + chunk(nm + "d", d, 0, D, NF)
        plan = []
        for n in range(4):
            plan += chunk("w_in", I["w_in"], 512 * n, 512)
        for n in range(4):
            plan += chunk("w_xkv", I["w_xkv"], 512 * n, 512)
        plan += chunk("w_out", I["w_out"], 0, D)
        for n in range(2):
            plan += chunk("w_xq", I["w_xq"], 512 * n, 512)
        plan += chunk("w_xo", I["w_xo"], 0, D)
        plan += ffn_list("f0", I["w_gate"], I["w_up"], I["w_down"])
        plan += chunk("mkv", I["w_mem_kv_2"], 0, 256) + chunk("mkv", I["w_mem_kv_2"], 256, 256)
        plan += ffn_list("f1", I["ffn1_w_gate_2"][0], I["ffn1_w_up_2"][0], I["ffn1_w_down_2"][0])
        for n in range(5):
            plan += chunk("rw", I["rwkv_w_in_2"][0], 512 * n, 512)
        plan += chunk("rw", I["rwkv_w_in_2"][0], 2560, 256)
        plan += chunk("wo0", I["w_out_2"][0], 0, D)
        plan += ffn_list("f2", I["ffn2_w_gate_2"][0], I["ffn2_w_up_2"][0], I["ffn2_w_down_2"][0])
        plan += ffn_list("f3", I["ffn1_w_gate_2"][1], I["ffn1_w_up_2"][1], I["ffn1_w_down_2"][1])
        for n in range(3):
            plan += chunk("sb", I["sb_w_in_2"][0], 512 * n, 512)
        plan += chunk("sb", I["sb_w_in_2"][0], 1536, 512) + chunk("sb", I["sb_w_in_2"][0], 2048, 256)
        plan += chunk("sb", I["sb_w_in_2"][0], 2304, 256)
        plan += chunk("wo1", I["w_out_2"][1], 0, D)
        plan += ffn_list("f4", I["ffn2_w_gate_2"][1], I["ffn2_w_up_2"][1], I["ffn2_w_down_2"][1])

        NU = len(plan)
        used = [0]
        hi_tok, lo_tok, pe_tok = {}, {}, {}
        owed = []

        def load(i):
            if i >= NU:
                return
            _, src, nk, n = plan[i]
            dst = raw[:, i % NR, :].rearrange("p (k n) -> p k n", k=nk)
            sp.wait(lo_tok.get(i - NR))
            sp.e.dma_start(dst, src).then_inc(s_raw[i % NR], 16)

        def split(i):
            if i >= NU:
                return
            came, freed = (s_raw[i % NR], 16 * (i // NR + 1)), pe_tok.get(i - NH)
            r, h, l = raw[:, i % NR, :], wh[:, i % NH, :], wl[:, i % NH, :]
            hi_tok[i] = act.do(lambda e: e.activation(h, r, ACT.Copy), came, freed)
            lo_tok[i] = dve.do(lambda e: e.tensor_tensor(l, r, h.bitcast(F32), ALU.subtract), hi_tok[i], freed)
            load(i + NR)

        def use(name):
            i = used[0]
            used[0] += 1
            assert plan[i][0] == name, (plan[i][0], name)
            _, _, nk, n = plan[i]
            view = lambda t: t[:, i % NH, :].rearrange("p (k n) -> p k n", k=nk)
            pe.wait(hi_tok[i], lo_tok[i])
            return i, nk, n, view(wh), view(wl)

        def release(i, tok, hold=False):
            pe_tok[i] = tok
            if hold:
                owed.append(i + NH)
            else:
                pay()
                split(i + NH)

        def pay():
            while owed:
                split(owed.pop(0))

        def mm(o, l, r, start, stop):
            return lambda e: e.matmul(o, l, r, start=start, stop=stop, skip_group_check=True)

        def three(lst, o, lh, ll, rh, rl, start, stop):
            lst += [(o, lh, rh, start, False), (o, lh, rl, False, False), (o, ll, rh, False, stop)]

        def emit(lst, *after):
            pe.wait(*after)
            for a in lst[:-1]:
                pe.go(mm(*a))
            return pe.do(mm(*lst[-1]))

        def mm_x(name, n0, xh, xl, xt, banks, last=False, hold=False):
            kt = 0
            pe.wait(bf[banks[0]], bf[banks[1]])
            while kt < 8:
                i, nk, n, h, l = use((name, n0))
                lst = []
                for k in range(nk):
                    pe.wait(xt[(kt + k) // 2])
                    for rb in range(2):
                        a = slice(rb * P, rb * P + P)
                        three(lst, ps[banks[rb]][:, 0:n], xh[:, kt + k, a], xl[:, kt + k, a], h[:, k, :], l[:, k, :],
                              kt + k == 0, kt + k == 7)
                tok = emit(lst)
                kt += nk
                release(i, tok, hold or last and kt == 8)
            return tok

        def mm_w(name, n0, xh, xl, xt, banks, last=False, hold=False):
            kt = 0
            while kt < 8:
                i, nk, n, h, l = use((name, n0))
                nj = n // P
                lst = []
                for k in range(nk):
                    pe.wait(xt[(kt + k) // 2])
                    for j in range(nj):
                        if kt + k == 0 and j % 2 == 0:
                            pe.wait(bf[banks[j // 2]])
                        o = ps[banks[j // 2]][:, (j % 2) * T:(j % 2) * T + T]
                        s = slice(j * P, j * P + P)
                        st_, sp_ = kt + k == 0 and j % 2 == 0, kt + k == 7
                        lst += [(o, h[:, k, s], xh[:, kt + k, :], st_, False),
                                (o, h[:, k, s], xl[:, kt + k, :], False, False),
                                (o, l[:, k, s], xh[:, kt + k, :], False, sp_)]
                tok = emit(lst)
                kt += nk
                release(i, tok, hold or last and kt == 8)
            return tok

        DN = [[6, 7], [0, 1]]

        def mm_d(name, ah, al, at, nk, mid=None, hold=2):
            for b in DN[0] + DN[1]:
                pe.wait(bf[b])
            for kt in range(nk):
                if kt == 3 and mid is not None:
                    mid()
                i, _, _, h, l = use((name, 0))
                pe.wait(at[kt])
                lst = []
                for rb in range(2):
                    a = slice(rb * P, rb * P + P)
                    for nh in range(2):
                        s = slice(nh * 512, nh * 512 + 512)
                        three(lst, ps[DN[rb][nh]][:, :], ah[:, kt, a], al[:, kt, a], h[:, 0, s], l[:, 0, s],
                              kt == 0, kt == nk - 1)
                tok = emit(lst)
                release(i, tok, kt >= nk - hold)
            return tok

        def split_evac(src, hi, lo, *after):
            t = act.do(lambda e: e.activation(hi, src, ACT.Copy), *after)
            return dve.do(lambda e: e.tensor_tensor(lo, src, hi.bitcast(F32), ALU.subtract), t)

        def to_T(src, hi, lo, after, banks=(2, 3, 4, 5), nkt=8):
            toks = []
            for g in range(nkt // 2):
                b = banks[g % len(banks)]
                pe.wait(bf[b])
                for k in range(2):
                    for rb in range(2):
                        pe.wait(after[rb])
                        o = ps[b][:, k * T + rb * P:k * T + rb * P + P]
                        i_ = src[:, rb, (2 * g + k) * P:(2 * g + k + 1) * P]
                        f = lambda e, o=o, i_=i_: e.transpose(o, i_, ident)
                        t = pe.do(f) if (k, rb) == (1, 1) else pe.go(f)
                v = ps[b][:, :].rearrange("p (k t) -> p k t", k=2)
                toks.append(split_evac(v, hi[:, 2 * g:2 * g + 2, :], lo[:, 2 * g:2 * g + 2, :], t))
                bf[b] = [toks[-1]]
            return toks

        gn = [0]
        gfree = {}
        s_gain = [Dmas(sem(f"s_gain{i}")) for i in range(3)]

        def gain(vec):
            g = gn[0] % 3
            gn[0] += 1
            t = s_gain[g].start(pool, gb[:, g, :], vec.partition_broadcast(P), gfree.get(g))
            return gb[:, g, :], t, g

        def rstd_of(var, rs, after, eps, scale):
            t = dve.do(lambda e: e.tensor_scalar(var, var, scale, eps, ALU.mult, ALU.add), after)
            n = var.free_size()
            return pool.do(lambda e: e.tensor_tensor(rs, var, C(K_HALF, n), ALU.pow), t, cst_tok)

        def rms_rows(src, after, g, dst):
            gt, gtok, gi = g
            toks = []
            for rb in range(2):
                t = square_sum(src[:, rb, :], st[:, rb:rb + 1], D, after[rb], st_free[0])
                t = rstd_of(st[:, rb:rb + 1], st[:, 2 + rb:3 + rb], t, EPS, 1.0 / D)
                t = dve.do(lambda e, rb=rb: e.scalar_tensor_tensor(
                    out=dst[:, rb, :], in0=src[:, rb, :], scalar=st[:, 2 + rb:3 + rb], in1=gt,
                    op0=ALU.mult, op1=ALU.mult), t, gtok, dst_free[0])
                toks.append(t)
            gfree[gi] = toks[-1]
            st_free[0] = toks[-1]
            return toks

        st_free, dst_free = [None], [None]
        junk_by = [None]

        def square_sum(src, dst, width, *after):
            junk_by[0] = act.do(lambda e: e.activation(junk[:, 0:width], src, ACT.Square, accum_out=dst), junk_by[0], *after)
            return junk_by[0]

        def rms_add(tok, g, tmp, *tmp_free):
            gt, gtok, gi = g
            toks = []
            for rb in range(2):
                for nh in range(2):
                    b = DN[rb][nh]
                    c = 8 + 2 * rb + nh
                    t = square_sum(ps[b][:, :], st[:, c:c + 1], 512, tok, st_free[0])
                t = dve.do(lambda e, rb=rb: e.tensor_tensor(st[:, 12 + rb:13 + rb], st[:, 8 + 2 * rb:9 + 2 * rb],
                                                            st[:, 9 + 2 * rb:10 + 2 * rb], ALU.add), t)
                t = rstd_of(st[:, 12 + rb:13 + rb], st[:, 14 + rb:15 + rb], t, EPS, 1.0 / D)
                for nh in range(2):
                    b, s = DN[rb][nh], slice(nh * 512, nh * 512 + 512)
                    t1 = dve.do(lambda e, b=b, s=s, rb=rb: e.scalar_tensor_tensor(
                        out=tmp[:, rb, s], in0=ps[b][:, :], scalar=st[:, 14 + rb:15 + rb], in1=gt[:, s],
                        op0=ALU.mult, op1=ALU.mult), t, gtok, list(tmp_free))
                    bf[b] = [t1]
                    t2 = dve.do(lambda e, s=s, rb=rb: e.tensor_tensor(x[:, rb, s], x[:, rb, s], tmp[:, rb, s],
                                                                      ALU.add), t1)
                toks.append(t2)
            gfree[gi] = st_free[0] = toks[-1]
            pay()
            return toks

        def ln_add(tok, scale, xtok, g, b_):
            (gt, gtok, gi), (bt, btok, bi) = g, b_
            toks = []
            for rb in range(2):
                for nh in range(2):
                    b, s = DN[rb][nh], slice(nh * 512, nh * 512 + 512)
                    t = dve.do(lambda e, b=b, s=s, rb=rb: e.scalar_tensor_tensor(
                        out=x[:, rb, s], in0=ps[b][:, :], scalar=scale, in1=x[:, rb, s],
                        op0=ALU.mult, op1=ALU.add), tok, xtok)
                    bf[b] = [t]
                    t = dve.do(lambda e, s=s, rb=rb, c=6 * nh + 12 * rb: e.bn_stats(st[:, 32 + c:38 + c], x[:, rb, s]),
                               t, st_free[0])
                t = dve.do(lambda e, rb=rb: e.bn_aggr(st[:, 16 + 2 * rb:18 + 2 * rb],
                                                      st[:, 32 + 12 * rb:44 + 12 * rb]), t)
                t = rstd_of(st[:, 17 + 2 * rb:18 + 2 * rb], st[:, 20 + rb:21 + rb], t, LN_EPS, 1.0)
                t = dve.do(lambda e, rb=rb: e.tensor_scalar(x[:, rb, :], x[:, rb, :], st[:, 16 + 2 * rb:17 + 2 * rb],
                                                            st[:, 20 + rb:21 + rb], ALU.subtract, ALU.mult), t)
                t = dve.do(lambda e, rb=rb: e.tensor_tensor(x[:, rb, :], x[:, rb, :], gt, ALU.mult), t, gtok)
                t = dve.do(lambda e, rb=rb: e.tensor_tensor(x[:, rb, :], x[:, rb, :], bt, ALU.add), t, btok)
                toks.append(t)
            gfree[gi] = gfree[bi] = st_free[0] = toks[-1]
            pay()
            return toks

        def ffn(nm, xh, xl, xt, hb, hh, hl, hold=2):
            ht = []
            waiting = []
            hb_free = {}

            def turn():
                n0, w, slot, toks = waiting.pop()
                for q in range(w // T):
                    b = 4 + q
                    pe.wait(bf[b])
                    for k in range(2):
                        for rb in range(2):
                            o = ps[b][:, k * T + rb * P:k * T + rb * P + P]
                            i_ = hb[:, slot, rb, (2 * q + k) * P:(2 * q + k + 1) * P]
                            pe.wait(toks[rb])
                            f = lambda e, o=o, i_=i_: e.transpose(o, i_, ident)
                            t = pe.do(f) if (k, rb) == (1, 1) else pe.go(f)
                    f0 = n0 // P + 2 * q
                    v = ps[b][:, :].rearrange("p (k t) -> p k t", k=2)
                    t2 = split_evac(v, hh[:, f0:f0 + 2, :], hl[:, f0:f0 + 2, :], t)
                    bf[b] = [t2]
                    ht.extend([t2, t2])
                hb_free[slot] = t

            for c, n0 in enumerate(range(0, FF, 512)):
                w, slot = min(512, FF - n0), c % 2
                tg = mm_x(nm + "g", n0, xh, xl, xt, (0, 1))
                sg = []
                for rb in range(2):
                    t = act.do(lambda e, rb=rb, w=w, slot=slot: e.activation(hb[:, slot, rb, 0:w], ps[rb][:, 0:w],
                                                                             ACT.Silu), tg, hb_free.get(slot))
                    bf[rb] = [t]
                    sg.append(t)
                if waiting:
                    turn()
                tu = mm_x(nm + "u", n0, xh, xl, xt, (2, 3), last=n0 + w == FF)
                toks = []
                for rb in range(2):
                    t = dve.do(lambda e, rb=rb, w=w, slot=slot: e.tensor_tensor(
                        hb[:, slot, rb, 0:w], hb[:, slot, rb, 0:w], ps[2 + rb][:, 0:w], ALU.mult), tu, sg[rb])
                    bf[2 + rb] = [t]
                    toks.append(t)
                waiting.append((n0, w, slot, toks))
            pay()
            return mm_d(nm + "d", hh, hl, ht, NF, turn, hold)

        def probe(name, ap, *after):
            if dbg is not None and name in dbg:
                d = Dmas(sem("s_dbg" + name))
                t = d.start(sp, dbg[name], ap, *after)
                sp.wait(t)

        s_x, s_c, s_v, s_l = (Dmas(sem(n)) for n in ("s_x", "s_c", "s_v", "s_l"))
        x_in = I["x"][0].rearrange("(b p) d -> p b d", p=P)
        x_tok = s_x.start(sp, x[:, :, :], x_in)
        cst_tok = s_c.start(sp, cst[:, :], cst_in)
        for i in range(NR):
            load(i)
        g_pre = gain(I["g_mix_pre"])
        g_mem = gain(I["g_mem"])
        r0 = 0
        vplace = {}
        for name, n in VROWS:
            src = I[name]
            if len(src.shape) == 3:
                src = src.rearrange("a h d -> (a h d)")
            elif len(src.shape) == 2:
                src = src.rearrange("a d -> (a d)")
            v_tok = s_v.start(pool, vrow[r0:r0 + n, :], src.rearrange("(r p) -> r p", p=P))
            vplace[name] = r0
            r0 += n
        V = lambda name, i=0, n=1: vcol[:, vplace[name] + i:vplace[name] + i + n]

        ph = ExitStack()
        pb = lambda n, s, d=F32: ph.enter_context(nc.sbuf_tensor(n, s, d))
        kxT = pb("kxT", [P, 8, T])
        vx = pb("vx", [P, 2, D])
        xh = pb("xh0", [P, 8, T], F32R)
        xl = pb("xl0", [P, 8, T], F32R)
        tmp = pb("tmp0", [P, 2, D])
        qkT = pb("qkT", [P, 8, T])
        inner = ExitStack()
        ib = lambda n, s, d=F32: inner.enter_context(nc.sbuf_tensor(n, s, d))
        xn = ib("xn", [P, 2, D])
        mh = ib("mh", [P, 8, T], F32R)
        ml = ib("ml", [P, 8, T], F32R)
        v_sb = ib("v_sb", [P, 2, 512])
        u_sb = ib("u_sb", [P, 2, 512])
        band = ib("band", [P, 8 * T])
        wpool = ib("wpool", [P, 4, P])
        lam_in = ib("lam_in", [P, 4, 64])
        rope = ib("rope", [P, 16 * 16])
        qk = tmp

        for j, name in enumerate(("lambda_q1", "lambda_q2", "lambda_k1", "lambda_k2")):
            l_tok = s_l.start(pool, lam_in[:, j, :], I[name].partition_broadcast(P))
        s_pos, s_band, s_mem = Dmas(sem("s_pos")), Dmas(sem("s_band")), Dmas(sem("s_mem"))
        pos_tok = s_pos.start(pool, pos_i[:, :], I["positions"].rearrange("a (b p) -> p (a b)", p=P),
                          allow_slow_non_contiguous=True)
        band_tok = s_band.start(pool, band[:, :], band_in)
        wp_tok = s_band.start(pool, wpool[:, :, :], I["w_pool"].rearrange("g c d -> c g d"))
        mem_tok = s_mem.start(pool, vx[:, :, :], I["mem"][0].rearrange("(b p) d -> p b d", p=P))

        ht = rms_rows(x, [x_tok, x_tok], g_pre, xn)
        for i in range(NH):
            split(i)
        xt = to_T(xn, xh, xl, [[t, cst_tok] for t in ht])
        probe("hT", xh[:, :, :].bitcast(F32), xt)

        pe.wait(bf[6])
        tv = pe.do(lambda e: e.transpose(ps[6][:, 0:NV], vrow[0:NV, :], cst[0:NV, 0:NV]), v_tok, cst_tok)
        v_ok = act.do(lambda e: e.activation(vcol[:, :], ps[6][:, 0:NV], ACT.Copy), tv)
        bf[6] = [v_ok]
        gs_ok = dve.do(lambda e: e.tensor_scalar(V("g_subln"), V("g_subln"), 1.0 - LAM0, None, ALU.mult), v_ok)

        t = dve.do(lambda e: e.tensor_tensor(lam_in[:, 0:2, :], lam_in[:, 0:2, :], lam_in[:, 2:4, :], ALU.mult), l_tok)
        t = dve.do(lambda e: e.tensor_reduce(st[:, 64:66], lam_in[:, 0:2, :], AX.X, ALU.add), t)
        t = act.do(lambda e: e.activation(st[:, 64:66], st[:, 64:66], ACT.Exp), t)
        t = dve.do(lambda e: e.tensor_tensor(st[:, 66:67], st[:, 65:66], st[:, 64:65], ALU.subtract), t)
        nlam = st[:, 66:67]
        lam_ok = dve.do(lambda e: e.tensor_scalar(nlam, nlam, -LAM0, None, ALU.add), t)

        R = lambda k: rope[:, 16 * k:16 * k + 16]
        R3 = lambda k: R(k).rearrange("p (b f) -> p b f", b=2)
        t = dve.do(lambda e: e.tensor_copy(st[:, 68:70], pos_i[:, :]), pos_tok)
        t = dve.do(lambda e: e.tensor_tensor(R3(0), st[:, 68:70].unsqueeze(2).to_broadcast([P, 2, 8]),
                                             C(K_FREQ, 8).unsqueeze(1).to_broadcast([P, 2, 8]), ALU.mult), t, cst_tok)
        t = dve.do(lambda e: e.tensor_scalar(R(1), R(0), 1.0 / (2 * math.pi), 12582912.0, ALU.mult, ALU.add), t)
        t = dve.do(lambda e: e.tensor_scalar(R(1), R(1), -12582912.0, None, ALU.add), t)
        c1 = 6.28125
        c2 = float(np.float32(np.round((2 * math.pi - c1) * 2 ** 20) / 2 ** 20))
        c3 = 2 * math.pi - c1 - c2
        for c in (c1, c2, c3):
            t = dve.do(lambda e, c=c: e.scalar_tensor_tensor(out=R(0), in0=R(1), scalar=-c, in1=R(0),
                                                             op0=ALU.mult, op1=ALU.add), t)
        lim = float(np.nextafter(np.float32(math.pi), np.float32(0)))
        t = dve.do(lambda e: e.tensor_scalar(R(0), R(0), lim, -lim, ALU.min, ALU.max), t)
        t2 = dve.do(lambda e: e.scalar_tensor_tensor(out=R(2), in0=R(0), scalar=-1.0, in1=R(0),
                                                     op0=ALU.mult, op1=ALU.min), t)
        t2 = dve.do(lambda e: e.tensor_scalar(R(2), R(2), math.pi / 2, None, ALU.add), t2)
        t = act.do(lambda e: e.activation(R(3), R(0), ACT.Sin), t)
        rope_ok = act.do(lambda e: e.activation(R(2), R(2), ACT.Sin), t2)
        COS, SIN = R3(2), R3(3)

        rot = []
        for c in range(2):
            banks = (0, 1) if c == 0 else (2, 3)
            tq = mm_x("w_in", 512 * c, xh, xl, xt, banks)
            for rb in range(2):
                b = banks[rb]
                t = act.do(lambda e, b=b, rb=rb, c=c: e.activation(qk[:, rb, 512 * c:512 * c + 512], ps[b][:, :],
                                                                   ACT.Copy), tq)
                bf[b] = [t]
                rot.append(t)
        rt = {}
        for rb in range(2):
            v = qk[:, rb, :].rearrange("p (h d) -> p h d", d=64)
            t1, t2 = v[:, :, 0:8], v[:, :, 8:16]
            cs, sn = (z[:, rb, :].unsqueeze(1).to_broadcast([P, 16, 8]) for z in (COS, SIN))
            w4 = [junk[:, 128 * j + 512 * rb:128 * j + 512 * rb + 128].rearrange("p (h d) -> p h d", d=8) for j in range(4)]
            tt = lambda o, a, b, op, *w: dve.do(lambda e: e.tensor_tensor(o, a, b, op), *w)
            a1 = tt(w4[0], t1, cs, ALU.mult, rot, rope_ok, junk_by[0])
            a2 = tt(w4[1], t2, sn, ALU.mult)
            a3 = tt(w4[2], t2, cs, ALU.mult)
            a4 = tt(w4[3], t1, sn, ALU.mult)
            tt(t1, w4[0], w4[1], ALU.subtract, a4)
            rt[rb] = tt(t2, w4[2], w4[3], ALU.add)

        tv = mm_x("w_in", 1024, xh, xl, xt, (0, 1))
        v_tok2 = []
        for rb in range(2):
            t = act.do(lambda e, rb=rb: e.activation(v_sb[:, rb, :], ps[rb][:, :], ACT.Copy), tv)
            bf[rb] = [t]
            v_tok2.append(t)
        tu = mm_x("w_in", 1536, xh, xl, xt, (2, 3))
        u_tok = []
        for rb in range(2):
            t = act.do(lambda e, rb=rb: e.activation(u_sb[:, rb, :], ps[2 + rb][:, :], ACT.Copy), tu)
            bf[2 + rb] = [t]
            u_tok.append(t)
        mixed_ready = tu

        qk_tok = []
        for g in range(4):
            b = 4 + g % 2
            pe.wait(bf[b])
            for k in range(2):
                for rb in range(2):
                    pe.wait(rt[rb])
                    o = ps[b][:, k * T + rb * P:k * T + rb * P + P]
                    i_ = qk[:, rb, (2 * g + k) * P:(2 * g + k + 1) * P]
                    f = lambda e, o=o, i_=i_: e.transpose(o, i_, ident)
                    t = pe.do(f) if (k, rb) == (1, 1) else pe.go(f)
            t = act.do(lambda e, b=b, g=g: e.activation(
                qkT[:, 2 * g:2 * g + 2, :], ps[b][:, :].rearrange("p (k t) -> p k t", k=2), ACT.Copy), t)
            bf[b] = [t]
            qk_tok.append(t)
        probe("qkT", qkT[:, :, :], qk_tok)

        dst_free[0] = xt[-1]
        mt = rms_rows(vx, [[mem_tok, rt[0], rt[1]]] * 2, g_mem, xn)
        mt = to_T(xn, mh, ml, mt, banks=(6, 7, 4, 5))

        pl = xn.rearrange("p b d -> p (b d)")[:, 0:1024].rearrange("p (g t) -> p g t", g=4)
        bandv = band[:, :].rearrange("p (s g t) -> p s g t", s=2, g=4)
        pl_tok = []
        for q in range(2):
            b = 6 + q
            lst = []
            for k in range(2):
                g = 2 * q + k
                for s in range(2):
                    lst.append((ps[b][:, k * T:k * T + T], u_sb[:, s, g * P:g * P + P], bandv[:, s, g, :], s == 0, s == 1))
            t = emit(lst, bf[b], u_tok, band_tok)
            t = act.do(lambda e, b=b, q=q: e.activation(
                pl[:, 2 * q:2 * q + 2, :], ps[b][:, :].rearrange("p (k t) -> p k t", k=2), ACT.Copy), t, mt)
            bf[b] = [t]
            pl_tok.append(t)
        mix_tok = {}
        for q in range(2):
            b = 4 + q
            lst = [(ps[b][:, k * T:k * T + T], wpool[:, 2 * q + k, :], pl[:, 2 * q + k, :], True, True) for k in range(2)]
            t = emit(lst, bf[b], pl_tok, wp_tok)
            half = [ps[b][:, k * T:k * T + T] for k in range(2)]
            for k in range(2):
                g = 2 * q + k
                t1 = act.do(lambda e, k=k, g=g, half=half: e.activation(xh[:, 4 + g, :], half[k], ACT.Copy,
                                                             scale=V("pool_scale", g)), t, v_ok, mixed_ready)
            for k in range(2):
                g = 2 * q + k
                t2 = dve.do(lambda e, k=k, g=g, half=half: e.scalar_tensor_tensor(
                    out=xl[:, 4 + g, :], in0=half[k], scalar=V("pool_scale", g), in1=xh[:, 4 + g, :].bitcast(F32),
                    op0=ALU.mult, op1=ALU.subtract), t1)
                mix_tok[4 + g] = t2
            bf[b] = [t2]

        kx_tok, vx_tok = [], []

        def kx_chunk(c):
            banks = (0, 1) if c == 0 else (2, 3)
            t = mm_w("w_xkv", 512 * c, mh, ml, mt, banks)
            for q in range(2):
                b = banks[q]
                t2 = act.do(lambda e, b=b, j=4 * c + 2 * q: e.activation(
                    kxT[:, j:j + 2, :], ps[b][:, :].rearrange("p (k t) -> p k t", k=2), ACT.Copy), t)
                bf[b] = [t2]
                kx_tok.append(t2)

        def vx_chunk(c):
            banks = (0, 1) if c == 0 else (2, 3)
            t = mm_x("w_xkv", 1024 + 512 * c, mh, ml, mt, banks)
            for rb in range(2):
                b = banks[rb]
                t2 = act.do(lambda e, b=b, rb=rb, c=c: e.activation(vx[:, rb, 512 * c:512 * c + 512], ps[b][:, :],
                                                                    ACT.Copy), t)
                bf[b] = [t2]
                vx_tok.append(t2)

        pbuf = qk[:, 0:2, :].rearrange("p b d -> p (b d)")[:, 0:1536].rearrange("p (s m k) -> p s m k", s=2, m=2)
        pT = inner.enter_context(nc.sbuf_tensor("aT", [P, 4, 3, P], F32))
        p_free = {}
        a_tok = {}
        sc8 = 64 ** -0.5
        KEYS = (slice(0, P), slice(P, 3 * P))

        def scores(h):
            s = h % 2
            banks = (4, 5) if s == 0 else (6, 7)
            c = 72 + 16 * s
            S = lambda k, i, m=0, n=2: st[:, c + 4 * k + 2 * i + m:c + 4 * k + 2 * i + m + n]
            tm = []
            for m in range(2):
                d = slice(64 * m, 64 * m + 64)
                t = emit([(ps[banks[m]][:, KEYS[i]], qkT[d, h, i * P:i * P + P], qkT[d, 4 + h, 0:(i + 1) * P], i == 0, i == 1)
                          for i in range(2)], bf[banks[m]], qk_tok)
                t = dve.do(lambda e, m=m: e.tensor_tensor(pbuf[:, s, m, :], ps[banks[m]][:, 0:384], C(K_AM, 384), ALU.add),
                           t, p_free.get(s), rt[0], rt[1])
                bf[banks[m]] = [t]
                tm.append(t)
            for i in range(2):
                t = dve.do(lambda e, i=i: e.tensor_reduce(S(0, i), pbuf[:, s, :, KEYS[i]], AX.X, ALU.max), tm)
            t = dve.do(lambda e: e.tensor_scalar(st[:, c + 4:c + 8], st[:, c:c + 4], -sc8, None, ALU.mult), t)
            for i in range(2):
                for m in range(2):
                    te = act.do(lambda e, i=i, m=m: e.activation(
                        pbuf[:, s, m, KEYS[i]], pbuf[:, s, m, KEYS[i]], ACT.Exp, scale=sc8, bias=S(1, i, m, 1),
                        accum_out=S(2, i, m, 1)), t)
            t = dve.do(lambda e: e.reciprocal(st[:, c + 12:c + 16], st[:, c + 8:c + 12]), te)
            o2 = st[:, c + 12:c + 16].rearrange("p (i m) -> p i m", i=2)[:, :, 1]
            t = dve.do(lambda e: e.tensor_tensor(o2, o2, nlam.to_broadcast([P, 2]), ALU.mult), t, lam_ok)
            for i in range(2):
                p0, p1 = pbuf[:, s, 0, KEYS[i]], pbuf[:, s, 1, KEYS[i]]
                t2 = dve.do(lambda e, p0=p0, i=i: e.tensor_scalar(p0, p0, S(3, i, 0, 1), None, ALU.mult), t)
                a_tok[h, i] = dve.do(lambda e, p0=p0, p1=p1, i=i: e.scalar_tensor_tensor(
                    out=p0, in0=p1, scalar=S(3, i, 1, 1), in1=p0, op0=ALU.mult, op1=ALU.add), t2)

        aT_tok = {}

        def turn_a(h):
            s = h % 2
            b = 4 + h
            pe.wait(bf[b], a_tok[h, 0], a_tok[h, 1])
            for k in range(3):
                f = lambda e, k=k: e.transpose(ps[b][:, k * P:k * P + P], pbuf[:, s, 0, k * P:k * P + P], ident)
                t = pe.do(f) if k == 2 else pe.go(f)
            p_free[s] = t
            aT_tok[h] = act.do(lambda e: e.activation(
                pT[:, h, :, :], ps[b][:, 0:384].rearrange("p (k t) -> p k t", k=3), ACT.Copy), t)
            bf[b] = [aT_tok[h]]

        kx_chunk(0)
        scores(0)
        scores(1)
        kx_chunk(1)
        turn_a(0)
        turn_a(1)
        scores(2)
        scores(3)
        vx_chunk(0)
        turn_a(2)
        turn_a(3)

        dan = u_sb
        for i in range(2):
            b = 4 + i
            lst = []
            for h in range(4):
                for k in range(i + 1):
                    lst.append((ps[b][:, h * P:h * P + P], pT[:, h, i + k, :], v_sb[:, k, h * P:h * P + P],
                                k == 0, k == i))
            t = emit(lst, bf[b], list(aT_tok.values()), v_tok2)
            sq = junk[:, 512 * i:512 * i + 512]
            t = act.do(lambda e, b=b, sq=sq: e.activation(sq, ps[b][:, :], ACT.Square), t)
            t = dve.do(lambda e, i=i, sq=sq: e.tensor_reduce(st[:, 104 + 4 * i:108 + 4 * i],
                                                      sq.rearrange("p (h d) -> p h d", h=4), AX.X, ALU.add), t)
            t = rstd_of(st[:, 104 + 4 * i:108 + 4 * i], st[:, 112 + 4 * i:116 + 4 * i], t, EPS, 1.0 / P)
            t = dve.do(lambda e, b=b, i=i: e.tensor_tensor(
                dan[:, i, :].rearrange("p (h d) -> p h d", h=4), ps[b][:, :].rearrange("p (h d) -> p h d", h=4),
                st[:, 112 + 4 * i:116 + 4 * i].unsqueeze(2).to_broadcast([P, 4, P]), ALU.mult), t, pl_tok)
            bf[b] = [t]
            if i == 0:
                d0 = t
        d1 = t
        probe("dan", dan[:, :, :], d1)
        vx_chunk(1)
        for q in range(2):
            b = 6 + q
            pe.wait(bf[b])
            for k in range(2):
                for rb in range(2):
                    pe.wait(d0, d1)
                    o = ps[b][:, k * T + rb * P:k * T + rb * P + P]
                    i_ = dan[:, rb, (2 * q + k) * P:(2 * q + k + 1) * P]
                    f = lambda e, o=o, i_=i_: e.transpose(o, i_, ident)
                    t = pe.do(f) if (k, rb) == (1, 1) else pe.go(f)
            v = ps[b][:, :].rearrange("p (k t) -> p k t", k=2)
            t1 = act.do(lambda e, v=v, q=q: e.activation(xh[:, 2 * q:2 * q + 2, :], v, ACT.Copy,
                                                         scale=V("g_subln")), t, gs_ok, mixed_ready)
            t2 = dve.do(lambda e, v=v, q=q: e.scalar_tensor_tensor(
                out=xl[:, 2 * q:2 * q + 2, :], in0=v, scalar=V("g_subln"), in1=xh[:, 2 * q:2 * q + 2, :].bitcast(F32),
                op0=ALU.mult, op1=ALU.subtract), t1)
            bf[b] = [t2]
            mix_tok[2 * q] = mix_tok[2 * q + 1] = t2
        probe("mixT", xh[:, :, :].bitcast(F32), list(mix_tok.values()))

        inner.close()
        g_post = gain(I["g_mix_post"])
        t = mm_d("w_out", xh, xl, mix_tok, 8)
        xk = rms_add(t, g_post, tmp, list(p_free.values()), qk_tok)
        probe("x1", x[:, :, :], xk)

        xn = pb("xn2", [P, 2, D])
        xqT = qkT
        pbx = pb("pbx", [P, 2, 2, T])
        pTx = pb("pTx", [P, 2, 2, T])
        dst_free[0] = [t, xk]
        pre = rms_rows(x, xk, gain(I["g_x_pre"]), xn)
        xt = to_T(xn, xh, xl, pre)
        xq_tok = []
        for c in range(2):
            banks = (0, 1) if c == 0 else (2, 3)
            t = mm_w("w_xq", 512 * c, xh, xl, xt, banks, last=c == 1)
            for q in range(2):
                b = banks[q]
                t2 = act.do(lambda e, b=b, j=4 * c + 2 * q: e.activation(
                    xqT[:, j:j + 2, :], ps[b][:, :].rearrange("p (k t) -> p k t", k=2), ACT.Copy), t, list(a_tok.values()))
                bf[b] = [t2]
                xq_tok.append(t2)
            xq_done = t

        def soft_attn(nh, qk_pairs, scale, pbuf, pTb, vtile, finish, ktok, vtok, sbanks, tbanks, obanks):
            free_p, free_t, tk = {}, {}, {}

            def one(h):
                s, b, c = h % 2, sbanks[h % 2], 128 + 8 * (h % 2)
                pw = ps[b][:, :].rearrange("p (b m) -> p b m", b=2)
                lst = []
                for tb in range(2):
                    prs = qk_pairs(h, tb)
                    for j, (l, r) in enumerate(prs):
                        lst.append((pw[:, tb, :], l, r, j == 0, j == len(prs) - 1))
                t = emit(lst, bf[b], ktok)
                t = dve.do(lambda e: e.tensor_reduce(st[:, c:c + 2], pw, AX.X, ALU.max), t, free_t.get(("st", s)))
                t = dve.do(lambda e: e.tensor_scalar(st[:, c + 2:c + 4], st[:, c:c + 2], -scale, None, ALU.mult), t)
                for tb in range(2):
                    t = act.do(lambda e, tb=tb: e.activation(pbuf[:, s, tb, :], pw[:, tb, :], ACT.Exp, scale=scale,
                                                             bias=st[:, c + 2 + tb:c + 3 + tb],
                                                             accum_out=st[:, c + 4 + tb:c + 5 + tb]), t, free_p.get(s))
                bf[b] = [t]
                t = dve.do(lambda e: e.reciprocal(st[:, c + 6:c + 8], st[:, c + 4:c + 6]), t)
                for tb in range(2):
                    t2 = dve.do(lambda e, tb=tb: e.tensor_scalar(pbuf[:, s, tb, :], pbuf[:, s, tb, :],
                                                                 st[:, c + 6 + tb:c + 7 + tb], None, ALU.mult), t)
                free_t["st", s] = t2
                tk[h] = t2

            def two(h):
                s, b = h % 2, tbanks[h % 2]
                pe.wait(bf[b], tk[h])
                for mb in range(2):
                    for tb in range(2):
                        o = ps[b][:, mb * T + tb * P:mb * T + tb * P + P]
                        f = lambda e, o=o, tb=tb, mb=mb: e.transpose(o, pbuf[:, s, tb, mb * P:mb * P + P], ident)
                        t = pe.do(f) if (mb, tb) == (1, 1) else pe.go(f)
                free_p[s] = t
                t = act.do(lambda e: e.activation(pTb[:, s, :, :], ps[b][:, :].rearrange("p (m t) -> p m t", m=2),
                                                  ACT.Copy), t, free_t.get(s))
                bf[b] = [t]
                ob = obanks[h % 2]
                lst = []
                lts = vtile(h)
                for j, lt in enumerate(lts):
                    for mb in range(2):
                        lst.append((ps[ob][:, j * T:j * T + T], lt(mb), pTb[:, s, mb, :], mb == 0, mb == 1))
                t = emit(lst, bf[ob], t, vtok)
                free_t[s] = t
                bf[ob] = [finish(h, ps[ob], t)]

            for h in range(nh + 1):
                if h < nh:
                    one(h)
                if h >= 1:
                    two(h - 1)

        xo_tok = {}

        def fin_x(h, bank, t):
            r = split_evac(bank[:, :].rearrange("p (k t) -> p k t", k=2), xh[:, 2 * h:2 * h + 2, :],
                           xl[:, 2 * h:2 * h + 2, :], t, xq_done)
            xo_tok[2 * h] = xo_tok[2 * h + 1] = r
            return r

        soft_attn(4, lambda h, tb: [(xqT[:, 2 * h + j, tb * P:tb * P + P], kxT[:, 2 * h + j, :]) for j in range(2)],
                  256 ** -0.5, pbx, pTx, lambda h: [lambda mb, j=j: vx[:, mb, (2 * h + j) * P:(2 * h + j + 1) * P]
                                                    for j in range(2)],
                  fin_x, kx_tok + xq_tok, vx_tok, (2, 3), (4, 5), (6, 7))
        pay()
        g_post = gain(I["g_x_post"])
        t = mm_d("w_xo", xh, xl, xo_tok, 8)
        xk = rms_add(t, g_post, tmp)
        probe("x2", x[:, :, :], xk)
        ph.close()

        def open_ffn(n):
            s = ExitStack()
            a = lambda nm, sh, d=F32: s.enter_context(nc.sbuf_tensor(nm + n, sh, d))
            return (s, a("fhb", [P, 2, 2, 512]), a("fxh", [P, 8, T], F32R), a("fxl", [P, 8, T], F32R),
                    a("fhh", [P, NF, T], F32R), a("fhl", [P, NF, T], F32R))

        rows = lambda hb: hb[:, :, :, :].rearrange("p s b n -> p (s b n)").rearrange("p (b n) -> p b n", b=2)

        ms = ExitStack()
        m2 = ms.enter_context(nc.sbuf_tensor("m2", [P, 2, D], F32))
        mh = ms.enter_context(nc.sbuf_tensor("mh2", [P, 8, T], F32R))
        ml = ms.enter_context(nc.sbuf_tensor("ml2", [P, 8, T], F32R))
        m2_tok = s_mem.start(pool, m2[:, :, :], I["mem_2"][0].rearrange("(b p) d -> p b d", p=P), xk)
        fs, hb, xh, xl, hh, hl = open_ffn("0")
        dst_free[0] = xk
        pre = rms_rows(x, xk, gain(I["g_ffn_pre"]), rows(hb))
        xt = to_T(rows(hb), xh, xl, pre)
        mt = to_T(m2, mh, ml, [m2_tok, m2_tok], banks=(6, 7, 4, 5))
        g_post = gain(I["g_ffn_post"])
        t = ffn("f0", xh, xl, xt, hb, hh, hl, hold=0)
        tk = mm_w("mkv", 0, mh, ml, mt, (2,), hold=True)
        tv = mm_x("mkv", 256, mh, ml, mt, (4, 5), hold=True)
        xk = rms_add(t, g_post, rows(hb))
        probe("x3", x[:, :, :], xk)
        mk_tok = act.do(lambda e: e.activation(mk2[:, :, :], ps[2][:, :].rearrange("p (k t) -> p k t", k=2), ACT.Copy), tk)
        bf[2] = [mk_tok]
        mv_tok = []
        for rb in range(2):
            t = act.do(lambda e, rb=rb: e.activation(mv2[:, rb, :], ps[4 + rb][:, 0:T], ACT.Copy), tv)
            bf[4 + rb] = [t]
            mv_tok.append(t)
        fs.close()
        ms.close()

        def scale_x(*after):
            return pool.do(lambda e: e.tensor_scalar(x[:, :, :], x[:, :, :], ALPHA, None, ALU.mult), *after)

        def norm_of(i, j):
            return gain(I["ln_g_2"][i, j]), gain(I["ln_b_2"][i, j])

        def half_ffn(nm, i, j, xk):
            fs, hb, xh, xl, hh, hl = open_ffn(nm)
            xt = to_T(x, xh, xl, xk)
            xa = scale_x(xt)
            g, b = norm_of(i, j)
            t = ffn(nm, xh, xl, xt, hb, hh, hl)
            xk = ln_add(t, 0.5, xa, g, b)
            probe("x" + nm, x[:, :, :], xk)
            fs.close()
            return xk

        def mem_attn(mqT, mq_tok, dst, pbm, pTm, sbanks, tbanks, obanks):
            toks = []

            def fin(h, bank, t):
                o = slice(64 * (h % 2), 64 * (h % 2) + 64)
                r = act.do(lambda e: e.activation(dst[o, h // 2, :], bank[o, 0:T], ACT.Copy), t)
                toks.append(r)
                return r

            def pairs(h, tb):
                o = slice(64 * (h % 2), 64 * (h % 2) + 64)
                return [(mqT[o, h // 2, tb * P:tb * P + P], mk2[o, h // 2, :])]

            soft_attn(4, pairs, 0.125, pbm, pTm,
                      lambda h: [lambda mb: mv2[:, mb, (h // 2) * P:(h // 2) * P + P]],
                      fin, [mk_tok, mq_tok], mv_tok, sbanks, tbanks, obanks)
            return toks

        xk = half_ffn("f1", 0, 0, xk)

        tt = lambda o, a, b, op, *w: dve.do(lambda e: e.tensor_tensor(o, a, b, op), *w)
        ts = lambda o, a, s1, s2, o1, o2, *w: dve.do(lambda e: e.tensor_scalar(o, a, s1, s2, o1, o2), *w)
        stt = lambda o, a, s_, b, o1, o2, *w: dve.do(
            lambda e: e.scalar_tensor_tensor(out=o, in0=a, scalar=s_, in1=b, op0=o1, op1=o2), *w)
        fn = lambda o, i_, f, *w, **k: act.do(lambda e: e.activation(o, i_, f, **k), *w)
        VB = lambda name: V(name, 0, 6).unsqueeze(2).to_broadcast([P, 6, T])
        flat = lambda a: a.rearrange("p c t -> p (c t)")

        rs = ExitStack()
        ra = lambda nm, sh, d=F32: rs.enter_context(nc.sbuf_tensor("r" + nm, sh, d))
        Rr, Kk, Vv, KK, AA, GG, BV = (ra(n, [P, 6, T]) for n in ("R", "K", "V", "KK", "AA", "GG", "BV"))
        Vtm = ra("Vtm", [P, 2, C7])
        mqT = ra("mq", [P, 2, T])
        mo = ra("mo", [P, 2, T])
        zsc = ra("zsc", [P, 6])
        s2 = ExitStack()
        rb_ = lambda nm, sh, d=F32: s2.enter_context(nc.sbuf_tensor("r" + nm, sh, d))
        DD = rb_("DD", [P, 2, T])
        wab = rb_("wab", [P, C7])
        gup = rb_("gup", [P, C7])
        s1 = ExitStack()
        rc = lambda nm, sh, d=F32: s1.enter_context(nc.sbuf_tensor("r" + nm, sh, d))
        xh, xl = rc("xh", [P, 8, T], F32R), rc("xl", [P, 8, T], F32R)
        zs = rc("zs", [P, 4, 2, T + 1])

        s_up = Dmas(sem("s_up"))
        s_up.start(pool, wab[0:64, :], I["rwkv_w_up_2"][0], xk)
        s_up.start(pool, wab[64:128, :], I["rwkv_a_up_2"][0])
        up_tok = s_up.start(pool, gup[:, :], I["rwkv_g_up_2"][0])
        z0_tok = pool.do(lambda e: e.memset(zs[:, :, :, 0:1], 0.0), xk)
        xt = to_T(x, xh, xl, xk)
        xa = scale_x(xt)
        g0b0 = norm_of(0, 1)

        tiles = {0: Rr, 1: Kk, 2: Vv, 3: DD}
        zfree = {}
        z_tok = []
        n_z = 0
        for c in range(5):
            banks = (0, 1) if c % 2 == 0 else (2, 3)
            t = mm_w("rw", 512 * c, xh, xl, xt, banks)
            for q in range(2):
                b, j, sl = banks[q], 4 * c + 2 * q, n_z % 4
                n_z += 1
                dst = tiles[j // 6][:, j % 6:j % 6 + 2, :]
                cur, prev = zs[:, sl, :, 1:T + 1], zs[:, sl, :, 0:T]
                t1 = fn(cur, ps[b][:, :].rearrange("p (k t) -> p k t", k=2), ACT.Copy, t, zfree.get(sl), z0_tok)
                bf[b] = [t1]
                t2 = tt(dst, prev, cur, ALU.subtract, t1)
                for k in range(2):
                    t2 = stt(dst[:, k, :], dst[:, k, :], V("rwkv_mu_2", j + k), cur[:, k, :], ALU.mult, ALU.add, t2)
                zfree[sl] = t2
                z_tok.append(t2)
        t = mm_w("rw", 2560, xh, xl, xt, (2,))
        mq_tok = fn(mqT[:, :, :], ps[2][:, :].rearrange("p (k t) -> p k t", k=2), ACT.Copy, t)
        bf[2] = [mq_tok]
        z_end = [mq_tok, z_tok[-1]]
        s1.close()

        s1 = ExitStack()
        rc = lambda nm, sh, d=F32: s1.enter_context(nc.sbuf_tensor("r" + nm, sh, d))
        tdw, dgs = rc("tdw", [P, T]), rc("dgs", [P, T])
        LD, w1, w2, scm = (rc(n, [P, 6, T]) for n in ("LD", "w1", "w2", "scm"))
        i24, iT = rc("i24", [P, 24]), rc("iT", [12, T])
        pbm, pTm = rc("pbm", [P, 2, 2, T]), rc("pTm", [P, 2, 2, T])
        t = pool.do(lambda e: e.memset(scm[:, :, :], 1.0), z_end)
        sc_tok = pool.do(lambda e: e.memset(flat(scm[:, :, :]).rearrange("p (n t) -> p n t", t=P)[:, :, 0:1], 0.0), t)

        td_tok = fn(tdw[0:64, :], DD[0:64, 0, :], ACT.Tanh, z_end)
        dg_tok = fn(dgs[:, :], DD[:, 1, :], ACT.Sigmoid, z_end)
        for q in range(3):
            bw, ba, bg = (0, 4, 6) if q % 2 == 0 else (1, 5, 7)
            cs_ = [slice((2 * q + k) * P, (2 * q + k + 1) * P) for k in range(2)]
            hf = [slice(k * T, k * T + T) for k in range(2)]
            t = emit([(ps[bw][:, hf[k]], wab[0:64, cs_[k]], tdw[0:64, :], True, True) for k in range(2)],
                     bf[bw], td_tok, up_tok)
            for k in range(2):
                w_tok = fn(LD[:, 2 * q + k, :], ps[bw][:, hf[k]], ACT.Sigmoid, t, bias=V("rwkv_w0_2", 2 * q + k))
            bf[bw] = [w_tok]
            t = emit([(ps[ba][:, hf[k]], wab[64:128, cs_[k]], DD[64:128, 0, :], True, True) for k in range(2)], bf[ba])
            for k in range(2):
                a_tok_ = fn(AA[:, 2 * q + k, :], ps[ba][:, hf[k]], ACT.Sigmoid, t, bias=V("rwkv_a0_2", 2 * q + k))
            bf[ba] = [a_tok_]
            t = emit([(ps[bg][:, hf[k]], gup[:, cs_[k]], dgs[:, :], True, True) for k in range(2)], bf[bg], dg_tok)
            g_tok = fn(GG[:, 2 * q:2 * q + 2, :], ps[bg][:, :].rearrange("p (k t) -> p k t", k=2), ACT.Copy, t)
            bf[bg] = [g_tok]

        t = tt(KK[:, :, :], Kk[:, :, :], VB("rwkv_k_k_2"), ALU.mult, z_end)
        t = fn(w1[:, :, :], KK[:, :, :], ACT.Square, t)
        t = emit([(ps[2][:, 12 * tb + 2 * c:12 * tb + 2 * c + 2], w1[:, c, tb * P:tb * P + P], C(K_SEL2, 2), True, True)
                  for tb in range(2) for c in range(6)], bf[2], t)
        t = ts(i24[:, :], ps[2][:, 0:24], 1e-24, None, ALU.max, ALU.bypass, t)
        bf[2] = [t]
        t = dve.do(lambda e: e.reciprocal(i24[:, :], i24[:, :]), t)
        t = fn(i24[:, :], i24[:, :], ACT.Sqrt, t)
        pe.wait(bf[3], t)
        for tb in range(2):
            f = lambda e, tb=tb: e.transpose(ps[3][0:12, tb * P:tb * P + P], i24[:, 12 * tb:12 * tb + 12], ident)
            t = pe.do(f)
        iT_tok = fn(iT[:, :], ps[3][0:12, 0:T], ACT.Copy, t)
        bf[3] = [iT_tok]
        for q in range(3):
            b = (2, 3, 4)[q]
            t = emit([(ps[b][:, k * T:k * T + T], C(K_SELH + (2 * q + k) * P, P, 12), iT[:, :], True, True)
                      for k in range(2)], bf[b], iT_tok)
            kk_tok = tt(KK[:, 2 * q:2 * q + 2, :], KK[:, 2 * q:2 * q + 2, :],
                        ps[b][:, :].rearrange("p (k t) -> p k t", k=2), ALU.mult, t)
            bf[b] = [kk_tok]

        t = stt(w1[:, :, :], AA[:, :, :], -1.0, VB("rwkv_k_a_2"), ALU.add, ALU.mult, a_tok_, kk_tok)
        k_tok = stt(Kk[:, :, :], w1[:, :, :], 1.0, Kk[:, :, :], ALU.add, ALU.mult, t)
        t = tt(w2[:, :, :], Rr[:, :, :], VB("rwkv_r_k_2"), ALU.mult)
        t = tt(w2[:, :, :], w2[:, :, :], Kk[:, :, :], ALU.mult, t, k_tok)
        for q in range(3):
            b = (5, 6, 7)[q]
            t2 = emit([(ps[b][:, :], C(K_BO, P), w2[:, 2 * q:2 * q + 2, :], True, True)], bf[b], t)
            bv_tok = tt(BV[:, 2 * q:2 * q + 2, :], Vv[:, 2 * q:2 * q + 2, :],
                        ps[b][:, :].rearrange("p (k t) -> p k t", k=2), ALU.mult, t2)
            bf[b] = [bv_tok]

        def turned(src, tb, dst, banks, after):
            for q, (b, n) in enumerate(zip(banks, (4, 2))):
                pe.wait(bf[b], after)
                for k in range(n):
                    f = lambda e, b=b, k=k, q=q: e.transpose(ps[b][:, k * P:k * P + P],
                                                             src[:, 4 * q + k, tb * P:tb * P + P], ident)
                    t = pe.do(f) if k == n - 1 else pe.go(f)
                t = fn(dst[:, 512 * q:512 * q + n * P], ps[b][:, 0:n * P], ACT.Copy, t)
                bf[b] = [t]
            return t

        v_t = [turned(Vv, tb, Vtm[:, tb, :], (0, 1), z_end) for tb in range(2)]

        t = ts(LD[:, :, :], LD[:, :, :], -math.exp(-0.5), None, ALU.mult, ALU.bypass, w_tok)
        l_tok = dve.do(lambda e: e.tensor_tensor_scan(flat(w1[:, :, :]), flat(scm[:, :, :]), flat(LD[:, :, :]), 0.0,
                                                      ALU.mult, ALU.add), t, sc_tok, k_tok)
        L4 = w1[:, :, :].rearrange("p c (n t) -> p c n t", t=P)
        L3 = flat(w1[:, :, :]).rearrange("p (n t) -> p n t", t=P)
        t = tt(zsc[:, :], L4[:, :, 0, P - 1], L4[:, :, 0, 63], ALU.subtract, l_tok)
        t = tt(zsc[:, :], zsc[:, :], L4[:, :, 1, 63], ALU.add, t)
        zs_tok = fn(zsc[:, :], zsc[:, :], ACT.Exp, t)
        w23 = flat(w2[:, :, :]).rearrange("p (n t) -> p n t", t=P)
        lr_tok = tt(w23, L3, L3[:, :, 63:64].to_broadcast([P, 12, P]), ALU.subtract, l_tok, bv_tok)
        lp_tok = tt(LD[:, :, :], w2[:, :, :], LD[:, :, :], ALU.subtract, lr_tok)
        e1 = fn(w1[:, :, :], w2[:, :, :], ACT.Exp, lr_tok)
        e2 = fn(LD[:, :, :], LD[:, :, :], ACT.Exp, lp_tok)
        r_tok = tt(Rr[:, :, :], Rr[:, :, :], w1[:, :, :], ALU.mult, e1)
        e3 = fn(w2[:, :, :], w2[:, :, :], ACT.Exp, lp_tok, scale=-1.0)
        t = stt(AA[:, :, :], KK[:, :, :], -1.0, AA[:, :, :], ALU.mult, ALU.mult, kk_tok)
        kp_tok = tt(KK[:, :, :], KK[:, :, :], LD[:, :, :], ALU.mult, e2)
        b_tok = tt(AA[:, :, :], AA[:, :, :], w2[:, :, :], ALU.mult, t, e3)
        kh_tok = tt(Kk[:, :, :], Kk[:, :, :], w2[:, :, :], ALU.mult, e3)
        feats = [r_tok, kp_tok, b_tok, kh_tok]
        for nm, a in (("R", Rr), ("KK", KK), ("AA", AA), ("K", Kk), ("BV", BV), ("GG", GG)):
            probe("rw" + nm, a[:, :, :], feats, bv_tok, g_tok)

        mo_tok = mem_attn(mqT, mq_tok, mo, pbm, pTm, (2, 3), (4, 5), (6, 7))
        s1.close()
        s2.close()

        s1 = ExitStack()
        rc = lambda nm, sh, d=F32: s1.enter_context(nc.sbuf_tensor("r" + nm, sh, d))
        BM, MR, AP_, XI, TI = rc("BM", [P, 12, 2 * P]), rc("MR", [P, 12, P]), rc("AP", [P, 12, P]), rc("XI", [P, 12, P]), rc("TI", [P, 12, P])
        Qm, Xs, Us = rc("Qm", [P, 12, 64]), rc("Xs", [P, C7]), rc("Us", [P, C7])
        khT, nbT = rc("khT", [P, C7]), rc("nbT", [P, C7])
        Z0 = rc("Z0", [P, 6, 64])
        oc = Vv[:, :, :].rearrange("p c t -> p (c t)").rearrange("p (b n) -> p b n", b=2)
        old = [feats, mo_tok, zs_tok, v_t]
        zr = [pool.do(lambda e, a=a: e.memset(a[:, :, :], 0.0), old) for a in (BM, MR, AP_)]
        M_ = lambda k, n=P: C(k, n).bitcast(I32)
        y_tok = []
        idb = ident.unsqueeze(1).to_broadcast([P, 12, P])
        kb_tok = [turned(Kk, 0, khT, (0, 1), old), turned(AA, 0, nbT, (2, 3), old)]
        u_done = o_done = None
        z_ok = None
        for ck in range(2):
            ts_ = slice(ck * P, ck * P + P)
            H = lambda h: (slice(64 * (h % 2), 64 * (h % 2) + 64), h // 2, ts_)
            xi_tok = pool.do(lambda e: e.tensor_copy(XI[:, :, :], idb), old, u_done)
            cp = lambda o, m, d, *w: dve.do(lambda e: e.copy_predicated(o, m, d), *w)
            for g in range(3):
                for par in range(2):
                    b0, b1 = (2 * par, 2 * par + 1) if g % 2 == 0 else (4 + 2 * par, 5 + 2 * par)
                    hs = (4 * g + par, 4 * g + 2 + par)
                    la, lb = [], []
                    for k, h in enumerate(hs):
                        for j, r in enumerate((KK, Rr)):
                            o = slice((2 * k + j) * P, (2 * k + j + 1) * P)
                            la.append((ps[b0][:, o], Kk[H(h)], r[H(h)], True, True))
                            lb.append((ps[b1][:, o], AA[H(h)], r[H(h)], True, True))
                    ta = emit(la, bf[b0], feats)
                    tb_ = emit(lb, bf[b1])
                    pa = ps[b0][:, :].rearrange("p (k t) -> p k t", k=2)
                    pb_ = ps[b1][:, :].rearrange("p (k t) -> p k t", k=2)
                    of = lambda a: a[:, 4 * g + par:4 * g + par + 3:2, :]
                    t = cp(of(BM), M_(K_SU, 2 * P).unsqueeze(1).to_broadcast([P, 2, 2 * P]), pa, ta, zr, o_done, xi_tok)
                    bf[b0] = [t]
                    t = cp(of(XI), M_(K_M1).unsqueeze(1).to_broadcast([P, 2, P]), pb_[:, :, 0:P], tb_)
                    t = cp(of(MR), M_(K_IU).unsqueeze(1).to_broadcast([P, 2, P]), pb_[:, :, P:2 * P])
                    bf[b1] = [t]
            gram = t
            for q, (n0, n) in enumerate(((0, 4), (4, 2))):
                for par in range(2):
                    b = 2 * par + q
                    hs = [2 * (n0 + k) + par for k in range(n)]
                    t = emit([(ps[b][:, k * P:k * P + P], KK[H(h)], AA[H(h)], True, True) for k, h in enumerate(hs)], bf[b])
                    t = cp(AP_[:, hs[0]:hs[-1] + 1:2, :], M_(K_SL).unsqueeze(1).to_broadcast([P, n, P]),
                           ps[b][:, 0:n * P].rearrange("p (k t) -> p k t", k=n), t)
                    bf[b] = [t]
            gram = [gram, t]

            xt_ = {g: gram for g in range(3)}
            for lv in range(6):
                bl = 2 << lv
                odd = lambda a: a.rearrange("p (n two b) -> p n two b", two=2, b=bl)[:, :, 1, :]
                lm = C(K_LV + 64 * lv, 64)
                tT, tQ = {}, {}
                for g in range(3):
                    b, bq = g, 3 + g
                    pe.wait(bf[b], xt_[g])
                    for k in range(4):
                        f = lambda e, b=b, k=k, g=g: e.transpose(ps[b][:, k * P:k * P + P], XI[:, 4 * g + k, :], ident)
                        t = pe.do(f) if k == 3 else pe.go(f)
                    tT[g] = fn(TI[:, 4 * g:4 * g + 4, :], ps[b][:, :].rearrange("p (k t) -> p k t", k=4), ACT.Copy, t)
                    bf[b] = [tT[g]]
                    t = emit([(ps[bq][:, 64 * k:64 * k + 64], AP_[:, 4 * g + k, :], odd(XI[:, 4 * g + k, :]), True, True)
                              for k in range(4)], bf[bq])
                    tQ[g] = tt(Qm[:, 4 * g:4 * g + 4, :], ps[bq][:, 0:256].rearrange("p (k t) -> p k t", k=4),
                               lm.unsqueeze(1).to_broadcast([P, 4, 64]), ALU.mult, t)
                    bf[bq] = [tQ[g]]
                for g in range(3):
                    bq = 3 + g
                    t = emit([(ps[bq][:, 256 + 64 * k:320 + 64 * k], TI[:, 4 * g + k, :], Qm[:, 4 * g + k, :], True, True)
                              for k in range(4)], tT[g], tQ[g])
                    xo = XI[:, 4 * g:4 * g + 4, :].rearrange("p k (n two b) -> p k n two b", two=2, b=bl)
                    dx = ps[bq][:, 256:512].rearrange("p (k n b) -> p k n b", k=4, b=bl)
                    for_k = [(xo[:, k, :, 1, :], dx[:, k, :, :]) for k in range(4)] if bl < 64 else \
                            [(xo[:, :, 0, 1, :], dx[:, :, 0, :])]
                    for xo_, dx_ in for_k:
                        t = tt(xo_, xo_, dx_, ALU.add, t)
                    bf[bq] = [t]
                    xt_[g] = t
            inv = list(xt_.values())
            probe(f"XI{ck}", XI[:, :, :], inv)

            par_of = lambda a, par: a.rearrange("p (c two d) -> p c two d", two=2, d=64)[:, :, par, :]
            hcol = lambda h: slice(64 * (h // 2), 64 * (h // 2) + 64)
            half = lambda b: ps[b][:, 0:384].rearrange("p (c d) -> p c d", d=64)
            x_t, u_t = [], []
            for par, b in ((0, 6), (1, 7)):
                lst = []
                for h in range(par, 12, 2):
                    v_ = Vtm[:, ck, 64 * h:64 * h + 64]
                    lst.append((ps[b][:, hcol(h)], BM[:, h, 0:P], v_, True, ck == 0))
                    if ck:
                        lst.append((ps[b][:, hcol(h)], KK[H(h)], Z0[H(h)[0], h // 2, :], False, True))
                t = emit(lst, bf[b], v_t, z_ok, inv)
                t = fn(par_of(Xs[:, :], par), half(b), ACT.Copy, t)
                bf[b] = [t]
                x_t.append(t)
            for (par, b), t in zip(((0, 6), (1, 7)), x_t):
                t = emit([(ps[b][:, hcol(h)], XI[:, h, :], Xs[:, 64 * h:64 * h + 64], True, True) for h in range(par, 12, 2)],
                         bf[b], t)
                t = fn(par_of(Us[:, :], par), half(b), ACT.Copy, t)
                bf[b] = [t]
                u_t.append(t)
            u_done = u_t[-1]
            if ck == 0:
                for q, (b, n) in enumerate(((0, 4), (1, 2))):
                    lst = []
                    for k in range(n):
                        s_ = slice((4 * q + k) * P, (4 * q + k + 1) * P)
                        lst += [(ps[b][:, k * P:k * P + P], khT[:, s_], Vtm[:, 0, s_], True, False),
                                (ps[b][:, k * P:k * P + P], nbT[:, s_], Us[:, s_], False, True)]
                    t = emit(lst, bf[b], kb_tok, u_t)
                    for o in range(2):
                        pr = slice(64 * o, 64 * o + 64)
                        z_ok = tt(Z0[pr, 4 * q:4 * q + n, :],
                                  ps[b][pr, 0:n * P].rearrange("p (k t) -> p k t", k=n)[:, :, 64 * o:64 * o + 64],
                                  zsc[pr, 4 * q:4 * q + n].unsqueeze(2).to_broadcast([64, n, 64]), ALU.mult, t, zs_tok)
                    bf[b] = [z_ok]
            for par, b in ((0, 6), (1, 7)):
                lst = []
                for h in range(par, 12, 2):
                    v_ = Vtm[:, ck, 64 * h:64 * h + 64]
                    lst.append((ps[b][:, hcol(h)], BM[:, h, P:2 * P], v_, True, False))
                    lst.append((ps[b][:, hcol(h)], MR[:, h, :], Us[:, 64 * h:64 * h + 64], False, ck == 0))
                    if ck:
                        lst.append((ps[b][:, hcol(h)], Rr[H(h)], Z0[H(h)[0], h // 2, :], False, True))
                t = emit(lst, bf[b], u_t)
                o_done = t
                o3, oc3 = half(b), par_of(oc[:, ck, :], par)
                sm, vr, rr = (st[:, 144 + 12 * k + 6 * par:150 + 12 * k + 6 * par] for k in range(3))
                bc = lambda a: a.unsqueeze(2).to_broadcast([P, 6, 64])
                sq = junk[:, 384 * par:384 * par + 384]
                t = dve.do(lambda e, sm=sm, o3=o3: e.tensor_reduce(sm, o3, AX.X, ALU.add), t, bv_tok, v_t)
                t = ts(sm, sm, 1.0 / 64, None, ALU.mult, ALU.bypass, t)
                t = tt(oc3, o3, bc(sm), ALU.subtract, t)
                bf[b] = [t]
                t = fn(sq.rearrange("p (c d) -> p c d", d=64), oc3, ACT.Square, t)
                t = dve.do(lambda e, vr=vr, sq=sq: e.tensor_reduce(vr, sq.rearrange("p (h d) -> p h d", d=64), AX.X, ALU.add), t)
                t = rstd_of(vr, rr, t, LNX_EPS, 1.0 / 64)
                y_tok.append(tt(oc3, oc3, bc(rr), ALU.mult, t))
        probe("oc", oc, y_tok)
        s1.close()

        s1 = ExitStack()
        rc = lambda nm, sh, d=F32: s1.enter_context(nc.sbuf_tensor("r" + nm, sh, d))
        yh, yl = rc("yh", [P, 8, T], F32R), rc("yl", [P, 8, T], F32R)
        yT = {}
        for q in range(3):
            b = 2 + q
            pe.wait(bf[b], y_tok)
            for k in range(2):
                for ck in range(2):
                    f = lambda e, b=b, k=k, ck=ck, q=q: e.transpose(
                        ps[b][:, k * T + ck * P:k * T + ck * P + P], oc[:, ck, (2 * q + k) * P:(2 * q + k + 1) * P], ident)
                    t = pe.do(f) if (k, ck) == (1, 1) else pe.go(f)
            two_ = slice(2 * q, 2 * q + 2)
            for k in range(2):
                c = 2 * q + k
                t = ts(Kk[:, c, :], ps[b][:, k * T:k * T + T], V("rwkv_lnx_g_2", c), V("rwkv_lnx_b_2", c), ALU.mult, ALU.add, t)
            bf[b] = [t]
            t = tt(Kk[:, two_, :], Kk[:, two_, :], BV[:, two_, :], ALU.add, t)
            t = tt(Kk[:, two_, :], Kk[:, two_, :], GG[:, two_, :], ALU.mult, t)
            yT[2 * q] = yT[2 * q + 1] = split_evac(Kk[:, two_, :], yh[:, two_, :], yl[:, two_, :], t)
        yT[6] = yT[7] = split_evac(mo[:, :, :], yh[:, 6:8, :], yl[:, 6:8, :], mo_tok, y_tok, o_done)
        probe("headsT", yh[:, :, :].bitcast(F32), yT[6], yT[5])
        pay()
        t = mm_d("wo0", yh, yl, yT, 8)
        xk = ln_add(t, 1.0, xa, *g0b0)
        probe("xw0", x[:, :, :], xk)
        s1.close()
        rs.close()

        xk = half_ffn("f2", 0, 2, xk)
        xk = half_ffn("f3", 1, 0, xk)

        rs = ExitStack()
        ra = lambda nm, sh, d=F32: rs.enter_context(nc.sbuf_tensor("b" + nm, sh, d))
        xh, xl = ra("xh", [P, 8, T], F32R), ra("xl", [P, 8, T], F32R)
        yh, yl = ra("yh", [P, 8, T], F32R), ra("yl", [P, 8, T], F32R)
        qT, kT = ra("qT", [P, 6, T]), ra("kT", [P, 6, T])
        mqT, mo = ra("mq", [P, 2, T]), ra("mo", [P, 2, T])
        vt = ra("vt", [P, 2, C7])
        m3 = ra("m3", [P, 384])
        NS = 3
        sa, sl_, sw, sk = (ra(n, [P, NS, 384]) for n in ("sa", "sl", "sw", "sk"))
        pbm, pTm = ra("pbm", [P, 2, 2, T]), ra("pTm", [P, 2, 2, T])
        xt = to_T(x, xh, xl, xk)
        xa = scale_x(xt)
        gb_ = norm_of(1, 1)
        m_tok = [pool.do(lambda e, o=o, k=k: e.tensor_copy(m3[:, o:o + P], C(k, P)), xk)
                 for o, k in ((0, K_SU), (P, K_ONE), (2 * P, K_SU))]
        q_tok, k_tok, v_tok3 = [], [], []
        for c in range(3):
            banks = (0, 1) if c % 2 == 0 else (2, 3)
            t = mm_w("sb", 512 * c, xh, xl, xt, banks)
            for q in range(2):
                b, j = banks[q], 4 * c + 2 * q
                src = ps[b][:, :].rearrange("p (k t) -> p k t", k=2)
                if j < 6:
                    t2 = fn(qT[:, j:j + 2, :], src, ACT.Copy, t, scale=0.125)
                    q_tok.append(t2)
                else:
                    t2 = fn(kT[:, j - 6:j - 4, :], src, ACT.Copy, t)
                    k_tok.append(t2)
                bf[b] = [t2]
        for c, (n0, w, banks) in enumerate(((1536, 512, (2, 3)), (2048, 256, (0, 1)))):
            t = mm_x("sb", n0, xh, xl, xt, banks)
            for rb in range(2):
                b = banks[rb]
                t2 = fn(vt[:, rb, 512 * c:512 * c + w], ps[b][:, 0:w], ACT.Copy, t)
                bf[b] = [t2]
                v_tok3.append(t2)
        t = mm_w("sb", 2304, xh, xl, xt, (2,))
        mq_tok = fn(mqT[:, :, :], ps[2][:, :].rearrange("p (k t) -> p k t", k=2), ACT.Copy, t)
        bf[2] = [mq_tok]

        free_s = {}
        att_tok, w_tok2, lk_tok = {}, {}, {}

        def sb_scores(h):
            s, b = h % NS, h % 2
            o, c = slice(64 * (h % 2), 64 * (h % 2) + 64), h // 2
            z = ps[b][:, 0:384]
            t = emit([(ps[b][:, 0:T], kT[o, c, 0:P], qT[o, c, :], True, True),
                      (ps[b][:, T:384], kT[o, c, P:T], qT[o, c, P:T], True, True)], bf[b], q_tok, k_tok)
            t = fn(sa[:, s, :], z, ACT.Abs, t, free_s.get(s))
            t = fn(sa[:, s, :], sa[:, s, :], ACT.Exp, t, scale=-1.0)
            t = fn(sa[:, s, :], sa[:, s, :], ACT.Ln, t, bias=1.0)
            t = stt(sl_[:, s, :], z, 0.0, sa[:, s, :], ALU.max, ALU.add, t)
            w_tok2[h] = tt(sw[:, s, :], z, sl_[:, s, :], ALU.subtract, t, free_s.get(s))
            bf[b] = [w_tok2[h]]
            lk_tok[h] = stt(sk[:, s, :], sl_[:, s, :], -1.0, m3[:, :], ALU.mult, ALU.mult, m_tok)

        def sb_later(h):
            s, b = h % NS, 2 + h % 2
            tri, one = C(K_SL, P), C(K_ONE, P)
            t = emit([(ps[b][:, 0:T], tri, sk[:, s, 0:T], True, False),
                      (ps[b][:, P:T], one, sk[:, s, T:384], False, True),
                      (ps[b][:, T:384], tri, sk[:, s, T:384], True, True)], bf[b], lk_tok[h])
            t = tt(sw[:, s, :], sw[:, s, :], ps[b][:, 0:384], ALU.add, t, w_tok2[h])
            bf[b] = [t]
            t = fn(sw[:, s, :], sw[:, s, :], ACT.Exp, t)
            att_tok[h] = pool.do(lambda e: e.tensor_tensor(sw[:, s, :], sw[:, s, :], m3[:, :], ALU.mult), t)

        yT = {}

        def sb_out(c):
            b = 4 + c % 2
            lst = []
            for k in range(2):
                s = (2 * c + k) % NS
                lst += [(ps[b][:, k * T:k * T + T], vt[:, 0, c * P:c * P + P], sw[:, s, 0:T], True, False),
                        (ps[b][:, k * T + P:k * T + T], vt[:, 1, c * P:c * P + P], sw[:, s, T:384], False, True)]
            t = emit(lst, bf[b], att_tok[2 * c], att_tok[2 * c + 1], v_tok3)
            for k in range(2):
                free_s[(2 * c + k) % NS] = t
            for k in range(2):
                o = slice(64 * k, 64 * k + 64)
                yT[c] = split_evac(ps[b][o, k * T:k * T + T], yh[o, c, :], yl[o, c, :], t)
            bf[b] = [yT[c]]

        for h in range(13):
            if h < 12:
                sb_scores(h)
            if h >= 1:
                sb_later(h - 1)
                if h % 2 == 0:
                    sb_out(h // 2 - 1)
        mo_tok = mem_attn(mqT, mq_tok, mo, pbm, pTm, (2, 3), (6, 7), (0, 1))
        yT[6] = yT[7] = split_evac(mo[:, :, :], yh[:, 6:8, :], yl[:, 6:8, :], mo_tok)
        probe("headsT1", yh[:, :, :].bitcast(F32), yT[6], yT[5])
        pay()
        t = mm_d("wo1", yh, yl, yT, 8)
        xk = ln_add(t, 1.0, xa, *gb_)
        probe("xw1", x[:, :, :], xk)
        rs.close()

        xk = half_ffn("f4", 1, 2, xk)

        s_out = Dmas(sem("s_out"))
        t = s_out.start(sp, out[0].rearrange("(b p) d -> p b d", p=P), x[:, :, :], xk)
        sp.wait(t)
        assert used[0] == NU, (used[0], NU)


def constants():
    c = np.zeros((P, NCST), np.float32)
    i, j = np.arange(P)[:, None], np.arange(P)[None, :]
    c[:, K_ID:K_ID + P] = i == j
    c[:, K_AM:K_AM + P] = c[:, K_AM + 2 * P:K_AM + 3 * P] = np.where(j > i, np.float32(NEG), np.float32(0))
    c[:, K_SU:K_SU + P] = i < j
    c[:, K_IU:K_IU + P] = i <= j
    c[:, K_M1:K_M1 + P] = (j == i + 1) & (i % 2 == 0)
    c[:, K_SL:K_SL + P] = i > j
    for lv in range(6):
        b = 2 << lv
        odd = (np.arange(64) // b) * 2 * b + b + np.arange(64) % b
        row = np.arange(P)[:, None]
        c[:, K_LV + 64 * lv:K_LV + 64 * lv + 64] = (row // (2 * b) == odd[None, :] // (2 * b)) & (row // b % 2 == 0)
    c[:, K_ONE:K_ONE + P] = 1
    c[:, K_SEL2:K_SEL2 + 2] = i // 64 == np.arange(2)[None, :]
    c[:, K_FREQ:K_FREQ + 8] = np.float32(500000.0) ** (-np.arange(0, 16, 2, dtype=np.float32) / np.float32(16))
    c[:, K_HALF:K_HALF + 24] = -0.5
    c[:, K_BO:K_BO + P] = i // 64 == j // 64
    f = np.arange(C7)[None, :]
    c[0:12, K_SELH:K_SELH + C7] = np.arange(12)[:, None] == f // 64
    s = np.arange(T)[:, None, None]
    w = np.array([2, 4, 8, 16])[None, :, None]
    t = np.arange(T)[None, None, :]
    band = np.where((s <= t) & (s > t - w), np.float32(1) / np.minimum(t + 1, w).astype(np.float32), np.float32(0))
    band = (band - (s == t)).astype(np.float32)
    band = band.reshape(2, P, 4, T).transpose(1, 0, 2, 3).reshape(P, 8 * T)
    return c, np.ascontiguousarray(band)


NAMES = [
    "x", "mem", "positions", "g_mix_pre", "w_in", "lambda_q1", "lambda_k1", "lambda_q2", "lambda_k2", "g_subln",
    "w_pool", "pool_scale", "w_out", "g_mix_post", "g_x_pre", "g_mem", "w_xq", "w_xkv", "w_xo", "g_x_post",
    "g_ffn_pre", "w_gate", "w_up", "w_down", "g_ffn_post", "mem_2", "ffn1_w_gate_2", "ffn1_w_up_2",
    "ffn1_w_down_2", "ffn2_w_gate_2", "ffn2_w_up_2", "ffn2_w_down_2", "ln_g_2", "ln_b_2", "w_out_2",
    "w_mem_kv_2", "rwkv_w_in_2", "rwkv_mu_2", "rwkv_w0_2", "rwkv_w_up_2", "rwkv_a0_2", "rwkv_a_up_2",
    "rwkv_g_up_2", "rwkv_k_k_2", "rwkv_k_a_2", "rwkv_r_k_2", "rwkv_lnx_g_2", "rwkv_lnx_b_2", "sb_w_in_2",
]


def kernel(**inputs):
    import concourse.bacc as bacc
    from concourse.bass_utils import run_bass_kernel_spmd

    nc = bacc.Bacc("TRN2", target_bir_lowering=False, num_devices=1)
    arrays, args = {}, {}
    for name in NAMES:
        a = np.ascontiguousarray(inputs[name])
        arrays["in_" + name] = a
        args[name] = nc.dram_tensor("in_" + name, a.shape, mybir.dt.from_np(a.dtype), kind="ExternalInput").ap()
    consts = []
    for name, a in zip(("c_tables", "c_band"), constants()):
        arrays[name] = a
        consts.append(nc.dram_tensor(name, a.shape, F32, kind="ExternalInput").ap())
    out = nc.dram_tensor("out_x", (1, T, D), F32, kind="ExternalOutput").ap()
    build_program(nc, args, consts[0], consts[1], out)
    r = run_bass_kernel_spmd(nc, [arrays], core_ids=[0])
    return r.results[0]["out_x"]
```

```python
import math
from contextlib import ExitStack

import numpy as np
import concourse.bass as bass
from concourse import mybir

F32 = mybir.dt.float32
F32R = mybir.dt.float32r
I32 = mybir.dt.int32
ALU = mybir.AluOpType
ACT = mybir.ActivationFunctionType
AX = mybir.AxisListType

P = 128
T = 256
D = 1024
FF = 2816
NF = FF // P
LAM0 = 0.8 - 0.6 * math.exp(0.0)
EPS = 1e-6
LN_EPS = 1e-5
LNX_EPS = 64e-5
ALPHA = 4.0 ** 0.25
C7 = 768
HC = C7 // P
NEG = -3.0e38

NR, NH = 4, 6
TAIL = 3
UW = 1024

K_ID, K_AM, K_SU, K_IU, K_M1, K_SL, K_LV = 0, 128, 512, 640, 768, 896, 1024
K_ONE, K_SEL2, K_FREQ, K_BO, K_SELH = 1408, 1536, 1538, 1546, 1674
NCST = K_SELH + C7

RW = [(2304, 256), (768, 512), (1280, 256), (0, 512), (512, 256), (1536, 512), (2048, 256), (2560, 256)]

VROWS = [("pool_scale", 4), ("g_subln", 1), ("rwkv_mu_2", 20), ("rwkv_w0_2", 6), ("rwkv_a0_2", 6),
         ("rwkv_k_k_2", 6), ("rwkv_k_a_2", 6), ("rwkv_r_k_2", 6), ("rwkv_lnx_g_2", 6), ("rwkv_lnx_b_2", 6)]
NV = sum(n for _, n in VROWS)


class Lane:

    def __init__(self, engine, sem):
        self.e, self.sem, self.n, self.seen = engine, sem, 0, {}

    def wait(self, *tokens):
        for t in tokens:
            if isinstance(t, list):
                self.wait(*t)
            elif t is not None and self.seen.get(t[0].name, 0) < t[1]:
                self.seen[t[0].name] = t[1]
                self.e.wait_ge(t[0], t[1])

    def go(self, fn, *after):
        self.wait(*after)
        fn(self.e)

    def do(self, fn, *after):
        self.wait(*after)
        self.n += 1
        fn(self.e).then_inc(self.sem, 1)
        return (self.sem, self.n)


class Dmas:

    def __init__(self, sem):
        self.sem, self.n = sem, 0

    def start(self, lane, out, in_, *after, **how):
        lane.wait(*after)
        self.n += 16
        lane.e.dma_start(out, in_, **how).then_inc(self.sem, 16)
        return (self.sem, self.n)


def cols(w, k0, nk, n0, n):
    return w[k0 * P:(k0 + nk) * P, n0:n0 + n].rearrange("(k p) n -> p k n", p=P)


def chunk(name, w, n0, n, nk=8):
    per = UW // n
    return [((name, n0), cols(w, k, per, n0, n), per, n) for k in range(0, nk, per)]


def build_program(nc, I, cst_in, band_in, out, dbg=None):
    es = ExitStack()
    with es:
        sem = lambda n: es.enter_context(nc.semaphore(n))
        sb = lambda n, s, d=F32: es.enter_context(nc.sbuf_tensor(n, s, d))
        pe, act, dve, pool, sp = (
            Lane(e, sem("s_" + n)) for e, n in ((nc.tensor, "pe"), (nc.scalar, "act"), (nc.vector, "dve"),
                                                (nc.gpsimd, "pool"), (nc.sync, "sp")))
        s_raw = [sem(f"s_raw{i}") for i in range(NR)]
        ps = [es.enter_context(nc.psum_tensor(f"ps{i}", [P, 512], F32)) for i in range(8)]
        bf = [[] for _ in range(8)]

        raw = sb("raw", [P, NR, UW])
        wh = sb("wh", [P, NH, UW], F32R)
        wl = sb("wl", [P, NH, UW], F32R)
        x = sb("xres", [P, 2, D])
        gb = sb("gb", [P, 2, D])
        at = nc.sbuf_base
        xh = sb("xh", [P, 8, T], F32R)
        xl = sb("xl", [P, 8, T], F32R)
        xf = nc.alloc_sbuf_tensor_at("xf", [P, 2, 2048], F32, offset=at)
        cst = sb("cst", [P, NCST])
        vcol = sb("vcol", [P, NV])
        vrow = sb("vrow", [P, P])
        junk = sb("junk", [P, D])
        st = sb("st", [P, 256])
        mk2 = sb("mk2", [P, 2, T])
        mv2 = sb("mv2", [P, 2, T])
        pos_i = sb("pos_i", [P, 2], I32)
        mhalf = sb("mhalf", [P, 24])

        ident = cst[:, K_ID:K_ID + P]
        C = lambda k, n, p=P: cst[0:p, k:k + n]

        W = {k: v for k, v in I.items()}
        ffn_list = lambda nm, g, u, d: sum(
            [chunk(nm + "g", g, n, min(512, FF - n)) + chunk(nm + "u", u, n, min(512, FF - n))
             for n in range(0, FF, 512)], []) + chunk(nm + "d", d, 0, D, NF)
        plan = []
        for n in range(4):
            plan += chunk("w_in", I["w_in"], 512 * n, 512)
        for n in range(3):
            plan += chunk("w_xkv", I["w_xkv"], 512 * n, 512)
        last_xkv = chunk("w_xkv", I["w_xkv"], 1536, 512)
        mkv = [chunk("mkv", I["w_mem_kv_2"], 256 * n, 256) for n in range(2)]
        plan += last_xkv[:1] + chunk("w_out", I["w_out"], 0, D) + last_xkv[1:]
        for n in range(2):
            plan += chunk("w_xq", I["w_xq"], 512 * n, 512)
        plan += chunk("w_xo", I["w_xo"], 0, D)
        plan += mkv[0] + ffn_list("f0", I["w_gate"], I["w_up"], I["w_down"])
        plan += ffn_list("f1", I["ffn1_w_gate_2"][0], I["ffn1_w_up_2"][0], I["ffn1_w_down_2"][0]) + mkv[1]
        for n0, n in RW:
            plan += chunk("rw", I["rwkv_w_in_2"][0], n0, n)
        plan += chunk("wo0", I["w_out_2"][0], 0, D)
        plan += ffn_list("f2", I["ffn2_w_gate_2"][0], I["ffn2_w_up_2"][0], I["ffn2_w_down_2"][0])
        plan += ffn_list("f3", I["ffn1_w_gate_2"][1], I["ffn1_w_up_2"][1], I["ffn1_w_down_2"][1])
        plan += chunk("sb", I["sb_w_in_2"][0], 1536, 512)
        for n in range(3):
            plan += chunk("sb", I["sb_w_in_2"][0], 512 * n, 512)
        plan += chunk("sb", I["sb_w_in_2"][0], 2304, 256) + chunk("sb", I["sb_w_in_2"][0], 2048, 256)
        plan += chunk("wo1", I["w_out_2"][1], 0, D)
        plan += ffn_list("f4", I["ffn2_w_gate_2"][1], I["ffn2_w_up_2"][1], I["ffn2_w_down_2"][1])

        NU = len(plan)
        used = [0]
        hi_tok, lo_tok, pe_tok = {}, {}, {}
        owed = []

        def load(i):
            if i >= NU:
                return
            _, src, nk, n = plan[i]
            dst = raw[:, i % NR, :].rearrange("p (k n) -> p k n", k=nk)
            sp.wait(lo_tok.get(i - NR))
            sp.e.dma_start(dst, src).then_inc(s_raw[i % NR], 16)

        def split(i):
            if i >= NU:
                return
            came, freed = (s_raw[i % NR], 16 * (i // NR + 1)), pe_tok.get(i - NH)
            r, h, l = raw[:, i % NR, :], wh[:, i % NH, :], wl[:, i % NH, :]
            hi_tok[i] = act.do(lambda e: e.activation(h, r, ACT.Copy), came, freed)
            lo_tok[i] = dve.do(lambda e: e.tensor_tensor(l, r, h.bitcast(F32), ALU.subtract), hi_tok[i], freed)
            load(i + NR)

        def use(name):
            i = used[0]
            used[0] += 1
            assert plan[i][0] == name, (plan[i][0], name)
            _, _, nk, n = plan[i]
            view = lambda t: t[:, i % NH, :].rearrange("p (k n) -> p k n", k=nk)
            pe.wait(hi_tok[i], lo_tok[i])
            return i, nk, n, view(wh), view(wl)

        def release(i, tok, hold=False):
            pe_tok[i] = tok
            if hold:
                owed.append(i + NH)
            else:
                pay()
                split(i + NH)

        def pay():
            while owed:
                split(owed.pop(0))

        def mm(o, l, r, start, stop):
            return lambda e: e.matmul(o, l, r, start=start, stop=stop, skip_group_check=True)

        def three(lst, o, lh, ll, rh, rl, start, stop):
            lst += [(o, lh, rh, start, False), (o, lh, rl, False, False), (o, ll, rh, False, stop)]

        def emit(lst, *after):
            pe.wait(*after)
            for a in lst[:-1]:
                pe.go(mm(*a))
            return pe.do(mm(*lst[-1]))

        def aside(side):
            if side:
                side.pop(0)()

        def put_x(name, n0, xh, xl, xt, banks, hold=False):
            at = {"kt": 0, "open": []}

            def take():
                u = use((name, n0))
                at["open"].append((at["kt"], u))
                at["kt"] += u[1]

            def half(rb):
                lst = []
                a = slice(rb * P, rb * P + P)
                kt, (i, nk, n, h, l) = at["open"][0] if rb else at["open"][-1]
                if kt == 0:
                    pe.wait(bf[banks[rb]])
                for k in range(nk):
                    pe.wait(xt[rb][(kt + k) // 4])
                    three(lst, ps[banks[rb]][:, 0:n], xh[:, kt + k, a], xl[:, kt + k, a], h[:, k, :], l[:, k, :],
                          kt + k == 0, kt + k == 7)
                tok = emit(lst)
                if rb:
                    at["open"].pop(0)
                    release(i, tok, hold)
                return tok

            return take, half

        def mm_x(name, n0, xh, xl, xt, banks, hold=False, side=None, lead=0, mid=None):
            take, half = put_x(name, n0, xh, xl, xt, banks, hold)
            per = sum(1 for q in plan if q[0] == (name, n0))
            for _ in range(lead):
                take()
                half(0)
            if mid is not None:
                mid()
            for _ in range(lead):
                tok = half(1)
            for _ in range(per - lead):
                take()
                t0 = half(0)
                tok = half(1)
                aside(side)
            return [t0, tok]

        def mm_w(name, n0, xh, xl, xt, banks, hold=False, side=None):
            kt = 0
            while kt < 8:
                i, nk, n, h, l = use((name, n0))
                nj = n // P
                lst = []
                for k in range(nk):
                    pe.wait(xt[0][(kt + k) // 4], xt[1][(kt + k) // 4])
                    for j in range(nj):
                        if kt + k == 0 and j % 2 == 0:
                            pe.wait(bf[banks[j // 2]])
                        o = ps[banks[j // 2]][:, (j % 2) * T:(j % 2) * T + T]
                        s = slice(j * P, j * P + P)
                        st_, sp_ = kt + k == 0 and j % 2 == 0, kt + k == 7
                        lst += [(o, h[:, k, s], xh[:, kt + k, :], st_, False),
                                (o, h[:, k, s], xl[:, kt + k, :], False, False),
                                (o, l[:, k, s], xh[:, kt + k, :], False, sp_)]
                tok = emit(lst)
                kt += nk
                release(i, tok, hold)
                aside(side)
            return tok

        DN = [[6, 7], [0, 1]]

        def mm_d(name, ah, al, at, nk, mid=None):
            for b in DN[0] + DN[1]:
                pe.wait(bf[b])

            def part(kt, rb, h, l):
                lst = []
                a = slice(rb * P, rb * P + P)
                for nh in range(2):
                    s = slice(nh * 512, nh * 512 + 512)
                    three(lst, ps[DN[rb][nh]][:, :], ah[:, kt, a], al[:, kt, a], h[:, 0, s], l[:, 0, s],
                          kt == 0, kt == nk - 1)
                return emit(lst, at[kt])

            tail = []
            for kt in range(nk):
                if kt == 3 and mid is not None:
                    mid()
                i, _, _, h, l = use((name, 0))
                t0 = part(kt, 0, h, l)
                if kt < nk - TAIL:
                    release(i, part(kt, 1, h, l))
                else:
                    tail.append((i, kt, h, l))
            for i, kt, h, l in tail:
                t1 = part(kt, 1, h, l)
                release(i, t1, True)
            return [t0, t1]

        def split_evac(src, hi, lo, *after):
            t = act.do(lambda e: e.activation(hi, src, ACT.Copy), *after)
            return dve.do(lambda e: e.tensor_tensor(lo, src, hi.bitcast(F32), ALU.subtract), t)

        def turn(src, rb, hi, lo, after, banks, between=None):
            toks = []
            for g in range(2):
                b = banks[g]
                pe.wait(bf[b], after[g])
                for k in range(4):
                    f = lambda e: e.transpose(ps[b][:, k * P:k * P + P], src[:, rb, (4 * g + k) * P:(4 * g + k + 1) * P], ident)
                    t = pe.do(f) if k == 3 else pe.go(f)
                v = ps[b][:, :].rearrange("p (k t) -> p k t", k=4)
                d = slice(rb * P, rb * P + P)
                toks.append(split_evac(v, hi[:, 4 * g:4 * g + 4, d], lo[:, 4 * g:4 * g + 4, d], t))
                bf[b] = [toks[-1]]
                if g == 0 and between is not None:
                    between()
            return toks

        def to_T(src, hi, lo, after, banks=((2, 3), (4, 5))):
            return [turn(src, rb, hi, lo, [after[rb]] * 2, banks[rb]) for rb in range(2)]

        def turn_to(src, banks=((4, 5), (6, 7))):
            toks = {}

            def mid(rb, after, between=None):
                toks[rb] = turn(src, rb, xh, xl, after, banks[rb], between)

            return toks, mid

        gn = [0]
        gfree = {}
        s_gain = [Dmas(sem(f"s_gain{i}")) for i in range(2)]

        def gain(vec):
            g = gn[0] % 2
            gn[0] += 1
            t = s_gain[g].start(pool, gb[:, g, :], vec.partition_broadcast(P), gfree.get(g))
            return gb[:, g, :], t, g

        def rstd_of(var, rs, after, eps, scale):
            t = dve.do(lambda e: e.tensor_scalar(var, var, scale, eps, ALU.mult, ALU.add), after)
            n = var.free_size()
            return pool.do(lambda e: e.tensor_tensor(rs, var, mhalf[:, 0:n], ALU.pow), t, half_tok)

        def rms_row(rb, src, after, g, dst):
            gt, gtok, gi = g
            t = square_sum(src[:, rb, :], st[:, rb:rb + 1], D, after, st_free[0])
            t = rstd_of(st[:, rb:rb + 1], st[:, 2 + rb:3 + rb], t, EPS, 1.0 / D)

            def scaled():
                gfree[gi] = dve.do(lambda e: e.scalar_tensor_tensor(
                    out=dst[:, rb, :], in0=src[:, rb, :], scalar=st[:, 2 + rb:3 + rb], in1=gt,
                    op0=ALU.mult, op1=ALU.mult), t, gtok, dst_free[0])
                st_free[0] = gfree[gi]
                return gfree[gi]

            return scaled

        def rms_rows(src, after, g, dst):
            return [rms_row(rb, src, after[rb], g, dst)() for rb in range(2)]

        st_free, dst_free = [None], [None]
        junk_by = [None]

        def square_sum(src, dst, width, *after):
            junk_by[0] = act.do(lambda e: e.activation(junk[:, 0:width], src, ACT.Square, accum_out=dst), junk_by[0], *after)
            return junk_by[0]

        def rms_add(toks, g, tmp, tmp_free, mid, pre=None, early=False):
            gt, gtok, gi = g
            done, rs, scaled = {}, {}, {}

            def head(rb):
                for nh in range(2):
                    c = 8 + 2 * rb + nh
                    t = square_sum(ps[DN[rb][nh]][:, :], st[:, c:c + 1], 512, toks[rb], st_free[0])
                t = dve.do(lambda e: e.tensor_tensor(st[:, 12 + rb:13 + rb], st[:, 8 + 2 * rb:9 + 2 * rb],
                                                     st[:, 9 + 2 * rb:10 + 2 * rb], ALU.add), t)
                rs[rb] = rstd_of(st[:, 12 + rb:13 + rb], st[:, 14 + rb:15 + rb], t, EPS, 1.0 / D)

            def body(rb):
                t = {}
                for nh in range(2):
                    b, s = DN[rb][nh], slice(nh * 512, nh * 512 + 512)
                    t[nh] = dve.do(lambda e: e.scalar_tensor_tensor(
                        out=tmp[:, rb, s], in0=ps[b][:, :], scalar=st[:, 14 + rb:15 + rb], in1=gt[:, s],
                        op0=ALU.mult, op1=ALU.mult), rs[rb], gtok, list(tmp_free))
                    bf[b] = [t[nh]]
                d = []
                for nh in range(2):
                    s = slice(nh * 512, nh * 512 + 512)
                    d.append(dve.do(lambda e: e.tensor_tensor(x[:, rb, s], x[:, rb, s], tmp[:, rb, s], ALU.add), t[nh]))
                gfree[gi] = t[1]
                done[rb] = d

            def norm(rb):
                if pre is not None:
                    scaled[rb] = rms_row(rb, x, done[rb], *pre)

            def norm_end(rb):
                if pre is not None:
                    done[rb] = [scaled[rb]()] * 2

            head(0)
            body(0)
            if early:
                pay()
            norm(0)
            head(1)
            norm_end(0)
            body(1)
            mid(0, done[0])
            norm(1)
            norm_end(1)

            def rest():
                mid(1, done[1])
                pay()
                st_free[0] = done[1][1]

            return rest

        def ln_add(toks, scale, xtok, g, b_, mid):
            (gt, gtok, gi), (bt, btok, bi) = g, b_

            s_ = [slice(nh * 512, nh * 512 + 512) for nh in range(2)]
            summed = {}

            def add(rb, nh):
                b, s = DN[rb][nh], s_[nh]
                summed[rb, nh] = dve.do(lambda e: e.scalar_tensor_tensor(
                    out=x[:, rb, s], in0=ps[b][:, :], scalar=scale, in1=x[:, rb, s],
                    op0=ALU.mult, op1=ALU.add), toks[rb], xtok)
                bf[b] = [summed[rb, nh]]

            def stats(rb):
                t = []
                for nh in range(2):
                    c = 32 + 6 * nh + 12 * rb
                    t.append(dve.do(lambda e: e.bn_stats(st[:, c:c + 6], x[:, rb, s_[nh]]), summed[rb, nh], st_free[0]))
                m, v, r = st[:, 16 + 2 * rb:17 + 2 * rb], st[:, 17 + 2 * rb:18 + 2 * rb], st[:, 20 + rb:21 + rb]
                t = dve.do(lambda e: e.bn_aggr(st[:, 16 + 2 * rb:18 + 2 * rb], st[:, 32 + 12 * rb:44 + 12 * rb]), t)
                tr = rstd_of(v, r, t, LN_EPS, 1.0)
                n = [dve.do(lambda e, s=s: e.scalar_tensor_tensor(out=x[:, rb, s], in0=x[:, rb, s], scalar=m, in1=gt[:, s],
                                                                  op0=ALU.subtract, op1=ALU.mult), t, gtok) for s in s_]
                d = [dve.do(lambda e, s=s: e.scalar_tensor_tensor(out=x[:, rb, s], in0=x[:, rb, s], scalar=r, in1=bt[:, s],
                                                                  op0=ALU.mult, op1=ALU.add), n[i], tr, btok)
                     for i, s in enumerate(s_)]
                gfree[gi] = gfree[bi] = st_free[0] = d[1]
                return d

            add(0, 0)
            add(0, 1)
            d0 = stats(0)
            add(1, 0)
            mid(0, d0, lambda: add(1, 1))
            d1 = stats(1)

            def rest():
                mid(1, d1)
                pay()
            def rest():
                mid(1, d1)
                pay()

            return rest

        def ffn(nm, xt, hb, hh, hl, rest):
            ht = []
            waiting = []
            hb_free = {}

            def back():
                n0, w, slot, toks = waiting.pop()
                for q in range(w // T):
                    b = 4 + q
                    pe.wait(bf[b])
                    for k in range(2):
                        for rb in range(2):
                            o = ps[b][:, k * T + rb * P:k * T + rb * P + P]
                            i_ = hb[:, slot, rb, (2 * q + k) * P:(2 * q + k + 1) * P]
                            pe.wait(toks[rb])
                            f = lambda e, o=o, i_=i_: e.transpose(o, i_, ident)
                            t = pe.do(f) if (k, rb) == (1, 1) else pe.go(f)
                    f0 = n0 // P + 2 * q
                    v = ps[b][:, :].rearrange("p (k t) -> p k t", k=2)
                    t2 = split_evac(v, hh[:, f0:f0 + 2, :], hl[:, f0:f0 + 2, :], t)
                    bf[b] = [t2]
                    ht.extend([t2, t2])
                hb_free[slot] = t

            for c, n0 in enumerate(range(0, FF, 512)):
                w, slot = min(512, FF - n0), c % 2
                tg = mm_x(nm + "g", n0, xh, xl, xt, (0, 1), lead=3 if c == 0 else 0, mid=rest if c == 0 else None)
                sg = []
                for rb in range(2):
                    t = act.do(lambda e, rb=rb, w=w, slot=slot: e.activation(hb[:, slot, rb, 0:w], ps[rb][:, 0:w],
                                                                             ACT.Silu), tg[rb], hb_free.get(slot))
                    bf[rb] = [t]
                    sg.append(t)
                if waiting:
                    back()
                tu = mm_x(nm + "u", n0, xh, xl, xt, (2, 3))
                toks = []
                for rb in range(2):
                    t = dve.do(lambda e, rb=rb, w=w, slot=slot: e.tensor_tensor(
                        hb[:, slot, rb, 0:w], hb[:, slot, rb, 0:w], ps[2 + rb][:, 0:w], ALU.mult), tu[rb], sg[rb])
                    bf[2 + rb] = [t]
                    toks.append(t)
                waiting.append((n0, w, slot, toks))
            return mm_d(nm + "d", hh, hl, ht, NF, back)

        def probe(name, ap, *after):
            if dbg is not None and name in dbg:
                d = Dmas(sem("s_dbg" + name))
                t = d.start(sp, dbg[name], ap, *after)
                sp.wait(t)

        s_i, s_c, s_v, s_l = (Dmas(sem(n)) for n in ("s_i", "s_c", "s_v", "s_l"))
        s_x = [Dmas(sem(f"s_x{rb}")) for rb in range(2)]
        x_in = I["x"][0].rearrange("(b p) d -> p b d", p=P)
        half_tok = pool.do(lambda e: e.memset(mhalf[:, :], -0.5))
        x_tok = [s_x[rb].start(sp, x[:, rb, :], x_in[:, rb, :]) for rb in range(2)]
        g_pre = gain(I["g_mix_pre"])
        id_tok = s_i.start(pool, cst[:, 0:P], cst_in[:, 0:P])
        for i in range(NR):
            load(i)
        vplace, r0 = {}, 0
        for name, n in VROWS:
            vplace[name] = r0
            r0 += n
        V = lambda name, i=0, n=1: vcol[:, vplace[name] + i:vplace[name] + i + n]

        ms = ExitStack()
        mh = ms.enter_context(nc.sbuf_tensor("mh", [P, 8, T], F32R))
        ml = ms.enter_context(nc.sbuf_tensor("ml", [P, 8, T], F32R))
        ph = ExitStack()
        pb = lambda n, s, d=F32: ph.enter_context(nc.sbuf_tensor(n, s, d))
        kxT = pb("kxT", [P, 8, T])
        vx = pb("vx", [P, 2, D])
        tmp = pb("tmp0", [P, 2, D])
        qkT = pb("qkT", [P, 8, T])
        inner = ExitStack()
        ib = lambda n, s, d=F32: inner.enter_context(nc.sbuf_tensor(n, s, d))
        xn = ib("xn", [P, 2, D])
        v_sb = ib("v_sb", [P, 2, 512])
        u_sb = ib("u_sb", [P, 2, 512])
        band = ib("band", [P, 8 * T])
        wpool = ib("wpool", [P, 4, P])
        lam_in = ib("lam_in", [P, 4, 64])
        rope = ib("rope", [P, 16 * 16])
        qk = tmp

        pre = [rms_row(rb, x, x_tok[rb], g_pre, xn) for rb in range(2)]
        xt = {}

        def first(rb):
            t = pre[rb]()
            xt[rb] = turn(xn, rb, xh, xl, [[t, id_tok]] * 2, ((2, 3), (4, 5))[rb])

        first(0)
        for i in range(3):
            split(i)
        cst_tok = s_c.start(pool, cst[:, P:NCST], cst_in[:, P:NCST])
        for name, n in VROWS:
            src = I[name]
            if len(src.shape) == 3:
                src = src.rearrange("a h d -> (a h d)")
            elif len(src.shape) == 2:
                src = src.rearrange("a d -> (a d)")
            v_tok = s_v.start(pool, vrow[vplace[name]:vplace[name] + n, :], src.rearrange("(r p) -> r p", p=P))
        for j, name in enumerate(("lambda_q1", "lambda_q2", "lambda_k1", "lambda_k2")):
            l_tok = s_l.start(pool, lam_in[:, j, :], I[name].partition_broadcast(P))
        s_pos, s_band, s_mem = Dmas(sem("s_pos")), Dmas(sem("s_band")), Dmas(sem("s_mem"))
        pos_tok = s_pos.start(pool, pos_i[:, :], I["positions"].rearrange("a (b p) -> p (a b)", p=P),
                          allow_slow_non_contiguous=True)
        band_tok = s_band.start(pool, band[:, :], band_in)
        wp_tok = s_band.start(pool, wpool[:, :, :], I["w_pool"].rearrange("g c d -> c g d"))
        mem_tok = s_mem.start(pool, vx[:, :, :], I["mem"][0].rearrange("(b p) d -> p b d", p=P))


        def second():
            first(1)
            for i in range(3, NH):
                split(i)

        rot = []
        for c in range(2):
            banks = (0, 1) if c == 0 else (2, 3)
            tq = mm_x("w_in", 512 * c, xh, xl, xt, banks, **(dict(lead=3, mid=second) if c == 0 else {}))
            for rb in range(2):
                b = banks[rb]
                t = act.do(lambda e, b=b, rb=rb, c=c: e.activation(qk[:, rb, 512 * c:512 * c + 512], ps[b][:, :],
                                                                   ACT.Copy), tq[rb])
                bf[b] = [t]
                rot.append(t)
        g_mem = gain(I["g_mem"])
        pe.wait(bf[6])
        tv = pe.do(lambda e: e.transpose(ps[6][:, 0:NV], vrow[0:NV, :], cst[0:NV, 0:NV]), v_tok, id_tok)
        v_ok = act.do(lambda e: e.activation(vcol[:, :], ps[6][:, 0:NV], ACT.Copy), tv)
        bf[6] = [v_ok]
        gs_ok = dve.do(lambda e: e.tensor_scalar(V("g_subln"), V("g_subln"), 1.0 - LAM0, None, ALU.mult), v_ok)

        t = dve.do(lambda e: e.tensor_tensor(lam_in[:, 0:2, :], lam_in[:, 0:2, :], lam_in[:, 2:4, :], ALU.mult), l_tok)
        t = dve.do(lambda e: e.tensor_reduce(st[:, 64:66], lam_in[:, 0:2, :], AX.X, ALU.add), t)
        t = act.do(lambda e: e.activation(st[:, 64:66], st[:, 64:66], ACT.Exp), t)
        t = dve.do(lambda e: e.tensor_tensor(st[:, 66:67], st[:, 65:66], st[:, 64:65], ALU.subtract), t)
        nlam = st[:, 66:67]
        lam_ok = dve.do(lambda e: e.tensor_scalar(nlam, nlam, -LAM0, None, ALU.add), t)

        R = lambda k: rope[:, 16 * k:16 * k + 16]
        R3 = lambda k: R(k).rearrange("p (b f) -> p b f", b=2)
        t = dve.do(lambda e: e.tensor_copy(st[:, 68:70], pos_i[:, :]), pos_tok)
        t = dve.do(lambda e: e.tensor_tensor(R3(0), st[:, 68:70].unsqueeze(2).to_broadcast([P, 2, 8]),
                                             C(K_FREQ, 8).unsqueeze(1).to_broadcast([P, 2, 8]), ALU.mult), t, cst_tok)
        t = dve.do(lambda e: e.tensor_scalar(R(1), R(0), 1.0 / (2 * math.pi), 12582912.0, ALU.mult, ALU.add), t)
        t = dve.do(lambda e: e.tensor_scalar(R(1), R(1), -12582912.0, None, ALU.add), t)
        c1 = 6.28125
        c2 = float(np.float32(np.round((2 * math.pi - c1) * 2 ** 20) / 2 ** 20))
        c3 = 2 * math.pi - c1 - c2
        for c in (c1, c2, c3):
            t = dve.do(lambda e, c=c: e.scalar_tensor_tensor(out=R(0), in0=R(1), scalar=-c, in1=R(0),
                                                             op0=ALU.mult, op1=ALU.add), t)
        lim = float(np.nextafter(np.float32(math.pi), np.float32(0)))
        t = dve.do(lambda e: e.tensor_scalar(R(0), R(0), lim, -lim, ALU.min, ALU.max), t)
        t2 = dve.do(lambda e: e.scalar_tensor_tensor(out=R(2), in0=R(0), scalar=-1.0, in1=R(0),
                                                     op0=ALU.mult, op1=ALU.min), t)
        t2 = dve.do(lambda e: e.tensor_scalar(R(2), R(2), math.pi / 2, None, ALU.add), t2)
        t = act.do(lambda e: e.activation(R(3), R(0), ACT.Sin), t)
        rope_ok = act.do(lambda e: e.activation(R(2), R(2), ACT.Sin), t2)
        COS, SIN = R3(2), R3(3)

        rt = {}
        for rb in range(2):
            v = qk[:, rb, :].rearrange("p (h d) -> p h d", d=64)
            t1, t2 = v[:, :, 0:8], v[:, :, 8:16]
            cs, sn = (z[:, rb, :].unsqueeze(1).to_broadcast([P, 16, 8]) for z in (COS, SIN))
            w4 = [junk[:, 128 * j + 512 * rb:128 * j + 512 * rb + 128].rearrange("p (h d) -> p h d", d=8) for j in range(4)]
            tt = lambda o, a, b, op, *w: dve.do(lambda e: e.tensor_tensor(o, a, b, op), *w)
            a1 = tt(w4[0], t1, cs, ALU.mult, rot, rope_ok, junk_by[0])
            a2 = tt(w4[1], t2, sn, ALU.mult)
            a3 = tt(w4[2], t2, cs, ALU.mult)
            a4 = tt(w4[3], t1, sn, ALU.mult)
            tt(t1, w4[0], w4[1], ALU.subtract, a4)
            rt[rb] = tt(t2, w4[2], w4[3], ALU.add)

        tv = mm_x("w_in", 1024, xh, xl, xt, (0, 1))
        v_tok2 = []
        for rb in range(2):
            t = act.do(lambda e, rb=rb: e.activation(v_sb[:, rb, :], ps[rb][:, :], ACT.Copy), tv[rb])
            bf[rb] = [t]
            v_tok2.append(t)
        tu = mm_x("w_in", 1536, xh, xl, xt, (2, 3))
        u_tok = []
        for rb in range(2):
            t = act.do(lambda e, rb=rb: e.activation(u_sb[:, rb, :], ps[2 + rb][:, :], ACT.Copy), tu[rb])
            bf[2 + rb] = [t]
            u_tok.append(t)
        mixed_ready = tu

        qk_tok = []
        for g in range(4):
            b = 4 + g % 2
            pe.wait(bf[b])
            for k in range(2):
                for rb in range(2):
                    pe.wait(rt[rb])
                    o = ps[b][:, k * T + rb * P:k * T + rb * P + P]
                    i_ = qk[:, rb, (2 * g + k) * P:(2 * g + k + 1) * P]
                    f = lambda e, o=o, i_=i_: e.transpose(o, i_, ident)
                    t = pe.do(f) if (k, rb) == (1, 1) else pe.go(f)
            t = act.do(lambda e, b=b, g=g: e.activation(
                qkT[:, 2 * g:2 * g + 2, :], ps[b][:, :].rearrange("p (k t) -> p k t", k=2), ACT.Copy), t)
            bf[b] = [t]
            qk_tok.append(t)
        probe("qkT", qkT[:, :, :], qk_tok)

        dst_free[0] = [xt[0], xt[1]]
        mt = rms_rows(vx, [[mem_tok, rt[0], rt[1]]] * 2, g_mem, xn)
        mt = to_T(xn, mh, ml, mt, banks=((6, 7), (4, 5)))

        pl = xn.rearrange("p b d -> p (b d)")[:, 0:1024].rearrange("p (g t) -> p g t", g=4)
        bandv = band[:, :].rearrange("p (s g t) -> p s g t", s=2, g=4)
        pl_tok = []
        for q in range(2):
            b = 6 + q
            lst = []
            for k in range(2):
                g = 2 * q + k
                for s in range(2):
                    lst.append((ps[b][:, k * T:k * T + T], u_sb[:, s, g * P:g * P + P], bandv[:, s, g, :], s == 0, s == 1))
            t = emit(lst, bf[b], u_tok, band_tok)
            t = act.do(lambda e, b=b, q=q: e.activation(
                pl[:, 2 * q:2 * q + 2, :], ps[b][:, :].rearrange("p (k t) -> p k t", k=2), ACT.Copy), t, mt)
            bf[b] = [t]
            pl_tok.append(t)
        mix_tok = {}
        for q in range(2):
            b = 4 + q
            lst = [(ps[b][:, k * T:k * T + T], wpool[:, 2 * q + k, :], pl[:, 2 * q + k, :], True, True) for k in range(2)]
            t = emit(lst, bf[b], pl_tok, wp_tok)
            half = [ps[b][:, k * T:k * T + T] for k in range(2)]
            for k in range(2):
                g = 2 * q + k
                t1 = act.do(lambda e, k=k, g=g, half=half: e.activation(xh[:, 4 + g, :], half[k], ACT.Copy,
                                                             scale=V("pool_scale", g)), t, v_ok, mixed_ready)
            for k in range(2):
                g = 2 * q + k
                t2 = dve.do(lambda e, k=k, g=g, half=half: e.scalar_tensor_tensor(
                    out=xl[:, 4 + g, :], in0=half[k], scalar=V("pool_scale", g), in1=xh[:, 4 + g, :].bitcast(F32),
                    op0=ALU.mult, op1=ALU.subtract), t1)
                mix_tok[4 + g] = t2
            bf[b] = [t2]

        kx_tok, vx_tok = [], []

        def kx_chunk(c):
            banks = (0, 1) if c == 0 else (2, 3)
            t = mm_w("w_xkv", 512 * c, mh, ml, mt, banks)
            for q in range(2):
                b = banks[q]
                t2 = act.do(lambda e, b=b, j=4 * c + 2 * q: e.activation(
                    kxT[:, j:j + 2, :], ps[b][:, :].rearrange("p (k t) -> p k t", k=2), ACT.Copy), t)
                bf[b] = [t2]
                kx_tok.append(t2)

        def vx_evac(c, banks, t):
            for rb in range(2):
                b = banks[rb]
                t2 = act.do(lambda e: e.activation(vx[:, rb, 512 * c:512 * c + 512], ps[b][:, :], ACT.Copy), t[rb])
                bf[b] = [t2]
                vx_tok.append(t2)

        pbuf = qk[:, 0:2, :].rearrange("p b d -> p (b d)")[:, 0:1536].rearrange("p (s m k) -> p s m k", s=2, m=2)
        pT = inner.enter_context(nc.sbuf_tensor("aT", [P, 4, 3, P], F32))
        p_free = {}
        a_tok = {}
        sc8 = 64 ** -0.5
        KEYS = (slice(0, P), slice(P, 3 * P))

        def scores(h):
            s = h % 2
            banks = (4, 5) if s == 0 else (6, 7)
            c = 72 + 16 * s
            S = lambda k, i, m=0, n=2: st[:, c + 4 * k + 2 * i + m:c + 4 * k + 2 * i + m + n]
            tm = []
            for m in range(2):
                d = slice(64 * m, 64 * m + 64)
                t = emit([(ps[banks[m]][:, KEYS[i]], qkT[d, h, i * P:i * P + P], qkT[d, 4 + h, 0:(i + 1) * P], i == 0, i == 1)
                          for i in range(2)], bf[banks[m]], qk_tok)
                t = dve.do(lambda e, m=m: e.tensor_tensor(pbuf[:, s, m, :], ps[banks[m]][:, 0:384], C(K_AM, 384), ALU.add),
                           t, p_free.get(s), rt[0], rt[1])
                bf[banks[m]] = [t]
                tm.append(t)
            for i in range(2):
                t = dve.do(lambda e, i=i: e.tensor_reduce(S(0, i), pbuf[:, s, :, KEYS[i]], AX.X, ALU.max), tm)
            t = dve.do(lambda e: e.tensor_scalar(st[:, c + 4:c + 8], st[:, c:c + 4], -sc8, None, ALU.mult), t)
            for i in range(2):
                for m in range(2):
                    te = act.do(lambda e, i=i, m=m: e.activation(
                        pbuf[:, s, m, KEYS[i]], pbuf[:, s, m, KEYS[i]], ACT.Exp, scale=sc8, bias=S(1, i, m, 1),
                        accum_out=S(2, i, m, 1)), t)
            t = dve.do(lambda e: e.reciprocal(st[:, c + 12:c + 16], st[:, c + 8:c + 12]), te)
            o2 = st[:, c + 12:c + 16].rearrange("p (i m) -> p i m", i=2)[:, :, 1]
            t = dve.do(lambda e: e.tensor_tensor(o2, o2, nlam.to_broadcast([P, 2]), ALU.mult), t, lam_ok)
            for i in range(2):
                p0, p1 = pbuf[:, s, 0, KEYS[i]], pbuf[:, s, 1, KEYS[i]]
                t2 = dve.do(lambda e, p0=p0, i=i: e.tensor_scalar(p0, p0, S(3, i, 0, 1), None, ALU.mult), t)
                a_tok[h, i] = dve.do(lambda e, p0=p0, p1=p1, i=i: e.scalar_tensor_tensor(
                    out=p0, in0=p1, scalar=S(3, i, 1, 1), in1=p0, op0=ALU.mult, op1=ALU.add), t2)

        aT_tok = {}

        def turn_a(h):
            s = h % 2
            b = 4 + h
            pe.wait(bf[b], a_tok[h, 0], a_tok[h, 1])
            for k in range(3):
                f = lambda e, k=k: e.transpose(ps[b][:, k * P:k * P + P], pbuf[:, s, 0, k * P:k * P + P], ident)
                t = pe.do(f) if k == 2 else pe.go(f)
            p_free[s] = t
            aT_tok[h] = act.do(lambda e: e.activation(
                pT[:, h, :, :], ps[b][:, 0:384].rearrange("p (k t) -> p k t", k=3), ACT.Copy), t)
            bf[b] = [aT_tok[h]]

        kx_chunk(0)
        scores(0)
        scores(1)
        kx_chunk(1)
        turn_a(0)
        turn_a(1)
        scores(2)
        scores(3)
        vx_evac(0, (0, 1), mm_x("w_xkv", 1024, mh, ml, mt, (0, 1)))
        turn_a(2)
        turn_a(3)

        dan = u_sb
        for i in range(2):
            b = 4 + i
            lst = []
            for h in range(4):
                for k in range(i + 1):
                    lst.append((ps[b][:, h * P:h * P + P], pT[:, h, i + k, :], v_sb[:, k, h * P:h * P + P],
                                k == 0, k == i))
            t = emit(lst, bf[b], list(aT_tok.values()), v_tok2)
            sq = junk[:, 512 * i:512 * i + 512]
            t = act.do(lambda e, b=b, sq=sq: e.activation(sq, ps[b][:, :], ACT.Square), t)
            t = dve.do(lambda e, i=i, sq=sq: e.tensor_reduce(st[:, 104 + 4 * i:108 + 4 * i],
                                                      sq.rearrange("p (h d) -> p h d", h=4), AX.X, ALU.add), t)
            t = rstd_of(st[:, 104 + 4 * i:108 + 4 * i], st[:, 112 + 4 * i:116 + 4 * i], t, EPS, 1.0 / P)
            t = dve.do(lambda e, b=b, i=i: e.tensor_tensor(
                dan[:, i, :].rearrange("p (h d) -> p h d", h=4), ps[b][:, :].rearrange("p (h d) -> p h d", h=4),
                st[:, 112 + 4 * i:116 + 4 * i].unsqueeze(2).to_broadcast([P, 4, P]), ALU.mult), t, pl_tok)
            bf[b] = [t]
            if i == 0:
                d0 = t
        d1 = t
        probe("dan", dan[:, :, :], d1)
        vx_take, vx_half = put_x("w_xkv", 1536, mh, ml, mt, (2, 3), True)
        vx_take()
        vx_half(0)
        vx_half(1)
        for q in range(2):
            b = 6 + q
            pe.wait(bf[b])
            for k in range(2):
                for rb in range(2):
                    pe.wait(d0, d1)
                    o = ps[b][:, k * T + rb * P:k * T + rb * P + P]
                    i_ = dan[:, rb, (2 * q + k) * P:(2 * q + k + 1) * P]
                    f = lambda e, o=o, i_=i_: e.transpose(o, i_, ident)
                    t = pe.do(f) if (k, rb) == (1, 1) else pe.go(f)
            v = ps[b][:, :].rearrange("p (k t) -> p k t", k=2)
            t1 = act.do(lambda e, v=v, q=q: e.activation(xh[:, 2 * q:2 * q + 2, :], v, ACT.Copy,
                                                         scale=V("g_subln")), t, gs_ok, mixed_ready)
            t2 = dve.do(lambda e, v=v, q=q: e.scalar_tensor_tensor(
                out=xl[:, 2 * q:2 * q + 2, :], in0=v, scalar=V("g_subln"), in1=xh[:, 2 * q:2 * q + 2, :].bitcast(F32),
                op0=ALU.mult, op1=ALU.subtract), t1)
            bf[b] = [t2]
            mix_tok[2 * q] = mix_tok[2 * q + 1] = t2
        probe("mixT", xh[:, :, :].bitcast(F32), list(mix_tok.values()))

        inner.close()
        xn = pb("xn2", [P, 2, D])
        pbx = pb("pbx", [P, 4, 2, T])
        pTx = pb("pTx", [P, 2, 2, T])
        m2 = pb("m2", [P, 2, D])
        g_post = gain(I["g_mix_post"])
        g_pre = gain(I["g_x_pre"])
        t = mm_d("w_out", xh, xl, mix_tok, 8)
        for _ in range(3):
            vx_take()
            tv = [vx_half(0), vx_half(1)]
        dst_free[0] = t
        m2_tok = s_mem.start(pool, m2[:, :, :], I["mem_2"][0].rearrange("(b p) d -> p b d", p=P), t)
        xt, mid = turn_to(xn)
        rest = rms_add(t, g_post, tmp, list(p_free.values()) + qk_tok, mid, pre=(g_pre, xn), early=True)
        vx_evac(1, (2, 3), tv)
        rest()
        probe("x1", x[:, :, :], xt[1])

        xqT = qkT
        xq_tok = []
        for c in range(2):
            banks = (0, 1) if c == 0 else (2, 3)
            t = mm_w("w_xq", 512 * c, xh, xl, xt, banks)
            for q in range(2):
                b = banks[q]
                t2 = act.do(lambda e, b=b, j=4 * c + 2 * q: e.activation(
                    xqT[:, j:j + 2, :], ps[b][:, :].rearrange("p (k t) -> p k t", k=2), ACT.Copy), t, list(a_tok.values()))
                bf[b] = [t2]
                xq_tok.append(t2)
            xq_done = t

        def soft_attn(nh, qk_pairs, scale, pbuf, pTb, vtile, finish, ktok, vtok, sbanks, tbanks, obanks, at=128):
            free_t, tk = {}, {}

            def one(h):
                s, b, c = h, sbanks[h % len(sbanks)], at + 8 * h
                pw = ps[b][:, :].rearrange("p (b m) -> p b m", b=2)
                lst = []
                for tb in range(2):
                    prs = qk_pairs(h, tb)
                    for j, (l, r) in enumerate(prs):
                        lst.append((pw[:, tb, :], l, r, j == 0, j == len(prs) - 1))
                t = emit(lst, bf[b], ktok)
                t = dve.do(lambda e: e.tensor_reduce(st[:, c:c + 2], pw, AX.X, ALU.max), t, st_att[0])
                t = dve.do(lambda e: e.tensor_scalar(st[:, c + 2:c + 4], st[:, c:c + 2], -scale, None, ALU.mult), t)
                for tb in range(2):
                    t = act.do(lambda e, tb=tb: e.activation(pbuf[:, s, tb, :], pw[:, tb, :], ACT.Exp, scale=scale,
                                                             bias=st[:, c + 2 + tb:c + 3 + tb],
                                                             accum_out=st[:, c + 4 + tb:c + 5 + tb]), t)
                bf[b] = [t]
                t = dve.do(lambda e: e.reciprocal(st[:, c + 6:c + 8], st[:, c + 4:c + 6]), t)
                for tb in range(2):
                    t2 = dve.do(lambda e, tb=tb: e.tensor_scalar(pbuf[:, s, tb, :], pbuf[:, s, tb, :],
                                                                 st[:, c + 6 + tb:c + 7 + tb], None, ALU.mult), t)
                tk[h] = t2

            def two(h):
                s, b = h % 2, tbanks[h % len(tbanks)]
                pe.wait(bf[b], tk[h])
                for mb in range(2):
                    for tb in range(2):
                        o = ps[b][:, mb * T + tb * P:mb * T + tb * P + P]
                        f = lambda e, o=o, tb=tb, mb=mb: e.transpose(o, pbuf[:, h, tb, mb * P:mb * P + P], ident)
                        t = pe.do(f) if (mb, tb) == (1, 1) else pe.go(f)
                t = act.do(lambda e: e.activation(pTb[:, s, :, :], ps[b][:, :].rearrange("p (m t) -> p m t", m=2),
                                                  ACT.Copy), t, free_t.get(s))
                bf[b] = [t]
                ob = obanks[h % len(obanks)]
                lst = []
                lts = vtile(h)
                for j, lt in enumerate(lts):
                    for mb in range(2):
                        lst.append((ps[ob][:, j * T:j * T + T], lt(mb), pTb[:, s, mb, :], mb == 0, mb == 1))
                t = emit(lst, bf[ob], t, vtok)
                free_t[s] = t
                bf[ob] = [finish(h, ps[ob], t)]

            return [lambda h=h: one(h) for h in range(nh)] + [lambda h=h: two(h) for h in range(nh)]

        st_att = [None]

        xo_tok = {}

        def fin_x(h, bank, t):
            r = split_evac(bank[:, :].rearrange("p (k t) -> p k t", k=2), xh[:, 2 * h:2 * h + 2, :],
                           xl[:, 2 * h:2 * h + 2, :], t, xq_done)
            xo_tok[2 * h] = xo_tok[2 * h + 1] = r
            return r

        steps = soft_attn(4, lambda h, tb: [(xqT[:, 2 * h + j, tb * P:tb * P + P], kxT[:, 2 * h + j, :]) for j in range(2)],
                  256 ** -0.5, pbx, pTx, lambda h: [lambda mb, j=j: vx[:, mb, (2 * h + j) * P:(2 * h + j + 1) * P]
                                                    for j in range(2)],
                  fin_x, kx_tok + xq_tok, vx_tok, (2, 3), (4, 5), (6, 7))
        for step in steps[:4]:
            step()
        mt = to_T(m2, mh, ml, [m2_tok, m2_tok], banks=((0, 1), (0, 1)))
        for step in steps[4:]:
            step()
        g_post = gain(I["g_x_post"])
        g_pre = gain(I["g_ffn_pre"])
        t = mm_d("w_xo", xh, xl, xo_tok, 8)
        tk = mm_w("mkv", 0, mh, ml, mt, (2,), hold=True)
        dst_free[0] = t
        xt, mid = turn_to(xn)
        rest = rms_add(t, g_post, tmp, [], mid, pre=(g_pre, xn), early=True)
        mk_tok = act.do(lambda e: e.activation(mk2[:, :, :], ps[2][:, :].rearrange("p (k t) -> p k t", k=2), ACT.Copy), tk)
        bf[2] = [mk_tok]
        probe("x2", x[:, :, :], xt[0])
        ph.close()

        def open_ffn(n):
            s = ExitStack()
            a = lambda nm, sh, d=F32: s.enter_context(nc.sbuf_tensor(nm + n, sh, d))
            return s, a("fhb", [P, 2, 2, 512]), a("fhh", [P, NF, T], F32R), a("fhl", [P, NF, T], F32R)

        fs, hb, hh, hl = open_ffn("0")
        t = ffn("f0", xt, hb, hh, hl, rest)
        g_post = gain(I["g_ffn_post"])
        xt, mid = turn_to(x)
        rest = rms_add(t, g_post, hb[:, :, :, :].rearrange("p s b n -> p (s b n)").rearrange("p (b n) -> p b n", b=2), [],
                       mid)
        fs.close()

        def scale_x(*after):
            return pool.do(lambda e: e.tensor_scalar(x[:, :, :], x[:, :, :], ALPHA, None, ALU.mult), *after)

        def norm_of(i, j):
            return gain(I["ln_g_2"][i, j]), gain(I["ln_b_2"][i, j])

        def half_ffn(nm, i, j, rest, xt, mid_of=None, side=None):
            fs, hb, hh, hl = open_ffn(nm)
            xa = []

            def start():
                rest()
                xa.append(scale_x(xt[0], xt[1]))

            g, b = norm_of(i, j)
            t = ffn(nm, xt, hb, hh, hl, start)
            if side is not None:
                side()
            xt2, mid = turn_to(x) if mid_of is None else (None, mid_of)
            rest2 = ln_add(t, 0.5, xa, g, b, mid)
            fs.close()
            return rest2, xt2

        def mem_attn(mqT, mq_tok, dst, pbm, pTm, sbanks, tbanks, obanks):
            toks = []
            st_att[0] = mq_tok

            def fin(h, bank, t):
                o = slice(64 * (h % 2), 64 * (h % 2) + 64)
                r = act.do(lambda e: e.activation(dst[o, h // 2, :], bank[o, 0:T], ACT.Copy), t)
                toks.append(r)
                return r

            def pairs(h, tb):
                o = slice(64 * (h % 2), 64 * (h % 2) + 64)
                return [(mqT[o, h // 2, tb * P:tb * P + P], mk2[o, h // 2, :])]

            return toks, soft_attn(4, pairs, 0.125, pbm, pTm,
                                   lambda h: [lambda mb: mv2[:, mb, (h // 2) * P:(h // 2) * P + P]],
                                   fin, [mk_tok, mq_tok], mv_tok, sbanks, tbanks, obanks)

        mv_done = []

        def mv():
            mv_done.extend(mm_x("mkv", 256, mh, ml, mt, (2, 3), hold=True))

        rest, xt = half_ffn("f1", 0, 0, rest, xt, side=mv)
        mv_tok = []
        for rb in range(2):
            t = act.do(lambda e: e.activation(mv2[:, rb, :], ps[2 + rb][:, 0:T], ACT.Copy), mv_done[rb])
            bf[2 + rb] = [t]
            mv_tok.append(t)
        ms.close()

        tt = lambda o, a, b, op, *w: dve.do(lambda e: e.tensor_tensor(o, a, b, op), *w)
        ts = lambda o, a, s1, s2, o1, o2, *w: dve.do(lambda e: e.tensor_scalar(o, a, s1, s2, o1, o2), *w)
        stt = lambda o, a, s_, b, o1, o2, *w: dve.do(
            lambda e: e.scalar_tensor_tensor(out=o, in0=a, scalar=s_, in1=b, op0=o1, op1=o2), *w)
        fn = lambda o, i_, f, *w, **k: act.do(lambda e: e.activation(o, i_, f, **k), *w)
        VB = lambda name: V(name, 0, 6).unsqueeze(2).to_broadcast([P, 6, T])
        flat = lambda a: a.rearrange("p c t -> p (c t)")

        rs = ExitStack()
        ra = lambda nm, sh, d=F32: rs.enter_context(nc.sbuf_tensor("r" + nm, sh, d))
        Rr, Kk, Vv, KK, AA, BV = (ra(n, [P, 6, T]) for n in ("R", "K", "V", "KK", "AA", "BV"))
        Vtm = ra("Vtm", [P, 2, C7])
        mqT = ra("mq", [P, 2, T])
        mo = ra("mo", [P, 2, T])
        DD = ra("DD", [P, 2, T])
        gup = ra("gup", [P, C7])
        zsc = ra("zsc", [P, 6])
        i24, iT = ra("i24", [P, 24]), ra("iT", [12, T])
        s1 = ExitStack()
        rc = lambda nm, n: s1.enter_context(nc.sbuf_tensor("r" + nm, [P, n], F32))
        ga, gb2, gc = rc("ga", 1536 + 6 * (T + 1)), rc("gb2", 3072), rc("gc", 3840)
        six = lambda a: a.rearrange("p (c t) -> p c t", t=T)
        LD, w1, w2 = six(ga[:, 0:1536]), six(gb2[:, 0:1536]), six(gb2[:, 1536:3072])
        zs = ga[:, 1536:1536 + 6 * (T + 1)].rearrange("p (s k t) -> p s k t", s=3, k=2)
        wab = gc[:, 0:C7]
        pbm = gc[:, 768:2816].rearrange("p (h b t) -> p h b t", h=4, b=2)
        pTm = gc[:, 2816:3840].rearrange("p (h b t) -> p h b t", h=2, b=2)

        rest()
        xk = [xt[0], xt[1]]
        s_up = Dmas(sem("s_up"))
        s_up.start(pool, wab[0:64, :], I["rwkv_w_up_2"][0], xk)
        s_up.start(pool, wab[64:128, :], I["rwkv_a_up_2"][0])
        up_tok = s_up.start(pool, gup[:, :], I["rwkv_g_up_2"][0])
        z0_tok = pool.do(lambda e: e.memset(zs[:, :, :, 0:1], 0.0), xk)
        xa = scale_x(xk)

        tiles = {0: Rr, 1: Kk, 2: Vv, 3: DD}
        zfree, z_tok = {}, {}
        n_z = [0]

        def shift(j, b, t):
            sl = n_z[0] % 3
            n_z[0] += 1
            dst = tiles[j // 6][:, j % 6:j % 6 + 2, :]
            cur, prev = zs[:, sl, :, 1:T + 1], zs[:, sl, :, 0:T]
            t1 = fn(cur, ps[b][:, :].rearrange("p (k t) -> p k t", k=2), ACT.Copy, t, zfree.get(sl), z0_tok)
            bf[b] = [t1]
            t2 = tt(dst, prev, cur, ALU.subtract, t1)
            for k in range(2):
                t2 = stt(dst[:, k, :], dst[:, k, :], V("rwkv_mu_2", j + k), cur[:, k, :], ALU.mult, ALU.add, t2)
            zfree[sl] = z_tok[j] = t2

        K = {}
        DEC = -math.exp(-0.5)
        hf = [slice(k * T, k * T + T) for k in range(2)]
        pair = lambda b: ps[b][:, :].rearrange("p (k t) -> p k t", k=2)

        def f_small():
            K["td"] = fn(DD[0:64, 0, :], DD[0:64, 0, :], ACT.Tanh, z_tok[18])
            K["dg"] = fn(DD[:, 1, :], DD[:, 1, :], ACT.Sigmoid, z_tok[18])

        def f_w(q):
            b = 4 + q % 2
            t = emit([(ps[b][:, hf[k]], wab[0:64, (2 * q + k) * P:(2 * q + k + 1) * P], DD[0:64, 0, :], True, True)
                      for k in range(2)], bf[b], K["td"], up_tok)
            for k in range(2):
                c = 2 * q + k
                t2 = fn(LD[:, c, :], ps[b][:, hf[k]], ACT.Sigmoid, t, bias=V("rwkv_w0_2", c))
                bf[b] = [t2]
                for n in range(2):
                    u = slice(n * P, n * P + P)
                    K["scan"] = dve.do(lambda e: e.tensor_tensor_scan(w1[:, c, u], C(K_ONE, P), LD[:, c, u], 0.0,
                                                                      ALU.mult, ALU.add), t2)

        def f_a(q):
            b = 6 + q % 2
            t = emit([(ps[b][:, hf[k]], wab[64:128, (2 * q + k) * P:(2 * q + k + 1) * P], DD[64:128, 0, :], True, True)
                      for k in range(2)], bf[b], z_tok[18], up_tok)
            for k in range(2):
                K["a"] = fn(AA[:, 2 * q + k, :], ps[b][:, hf[k]], ACT.Sigmoid, t, bias=V("rwkv_a0_2", 2 * q + k))
            bf[b] = [K["a"]]

        def f_ka():
            K["ka"] = stt(BV[:, :, :], AA[:, :, :], -1.0, VB("rwkv_k_a_2"), ALU.add, ALU.mult, K["a"], K["n2"])

        def f_mid():
            L4 = w1.rearrange("p c (n t) -> p c n t", t=P)
            t = tt(zsc[:, :], L4[:, :, 0, P - 1], L4[:, :, 0, 63], ALU.subtract, K["scan"])
            K["zsc"] = tt(zsc[:, :], zsc[:, :], L4[:, :, 1, 63], ALU.add, t)
            f3 = lambda a: flat(a).rearrange("p (n t) -> p n t", t=P)
            K["lr"] = tt(f3(w2), f3(w1), f3(w1)[:, :, 63:64].to_broadcast([P, 12, P]), ALU.subtract, K["scan"])

        def f_lp():
            K["lp"] = tt(LD, w2, LD, ALU.subtract, K["lr"])

        def f_exp1():
            K["e3"] = fn(w1, w2, ACT.Exp, K["lr"], scale=-DEC)

        def f_exp2():
            K["e2"] = fn(LD, LD, ACT.Exp, K["lp"], scale=DEC)

        def f_exp3():
            K["e1"] = fn(w2, w2, ACT.Exp, K["lp"], K["e3"], scale=DEC)
            K["zs"] = fn(zsc[:, :], zsc[:, :], ACT.Exp, K["zsc"], scale=DEC)

        def f_kk():
            K["kk"] = pool.do(lambda e: e.tensor_tensor(KK[:, :, :], Kk[:, :, :], VB("rwkv_k_k_2"), ALU.mult), z_tok[10])

        def f_sq():
            K["sq"] = fn(BV[:, :, :], KK[:, :, :], ACT.Square, K["kk"])

        def f_norm():
            t = emit([(ps[4][:, 12 * tb + 2 * c:12 * tb + 2 * c + 2], BV[:, c, tb * P:tb * P + P], C(K_SEL2, 2), True, True)
                      for tb in range(2) for c in range(6)], bf[4], K["sq"])
            K["n2"] = t
            t = ts(i24[:, :], ps[4][:, 0:24], 1e-24, None, ALU.max, ALU.bypass, t)
            bf[4] = [t]
            t = dve.do(lambda e: e.reciprocal(i24[:, :], i24[:, :]), t)
            K["i24"] = fn(i24[:, :], i24[:, :], ACT.Sqrt, t)

        def f_normT():
            pe.wait(bf[5], K["i24"])
            for tb in range(2):
                t = pe.do(lambda e: e.transpose(ps[5][0:12, tb * P:tb * P + P], i24[:, 12 * tb:12 * tb + 12], ident))
            K["iT"] = fn(iT[:, :], ps[5][0:12, 0:T], ACT.Copy, t)
            bf[5] = [K["iT"]]

        def f_unit(q):
            b = (4, 6, 7)[q]
            t = emit([(ps[b][:, hf[k]], C(K_SELH + (2 * q + k) * P, P, 12), iT[:, :], True, True)
                      for k in range(2)], bf[b], K["iT"])
            two_ = slice(2 * q, 2 * q + 2)
            K["u"] = tt(KK[:, two_, :], KK[:, two_, :], pair(b), ALU.mult, t)
            bf[b] = [K["u"]]

        def f_nb():
            K["k1"] = stt(Kk[:, :, :], BV[:, :, :], 1.0, Kk[:, :, :], ALU.add, ALU.mult, K["ka"], K["kk"])
            K["nb"] = stt(AA[:, :, :], KK[:, :, :], -1.0, AA[:, :, :], ALU.mult, ALU.mult, K["u"], K["ka"])

        def f_hats():
            K["kp"] = tt(KK[:, :, :], KK[:, :, :], LD, ALU.mult, K["e2"], K["nb"])
            K["b"] = tt(AA[:, :, :], AA[:, :, :], w1, ALU.mult, K["e3"], K["nb"])

        steps1 = [f_small, lambda: f_w(0), lambda: f_w(1), lambda: f_w(2), lambda: f_a(0), lambda: f_a(1), lambda: f_a(2),
                  f_mid, f_lp, f_exp1, f_exp2]
        steps2 = [f_kk, lambda: None, f_exp3, f_sq, f_norm, lambda: (f_ka(), f_normT()), lambda: f_unit(0),
                  lambda: f_unit(1), lambda: f_unit(2), f_nb, f_hats]
        side = []
        for c, (n0, w) in enumerate(RW):
            banks = ((0, 1), (2, 3))[c % 2]
            t = mm_w("rw", n0, xh, xl, xt, banks, side=side)
            if n0 == 2560:
                mq_tok = fn(mqT[:, :, :], pair(banks[0]), ACT.Copy, t)
                bf[banks[0]] = [mq_tok]
            else:
                for q in range(w // T):
                    shift(n0 // P + 2 * q, banks[q], t)
            if n0 == 2304:
                side += steps1
            if n0 == 1280:
                side += steps2
        in_done = t

        def turned(src, tb, dst, banks, after):
            def part(q):
                b, n = banks[q], (4, 2)[q]
                pe.wait(bf[b], after, K.get("kh"), K.get("b"))
                for k in range(n):
                    f = lambda e: e.transpose(ps[b][:, k * P:k * P + P], src[:, 4 * q + k, tb * P:tb * P + P], ident)
                    t = pe.do(f) if k == n - 1 else pe.go(f)
                t = fn(dst[:, 512 * q:512 * q + n * P], ps[b][:, 0:n * P], ACT.Copy, t)
                bf[b] = [t]
                return t
            return part

        mo_tok, steps = mem_attn(mqT, mq_tok, mo, pbm, pTm, (0, 1, 2, 3), (0, 1), (2, 3))
        for step in steps[:4]:
            step()
        while side:
            side.pop(0)()
        for step in steps[4:]:
            step()

        XI = ga[:, 0:3072].rearrange("p (m t) -> p m t", t=P)
        XIg = lambda g: XI[:, 4 * g:4 * g + 4, :]
        APg = lambda g: xf[:, g // 4, 512 * (g % 4):512 * (g % 4) + 512].rearrange("p (m t) -> p m t", t=P)
        TI = [gc[:, 768 * k:768 * k + 512].rearrange("p (m t) -> p m t", t=P) for k in range(3)]
        Qm = [gc[:, 768 * k + 512:768 * k + 768].rearrange("p (m t) -> p m t", t=64) for k in range(3)]
        MR = gc[:, 2304:3840].rearrange("p (m t) -> p m t", t=P)
        BM = gb2[:, :].rearrange("p (m t) -> p m t", t=2 * P)
        M_ = lambda k, n=P: C(k, n).bitcast(I32)
        H = lambda h, ck: (slice(64 * (h % 2), 64 * (h % 2) + 64), h // 2, slice(ck * P, ck * P + P))
        cp = lambda o, m, d, *w: dve.do(lambda e: e.copy_predicated(o, m, d), *w)
        feats = [K["kp"], K["b"]]
        gram = {}

        def gram_a(g):
            ck, h0 = g // 3, 4 * (g % 3)
            xi = fn(XIg(g), ident.unsqueeze(1).to_broadcast([P, 4, P]), ACT.Copy, feats, z_tok[16], in_done)
            for par in range(2):
                b = 4 + 2 * (g % 2) + par
                lst = []
                for k in range(2):
                    h = h0 + 2 * k + par
                    lst.append((ps[b][:, k * P:k * P + P], KK[H(h, ck)], AA[H(h, ck)], True, True))
                    lst.append((ps[b][:, T + k * P:T + k * P + P], AA[H(h, ck)], KK[H(h, ck)], True, True))
                t = emit(lst, bf[b], feats)
                pv = ps[b][:, :].rearrange("p (a k t) -> p a k t", a=2, k=2)
                tt(APg(g)[:, par::2, :], pv[:, 0, :, :], C(K_SL, P).unsqueeze(1).to_broadcast([P, 2, P]), ALU.mult, t, in_done)
                gram[g] = cp(XIg(g)[:, par::2, :], M_(K_M1).unsqueeze(1).to_broadcast([P, 2, P]), pv[:, 1, :, :], xi)
                bf[b] = [gram[g]]

        cut_ = lambda a, bl, w: a.rearrange("p (n two b) -> p n two b", two=2, b=bl)[:, :, w, :]
        xi_tok, ti_tok, qm_tok, slot = {}, {}, {}, {}

        def inv_a(i):
            lv, g = divmod(i, 6)
            bl, k3, bT, bQ = 2 << lv, i % 3, i % 2, 2 + i % 2
            pe.wait(bf[bT], xi_tok.get(g, gram[g]))
            for k in range(4):
                f = lambda e: e.transpose(ps[bT][:, k * P:k * P + P], XI[:, 4 * g + k, :], ident)
                t = pe.do(f) if k == 3 else pe.go(f)
            ti_tok[i] = fn(TI[k3], ps[bT][:, :].rearrange("p (k t) -> p k t", k=4), ACT.Copy, t, slot.get(k3))
            bf[bT] = [ti_tok[i]]
            t = emit([(ps[bQ][:, 64 * k:64 * k + 64], APg(g)[:, k, :], cut_(XI[:, 4 * g + k, :], bl, 1), True, True)
                      for k in range(4)], bf[bQ])
            qm_tok[i] = tt(Qm[k3], ps[bQ][:, 0:256].rearrange("p (k t) -> p k t", k=4),
                           C(K_LV + 64 * lv, 64).unsqueeze(1).to_broadcast([P, 4, 64]), ALU.mult, t, slot.get(k3))
            bf[bQ] = [qm_tok[i]]

        def inv_b(i):
            lv, g = divmod(i, 6)
            bl, k3, b = 2 << lv, i % 3, 4 + i % 2
            t = emit([(ps[b][:, 64 * k:64 * k + 64], TI[k3][:, k, :], Qm[k3][:, k, :], True, True) for k in range(4)],
                     bf[b], ti_tok[i], qm_tok[i])
            slot[k3] = t
            xo = cut_(XIg(g).rearrange("p m t -> p (m t)"), bl, 1)
            xi_tok[g] = tt(xo, xo, ps[b][:, 0:256].rearrange("p (n b) -> p n b", b=bl), ALU.add, t)
            bf[b] = [xi_tok[g]]

        khT, nbT, Xs = gb[:, 0, 0:C7], gb[:, 1, 0:C7], junk[:, 0:C7]
        gb_free = [gfree[0], gfree[1]]
        par_of = lambda a, par: a.rearrange("p (c two d) -> p c two d", two=2, d=64)[:, :, par, :]
        hcol = lambda h: slice(64 * (h // 2), 64 * (h // 2) + 64)
        half = lambda b: ps[b][:, 0:384].rearrange("p (c d) -> p c d", d=64)

        def g_bonus():
            t = pool.do(lambda e: e.tensor_tensor(BV[:, :, :], Rr[:, :, :], VB("rwkv_r_k_2"), ALU.mult), K["k1"], z_tok[4])
            K["bo"] = pool.do(lambda e: e.tensor_tensor(BV[:, :, :], BV[:, :, :], Kk[:, :, :], ALU.mult), t)

        def g_hats():
            K["r"] = tt(Rr[:, :, :], Rr[:, :, :], w2, ALU.mult, K["e1"], K["bo"])
            K["kh"] = tt(Kk[:, :, :], Kk[:, :, :], w1, ALU.mult, K["bo"])
            free = [K["r"], K["kh"], K["b"], mo_tok]
            pool.do(lambda e: e.memset(BM[:, :, :], 0.0), free)
            K["zero"] = pool.do(lambda e: e.memset(MR[:, :, :], 0.0), free)

        def g_bv(q):
            b = 6 + q % 2
            two_ = slice(2 * q, 2 * q + 2)
            t = emit([(ps[b][:, :], C(K_BO, P), BV[:, two_, :], True, True)], bf[b], K["bo"])
            t = tt(BV[:, two_, :], Vv[:, two_, :], pair(b), ALU.mult, t, z_tok[16])
            bf[b] = [t]
            for k in range(2):
                c = 2 * q + k
                K["bv"] = pool.do(lambda e: e.tensor_scalar(BV[:, c, :], BV[:, c, :], V("rwkv_lnx_b_2", c), None, ALU.add), t)

        def keep(name, f, *a):
            K.setdefault(name, []).append(f(*a))

        v_t = [turned(Vv, tb, Vtm[:, tb, :], (6, 7), z_tok[16]) for tb in range(2)]
        k_t = [turned(Kk, 0, khT, (6, 7), gb_free), turned(AA, 0, nbT, (6, 7), gb_free)]
        o_done = [None]

        def gram_b(ck, g, par):
            hs = (4 * g + par, 4 * g + 2 + par)
            la = [(ps[6][:, (2 * k + j) * P:(2 * k + j + 1) * P], Kk[H(h, ck)], r[H(h, ck)], True, True)
                  for k, h in enumerate(hs) for j, r in enumerate((KK, Rr))]
            lb = [(ps[7][:, k * P:k * P + P], AA[H(h, ck)], Rr[H(h, ck)], True, True) for k, h in enumerate(hs)]
            ta = emit(la, bf[6], K["r"], K["kh"])
            tb_ = emit(lb, bf[7])
            of = lambda a: a[:, hs[0]:hs[1] + 1:2, :]
            t = cp(of(BM), M_(K_SU, 2 * P).unsqueeze(1).to_broadcast([P, 2, 2 * P]),
                   ps[6][:, :].rearrange("p (k t) -> p k t", k=2), ta, K["zero"], o_done[0])
            bf[6] = [t]
            t = cp(of(MR), M_(K_IU).unsqueeze(1).to_broadcast([P, 2, P]),
                   ps[7][:, 0:T].rearrange("p (k t) -> p k t", k=2), tb_)
            bf[7] = [t]
            K["bm"] = t

        def x_start(par):
            b = 6 + par
            t = emit([(ps[b][:, hcol(h)], BM[:, h, 0:P], Vtm[:, 0, 64 * h:64 * h + 64], True, True)
                      for h in range(par, 12, 2)], bf[b], K["v"], K["bm"])
            t = fn(par_of(Xs, par), half(b), ACT.Copy, t, junk_by[0])
            bf[b] = [t]
            keep("x", lambda: t)

        fill = [g_bonus, lambda: keep("v", v_t[0], 0), lambda: keep("v", v_t[0], 1), lambda: keep("v", v_t[1], 0),
                lambda: keep("v", v_t[1], 1), lambda: keep("nb_t", k_t[1], 0), lambda: keep("nb_t", k_t[1], 1), g_hats]
        fill += [lambda q=q: g_bv(q) for q in range(3)]
        fill += [lambda: keep("kh_t", k_t[0], 0), lambda: keep("kh_t", k_t[0], 1)]
        fill += [lambda g=g, par=par: gram_b(0, g, par) for g in range(3) for par in range(2)]
        fill += [lambda par=par: x_start(par) for par in range(2)]

        gram_a(0)
        gram_a(1)
        NI = 36
        for i in range(NI + 2):
            if i < NI:
                inv_a(i)
            if i < 4:
                gram_a(i + 2)
            if i >= 2:
                inv_b(i - 2)
            if i >= 5 and fill:
                fill.pop(0)()
        for f in fill:
            f()
        inv = list(xi_tok.values())

        Z0 = mqT[:, :, :].rearrange("p c t -> p (c t)")[:, 0:384].rearrange("p (c d) -> p c d", d=64)
        Us, sqs = xf[:, 0, 0:C7], xf[:, 1, 0:C7]
        oc = Vv[:, :, :].rearrange("p c t -> p (c t)").rearrange("p (b n) -> p b n", b=2)
        y_tok, x_t = [], K["x"]
        z_ok = u_old = None
        for ck in range(2):
            if ck:
                for g in range(3):
                    for par in range(2):
                        gram_b(1, g, par)
                x_t = []
                for par, b in ((0, 0), (1, 1)):
                    lst = []
                    for h in range(par, 12, 2):
                        lst.append((ps[b][:, hcol(h)], BM[:, h, 0:P], Vtm[:, 1, 64 * h:64 * h + 64], True, False))
                        lst.append((ps[b][:, hcol(h)], KK[H(h, 1)], Z0[H(h, 1)[0], h // 2, :], False, True))
                    t = emit(lst, bf[b], K["bm"], z_ok)
                    t = fn(par_of(Xs, par), half(b), ACT.Copy, t, u_old)
                    bf[b] = [t]
                    x_t.append(t)
            u_t = []
            for par, b in ((0, 2), (1, 3)):
                t = emit([(ps[b][:, hcol(h)], XI[:, 12 * ck + h, :], Xs[:, 64 * h:64 * h + 64], True, True)
                          for h in range(par, 12, 2)], bf[b], x_t[par], inv)
                u_old = t
                t = fn(par_of(Us, par), half(b), ACT.Copy, t, o_done[0])
                bf[b] = [t]
                u_t.append(t)
            if ck == 0:
                for q, (b, n) in enumerate(((4, 4), (5, 2))):
                    lst = []
                    for k in range(n):
                        s_ = slice((4 * q + k) * P, (4 * q + k + 1) * P)
                        lst += [(ps[b][:, k * P:k * P + P], khT[:, s_], Vtm[:, 0, s_], True, False),
                                (ps[b][:, k * P:k * P + P], nbT[:, s_], Us[:, s_], False, True)]
                    t = emit(lst, bf[b], K["kh_t"], K["nb_t"], u_t)
                    for o in range(2):
                        pr = slice(64 * o, 64 * o + 64)
                        z_ok = tt(Z0[pr, 4 * q:4 * q + n, :],
                                  ps[b][pr, 0:n * P].rearrange("p (k t) -> p k t", k=n)[:, :, 64 * o:64 * o + 64],
                                  zsc[pr, 4 * q:4 * q + n].unsqueeze(2).to_broadcast([64, n, 64]), ALU.mult, t, K["zs"], mo_tok)
                    bf[b] = [z_ok]
                gfree[0] = gfree[1] = t
            for par, b in ((0, 0), (1, 1)):
                lst = []
                for h in range(par, 12, 2):
                    v_ = Vtm[:, ck, 64 * h:64 * h + 64]
                    lst.append((ps[b][:, hcol(h)], BM[:, h, P:2 * P], v_, True, False))
                    if ck:
                        lst.append((ps[b][:, hcol(h)], Rr[H(h, 1)], Z0[H(h, 1)[0], h // 2, :], False, False))
                    lst.append((ps[b][:, hcol(h)], MR[:, h, :], Us[:, 64 * h:64 * h + 64], False, True))
                t = emit(lst, bf[b], u_t)
                o_done[0] = t
                o3, oc3 = half(b), par_of(oc[:, ck, :], par)
                sm, vr, rr = (st[:, 144 + 12 * k + 6 * par:150 + 12 * k + 6 * par] for k in range(3))
                bc = lambda a: a.unsqueeze(2).to_broadcast([P, 6, 64])
                sq = sqs[:, 384 * par:384 * par + 384]
                t = dve.do(lambda e: e.tensor_reduce(sm, o3, AX.X, ALU.add), t, K["bv"], K["v"])
                t = ts(sm, sm, 1.0 / 64, None, ALU.mult, ALU.bypass, t)
                t = tt(oc3, o3, bc(sm), ALU.subtract, t)
                bf[b] = [t]
                t = fn(sq.rearrange("p (c d) -> p c d", d=64), oc3, ACT.Square, t)
                t = dve.do(lambda e: e.tensor_reduce(vr, sq.rearrange("p (h d) -> p h d", d=64), AX.X, ALU.add), t)
                t = rstd_of(vr, rr, t, LNX_EPS, 1.0 / 64)
                y_tok.append(tt(oc3, oc3, bc(rr), ALU.mult, t))
        probe("oc", oc, y_tok)
        g0b0 = norm_of(0, 1)
        s1.close()

        yh, yl = ra("yh", [P, 8, T], F32R), ra("yl", [P, 8, T], F32R)
        yT = {}
        yT[6] = yT[7] = split_evac(mo[:, :, :], yh[:, 6:8, :], yl[:, 6:8, :], mo_tok, o_done[0])
        g_t = {}
        for q in range(3):
            b = 5 + q
            g_t[q] = emit([(ps[b][:, hf[k]], gup[:, (2 * q + k) * P:(2 * q + k + 1) * P], DD[:, 1, :], True, True)
                           for k in range(2)], bf[b], K["dg"], up_tok)
        for q in range(3):
            b = 2 + q
            pe.wait(bf[b], y_tok)
            for k in range(2):
                for ck in range(2):
                    f = lambda e: e.transpose(ps[b][:, k * T + ck * P:k * T + ck * P + P],
                                              oc[:, ck, (2 * q + k) * P:(2 * q + k + 1) * P], ident)
                    t = pe.do(f) if (k, ck) == (1, 1) else pe.go(f)
            two_ = slice(2 * q, 2 * q + 2)
            d = [stt(Kk[:, 2 * q + k, :], ps[b][:, hf[k]], V("rwkv_lnx_g_2", 2 * q + k), BV[:, 2 * q + k, :], ALU.mult, ALU.add, t)
                 for k in range(2)]
            bf[b] = d
            t = tt(Kk[:, two_, :], Kk[:, two_, :], pair(5 + q), ALU.mult, d, g_t[q])
            bf[5 + q] = [t]
            yT[2 * q] = yT[2 * q + 1] = split_evac(Kk[:, two_, :], yh[:, two_, :], yl[:, two_, :], t)
        probe("headsT", yh[:, :, :].bitcast(F32), yT[6], yT[5])
        t = mm_d("wo0", yh, yl, yT, 8)
        xt, mid = turn_to(x)
        rest = ln_add(t, 1.0, xa, *g0b0, mid)
        rs.close()

        rest, xt = half_ffn("f2", 0, 2, rest, xt)
        rest, xt = half_ffn("f3", 1, 0, rest, xt)

        rs = ExitStack()
        ra = lambda nm, sh, d=F32: rs.enter_context(nc.sbuf_tensor("b" + nm, sh, d))
        yh, yl = ra("yh", [P, 8, T], F32R), ra("yl", [P, 8, T], F32R)
        qT, kT = ra("qT", [P, 6, T]), ra("kT", [P, 6, T])
        mqT, mo = ra("mq", [P, 2, T]), ra("mo", [P, 2, T])
        vt = ra("vt", [P, 2, C7])
        m3, m3n = ra("m3", [P, 384]), ra("m3n", [P, 384])
        NS = 8
        sa, sw = (ra(n, [P, NS, 384]) for n in ("sa", "sw"))
        pbm, pTm = ra("pbm", [P, 4, 2, T]), ra("pTm", [P, 2, 2, T])
        xa = []

        def start():
            rest()
            xa.append(scale_x(xt[0], xt[1]))

        xk = xt[0]
        gb_ = norm_of(1, 1)
        m_tok = [pool.do(lambda e, o=o, k=k: e.tensor_copy(m3[:, o:o + P], C(k, P)), xk)
                 for o, k in ((0, K_SU), (P, K_ONE), (2 * P, K_SU))]
        m_tok = [pool.do(lambda e: e.tensor_scalar(m3n[:, :], m3[:, :], -1.0, None, ALU.mult), m_tok)]
        q_tok, k_tok, v_tok3, mq_tok = [], [], [], []

        free_s = {}
        att_tok, w_tok2, lk_tok = {}, {}, {}

        def sb_scores(h):
            s, b = h % NS, 4 + h % 2
            o, c = slice(64 * (h % 2), 64 * (h % 2) + 64), h // 2
            z = ps[b][:, 0:384]
            t = emit([(ps[b][:, 0:T], kT[o, c, 0:P], qT[o, c, :], True, True),
                      (ps[b][:, T:384], kT[o, c, P:T], qT[o, c, P:T], True, True)], bf[b], q_tok, k_tok)
            t = fn(sa[:, s, :], z, ACT.Abs, t, free_s.get(s))
            t = fn(sa[:, s, :], sa[:, s, :], ACT.Exp, t, scale=-1.0)
            t = fn(sa[:, s, :], sa[:, s, :], ACT.Ln, t, bias=1.0)
            t = stt(sa[:, s, :], z, 0.0, sa[:, s, :], ALU.max, ALU.add, t)
            w_tok2[h] = tt(sw[:, s, :], z, sa[:, s, :], ALU.subtract, t, free_s.get(s))
            bf[b] = [w_tok2[h]]
            lk_tok[h] = pool.do(lambda e: e.tensor_tensor(sa[:, s, :], sa[:, s, :], m3n[:, :], ALU.mult), w_tok2[h], m_tok)

        def sb_later(h):
            s, b = h % NS, 6 + h % 2
            tri, one = C(K_SL, P), C(K_ONE, P)
            t = emit([(ps[b][:, 0:T], tri, sa[:, s, 0:T], True, False),
                      (ps[b][:, P:T], one, sa[:, s, T:384], False, True),
                      (ps[b][:, T:384], tri, sa[:, s, T:384], True, True)], bf[b], lk_tok[h])
            t = tt(sw[:, s, :], sw[:, s, :], ps[b][:, 0:384], ALU.add, t, w_tok2[h])
            bf[b] = [t]
            t = fn(sw[:, s, :], sw[:, s, :], ACT.Exp, t)
            att_tok[h] = pool.do(lambda e: e.tensor_tensor(sw[:, s, :], sw[:, s, :], m3[:, :], ALU.mult), t)

        yT = {}

        def sb_out(c):
            b = 2 + c % 2
            lst = []
            for k in range(2):
                s = (2 * c + k) % NS
                lst += [(ps[b][:, k * T:k * T + T], vt[:, 0, c * P:c * P + P], sw[:, s, 0:T], True, False),
                        (ps[b][:, k * T + P:k * T + T], vt[:, 1, c * P:c * P + P], sw[:, s, T:384], False, True)]
            t = emit(lst, bf[b], att_tok[2 * c], att_tok[2 * c + 1], v_tok3)
            for k in range(2):
                free_s[(2 * c + k) % NS] = t
            for k in range(2):
                o = slice(64 * k, 64 * k + 64)
                yT[c] = split_evac(ps[b][o, k * T:k * T + T], yh[o, c, :], yl[o, c, :], t)
            bf[b] = [yT[c]]

        def v_chunk(c, n0, w, banks, **how):
            t = mm_x("sb", n0, xh, xl, xt, banks, **how)
            for rb in range(2):
                b = banks[rb]
                t2 = fn(vt[:, rb, 512 * c:512 * c + w], ps[b][:, 0:w], ACT.Copy, t[rb])
                bf[b] = [t2]
                v_tok3.append(t2)

        v_chunk(0, 1536, 512, (0, 1), lead=3, mid=start)
        for c in range(3):
            banks = (0, 1) if c % 2 == 1 else (2, 3)
            t = mm_w("sb", 512 * c, xh, xl, xt, banks)
            for q in range(2):
                b, j = banks[q], 4 * c + 2 * q
                src = ps[b][:, :].rearrange("p (k t) -> p k t", k=2)
                if j < 6:
                    t2 = fn(qT[:, j:j + 2, :], src, ACT.Copy, t, scale=0.125)
                    q_tok.append(t2)
                else:
                    t2 = fn(kT[:, j - 6:j - 4, :], src, ACT.Copy, t)
                    k_tok.append(t2)
                bf[b] = [t2]
        act.go(lambda e: e.preload_act_table_set("natural_log_exp_and_others"))
        side = [lambda: None] + [lambda h=h: sb_scores(h) for h in range(8)]
        t = mm_w("sb", 2304, xh, xl, xt, (0,), side=side)
        mq_tok.append(fn(mqT[:, :, :], ps[0][:, :].rearrange("p (k t) -> p k t", k=2), ACT.Copy, t))
        bf[0] = mq_tok[:]
        v_chunk(1, 2048, 256, (2, 3), side=side)
        for step in side:
            step()
        mo_tok, steps = mem_attn(mqT, mq_tok, mo, pbm, pTm, (0, 1), (0, 1), (0, 1))
        for h in range(12):
            sb_later(h)
            if h >= 3 and h % 2 == 1:
                sb_out((h - 3) // 2)
                for k in (h + 5, h + 6):
                    if k < 12:
                        sb_scores(k)
            if h >= 1 and steps:
                steps.pop(0)()
        for step in steps:
            step()
        sb_out(5)
        yT[6] = yT[7] = split_evac(mo[:, :, :], yh[:, 6:8, :], yl[:, 6:8, :], mo_tok)
        probe("headsT1", yh[:, :, :].bitcast(F32), yT[6], yT[5])
        t = mm_d("wo1", yh, yl, yT, 8)
        xt, mid = turn_to(x)
        rest = ln_add(t, 1.0, xa, *gb_, mid)
        rs.close()

        s_out = Dmas(sem("s_out"))
        gone = []

        def store(rb, toks, between=None):
            if between is not None:
                between()
            gone.append(s_out.start(sp, out[0, rb * P:rb * P + P, :], x[:, rb, :], toks))

        rest, _ = half_ffn("f4", 1, 2, rest, xt, store)
        rest()
        sp.wait(gone)
        assert used[0] == NU, (used[0], NU)


def constants():
    c = np.zeros((P, NCST), np.float32)
    i, j = np.arange(P)[:, None], np.arange(P)[None, :]
    c[:, K_ID:K_ID + P] = i == j
    c[:, K_AM:K_AM + P] = c[:, K_AM + 2 * P:K_AM + 3 * P] = np.where(j > i, np.float32(NEG), np.float32(0))
    c[:, K_SU:K_SU + P] = i < j
    c[:, K_IU:K_IU + P] = i <= j
    c[:, K_M1:K_M1 + P] = (j == i + 1) & (i % 2 == 0)
    c[:, K_SL:K_SL + P] = i > j
    for lv in range(6):
        b = 2 << lv
        odd = (np.arange(64) // b) * 2 * b + b + np.arange(64) % b
        row = np.arange(P)[:, None]
        c[:, K_LV + 64 * lv:K_LV + 64 * lv + 64] = (row // (2 * b) == odd[None, :] // (2 * b)) & (row // b % 2 == 0)
    c[:, K_ONE:K_ONE + P] = 1
    c[:, K_SEL2:K_SEL2 + 2] = i // 64 == np.arange(2)[None, :]
    c[:, K_FREQ:K_FREQ + 8] = np.float32(500000.0) ** (-np.arange(0, 16, 2, dtype=np.float32) / np.float32(16))
    c[:, K_BO:K_BO + P] = i // 64 == j // 64
    f = np.arange(C7)[None, :]
    c[0:12, K_SELH:K_SELH + C7] = np.arange(12)[:, None] == f // 64
    s = np.arange(T)[:, None, None]
    w = np.array([2, 4, 8, 16])[None, :, None]
    t = np.arange(T)[None, None, :]
    band = np.where((s <= t) & (s > t - w), np.float32(1) / np.minimum(t + 1, w).astype(np.float32), np.float32(0))
    band = (band - (s == t)).astype(np.float32)
    band = band.reshape(2, P, 4, T).transpose(1, 0, 2, 3).reshape(P, 8 * T)
    return c, np.ascontiguousarray(band)


NAMES = [
    "x", "mem", "positions", "g_mix_pre", "w_in", "lambda_q1", "lambda_k1", "lambda_q2", "lambda_k2", "g_subln",
    "w_pool", "pool_scale", "w_out", "g_mix_post", "g_x_pre", "g_mem", "w_xq", "w_xkv", "w_xo", "g_x_post",
    "g_ffn_pre", "w_gate", "w_up", "w_down", "g_ffn_post", "mem_2", "ffn1_w_gate_2", "ffn1_w_up_2",
    "ffn1_w_down_2", "ffn2_w_gate_2", "ffn2_w_up_2", "ffn2_w_down_2", "ln_g_2", "ln_b_2", "w_out_2",
    "w_mem_kv_2", "rwkv_w_in_2", "rwkv_mu_2", "rwkv_w0_2", "rwkv_w_up_2", "rwkv_a0_2", "rwkv_a_up_2",
    "rwkv_g_up_2", "rwkv_k_k_2", "rwkv_k_a_2", "rwkv_r_k_2", "rwkv_lnx_g_2", "rwkv_lnx_b_2", "sb_w_in_2",
]


def kernel(**inputs):
    import concourse.bacc as bacc
    from concourse.bass_utils import run_bass_kernel_spmd

    nc = bacc.Bacc("TRN2", target_bir_lowering=False, num_devices=1)
    arrays, args = {}, {}
    for name in NAMES:
        a = np.ascontiguousarray(inputs[name])
        arrays["in_" + name] = a
        args[name] = nc.dram_tensor("in_" + name, a.shape, mybir.dt.from_np(a.dtype), kind="ExternalInput").ap()
    consts = []
    for name, a in zip(("c_tables", "c_band"), constants()):
        arrays[name] = a
        consts.append(nc.dram_tensor(name, a.shape, F32, kind="ExternalInput").ap())
    out = nc.dram_tensor("out_x", (1, T, D), F32, kind="ExternalOutput").ap()
    build_program(nc, args, consts[0], consts[1], out)
    r = run_bass_kernel_spmd(nc, [arrays], core_ids=[0])
    return r.results[0]["out_x"]
```

```python
import math
from contextlib import ExitStack

import numpy as np
import concourse.bass as bass
from concourse import mybir

F32 = mybir.dt.float32
F32R = mybir.dt.float32r
I32 = mybir.dt.int32
ALU = mybir.AluOpType
ACT = mybir.ActivationFunctionType
AX = mybir.AxisListType

P = 128
T = 256
D = 1024
FF = 2816
NF = FF // P
LAM0 = 0.8 - 0.6 * math.exp(0.0)
EPS = 1e-6
LN_EPS = 1e-5
LNX_EPS = 64e-5
ALPHA = 4.0 ** 0.25
C7 = 768
HC = C7 // P
NEG = -3.0e38

NR, NH = 4, 6
TAIL = 3
UW = 1024

K_ID, K_AM, K_SU, K_IU, K_M1, K_SL, K_LV = 0, 128, 512, 640, 768, 896, 1024
K_ONE, K_SEL2, K_FREQ, K_BO, K_SELH = 1408, 1536, 1538, 1546, 1674
NCST = K_SELH + C7

RW = [(2304, 256), (768, 512), (1280, 256), (0, 512), (512, 256), (1536, 512), (2048, 256), (2560, 256)]

LATE = [6, 7, 0, 1, 2, 3, 4, 5]
SB = [(1536, 512)] + [(n, 256) for n in (0, 768, 2304, 256, 1024, 512, 1280, 2048)]
POOLED = [4, 5, 6, 7, 0, 1, 2, 3]

VROWS = [("pool_scale", 4), ("g_subln", 1), ("rwkv_mu_2", 20), ("rwkv_w0_2", 6), ("rwkv_a0_2", 6),
         ("rwkv_k_k_2", 6), ("rwkv_k_a_2", 6), ("rwkv_r_k_2", 6), ("rwkv_lnx_g_2", 6), ("rwkv_lnx_b_2", 6)]
NV = sum(n for _, n in VROWS)


class Lane:

    def __init__(self, engine, sem):
        self.e, self.sem, self.n, self.seen = engine, sem, 0, {}

    def wait(self, *tokens):
        for t in tokens:
            if isinstance(t, list):
                self.wait(*t)
            elif t is not None and self.seen.get(t[0].name, 0) < t[1]:
                self.seen[t[0].name] = t[1]
                self.e.wait_ge(t[0], t[1])

    def go(self, fn, *after):
        self.wait(*after)
        fn(self.e)

    def do(self, fn, *after):
        self.wait(*after)
        self.n += 1
        fn(self.e).then_inc(self.sem, 1)
        return (self.sem, self.n)


class Dmas:

    def __init__(self, sem):
        self.sem, self.n = sem, 0

    def start(self, lane, out, in_, *after, **how):
        lane.wait(*after)
        self.n += 16
        lane.e.dma_start(out, in_, **how).then_inc(self.sem, 16)
        return (self.sem, self.n)


def cols(w, k0, nk, n0, n):
    return w[k0 * P:(k0 + nk) * P, n0:n0 + n].rearrange("(k p) n -> p k n", p=P)


def chunk(name, w, n0, n, nk=8):
    per = UW // n
    return [((name, n0), cols(w, k, per, n0, n), per, n) for k in range(0, nk, per)]


def build_program(nc, I, cst_in, band_in, out, dbg=None):
    es = ExitStack()
    with es:
        sem = lambda n: es.enter_context(nc.semaphore(n))
        sb = lambda n, s, d=F32: es.enter_context(nc.sbuf_tensor(n, s, d))
        pe, act, dve, pool, sp = (
            Lane(e, sem("s_" + n)) for e, n in ((nc.tensor, "pe"), (nc.scalar, "act"), (nc.vector, "dve"),
                                                (nc.gpsimd, "pool"), (nc.sync, "sp")))
        s_raw = [sem(f"s_raw{i}") for i in range(NR)]
        ps = [es.enter_context(nc.psum_tensor(f"ps{i}", [P, 512], F32)) for i in range(8)]
        bf = [[] for _ in range(8)]

        raw = sb("raw", [P, NR, UW])
        wh = sb("wh", [P, NH, UW], F32R)
        wl = sb("wl", [P, NH, UW], F32R)
        x = sb("xres", [P, 2, D])
        gb = sb("gb", [P, 2, D])
        at = nc.sbuf_base
        xh = sb("xh", [P, 8, T], F32R)
        xl = sb("xl", [P, 8, T], F32R)
        xf = nc.alloc_sbuf_tensor_at("xf", [P, 2, 2048], F32, offset=at)
        cst = sb("cst", [P, NCST])
        vcol = sb("vcol", [P, NV])
        vrow = sb("vrow", [P, P])
        junk = sb("junk", [P, D])
        st = sb("st", [P, 256])
        mk2 = sb("mk2", [P, 2, T])
        mv2 = sb("mv2", [P, 2, T])
        pos_i = sb("pos_i", [P, 2], I32)
        mhalf = sb("mhalf", [P, 24])

        ident = cst[:, K_ID:K_ID + P]
        C = lambda k, n, p=P: cst[0:p, k:k + n]

        W = {k: v for k, v in I.items()}
        ffn_list = lambda nm, g, u, d: sum(
            [chunk(nm + "g", g, n, min(512, FF - n)) + chunk(nm + "u", u, n, min(512, FF - n))
             for n in range(0, FF, 512)], []) + chunk(nm + "d", d, 0, D, NF)
        plan = []
        for n in range(4):
            plan += chunk("w_in", I["w_in"], 512 * n, 512)
        for n in range(3):
            plan += chunk("w_xkv", I["w_xkv"], 512 * n, 512)
        rows = chunk("w_out", I["w_out"], 0, D)
        mkv = [chunk("mkv", I["w_mem_kv_2"], 256 * n, 256) for n in range(2)]
        plan += [rows[k] for k in POOLED] + chunk("w_xkv", I["w_xkv"], 1536, 512)
        for n in range(2):
            plan += chunk("w_xq", I["w_xq"], 512 * n, 512)
        plan += chunk("w_xo", I["w_xo"], 0, D)
        plan += mkv[0] + ffn_list("f0", I["w_gate"], I["w_up"], I["w_down"])
        plan += ffn_list("f1", I["ffn1_w_gate_2"][0], I["ffn1_w_up_2"][0], I["ffn1_w_down_2"][0]) + mkv[1]
        for n0, n in RW:
            plan += chunk("rw", I["rwkv_w_in_2"][0], n0, n)
        rows = chunk("wo0", I["w_out_2"][0], 0, D)
        plan += [rows[k] for k in LATE]
        plan += ffn_list("f2", I["ffn2_w_gate_2"][0], I["ffn2_w_up_2"][0], I["ffn2_w_down_2"][0])
        plan += ffn_list("f3", I["ffn1_w_gate_2"][1], I["ffn1_w_up_2"][1], I["ffn1_w_down_2"][1])
        for n0, n in SB:
            plan += chunk("sb", I["sb_w_in_2"][0], n0, n)
        rows = chunk("wo1", I["w_out_2"][1], 0, D)
        plan += [rows[k] for k in LATE]
        plan += ffn_list("f4", I["ffn2_w_gate_2"][1], I["ffn2_w_up_2"][1], I["ffn2_w_down_2"][1])

        NU = len(plan)
        used = [0]
        hi_tok, lo_tok, pe_tok = {}, {}, {}
        owed = []

        def load(i):
            if i >= NU:
                return
            _, src, nk, n = plan[i]
            dst = raw[:, i % NR, :].rearrange("p (k n) -> p k n", k=nk)
            sp.wait(lo_tok.get(i - NR))
            sp.e.dma_start(dst, src).then_inc(s_raw[i % NR], 16)

        def split(i):
            if i >= NU:
                return
            came, freed = (s_raw[i % NR], 16 * (i // NR + 1)), pe_tok.get(i - NH)
            r, h, l = raw[:, i % NR, :], wh[:, i % NH, :], wl[:, i % NH, :]
            hi_tok[i] = act.do(lambda e: e.activation(h, r, ACT.Copy), came, freed)
            lo_tok[i] = dve.do(lambda e: e.tensor_tensor(l, r, h.bitcast(F32), ALU.subtract), hi_tok[i], freed)
            load(i + NR)

        def use(name):
            i = used[0]
            used[0] += 1
            assert plan[i][0] == name, (plan[i][0], name)
            _, _, nk, n = plan[i]
            view = lambda t: t[:, i % NH, :].rearrange("p (k n) -> p k n", k=nk)
            pe.wait(hi_tok[i], lo_tok[i])
            return i, nk, n, view(wh), view(wl)

        def release(i, tok, hold=False):
            pe_tok[i] = tok
            if hold:
                owed.append(i + NH)
            else:
                pay()
                split(i + NH)

        def pay(n=NU):
            while owed and n:
                split(owed.pop(0))
                n -= 1

        def mm(o, l, r, start, stop):
            return lambda e: e.matmul(o, l, r, start=start, stop=stop, skip_group_check=True)

        def three(lst, o, lh, ll, rh, rl, start, stop):
            lst += [(o, lh, rh, start, False), (o, lh, rl, False, False), (o, ll, rh, False, stop)]

        def emit(lst, *after):
            pe.wait(*after)
            for a in lst[:-1]:
                pe.go(mm(*a))
            return pe.do(mm(*lst[-1]))

        def aside(side):
            if side:
                side.pop(0)()

        def put_x(name, n0, xh, xl, xt, banks, hold=False):
            at = {"kt": 0, "open": []}

            def take():
                u = use((name, n0))
                at["open"].append((at["kt"], u))
                at["kt"] += u[1]

            def half(rb):
                lst = []
                a = slice(rb * P, rb * P + P)
                kt, (i, nk, n, h, l) = at["open"][0] if rb else at["open"][-1]
                if kt == 0:
                    pe.wait(bf[banks[rb]])
                for k in range(nk):
                    pe.wait(xt[rb][(kt + k) // 4])
                    three(lst, ps[banks[rb]][:, 0:n], xh[:, kt + k, a], xl[:, kt + k, a], h[:, k, :], l[:, k, :],
                          kt + k == 0, kt + k == 7)
                tok = emit(lst)
                if rb:
                    at["open"].pop(0)
                    release(i, tok, hold)
                return tok

            return take, half

        def mm_x(name, n0, xh, xl, xt, banks, hold=False, side=None, lead=0, mid=None):
            take, half = put_x(name, n0, xh, xl, xt, banks, hold)
            per = sum(1 for q in plan if q[0] == (name, n0))
            for _ in range(lead):
                take()
                half(0)
            if mid is not None:
                mid()
                take()
                t0 = half(0)
                lead += 1
            for _ in range(lead):
                tok = half(1)
            for _ in range(per - lead):
                take()
                t0 = half(0)
                tok = half(1)
                aside(side)
            return [t0, tok]

        def mm_w(name, n0, xh, xl, xt, banks, hold=False, side=None, end=None):
            kt = 0
            while kt < 8:
                i, nk, n, h, l = use((name, n0))
                nj = n // P
                lst = []
                for k in range(nk):
                    pe.wait(xt[0][(kt + k) // 4], xt[1][(kt + k) // 4])
                    for j in range(nj):
                        if kt + k == 0 and j % 2 == 0:
                            pe.wait(bf[banks[j // 2]])
                        o = ps[banks[j // 2]][:, (j % 2) * T:(j % 2) * T + T]
                        s = slice(j * P, j * P + P)
                        st_, sp_ = kt + k == 0 and j % 2 == 0, kt + k == 7
                        lst += [(o, h[:, k, s], xh[:, kt + k, :], st_, False),
                                (o, h[:, k, s], xl[:, kt + k, :], False, False),
                                (o, l[:, k, s], xh[:, kt + k, :], False, sp_)]
                tok = emit(lst)
                kt += nk
                release(i, tok, hold)
                if kt == 8 and end is not None:
                    end(tok)
                aside(side)
            return tok

        DN = [[6, 7], [0, 1]]

        each = lambda a, n=8: [a[:, k, :] for k in range(n)]

        def mm_d(name, ah, al, at, nk, mids={}, order=None):
            for b in DN[0] + DN[1]:
                pe.wait(bf[b])

            def part(n, rb, h, l):
                lst = []
                kt = n if order is None else order[n]
                a = slice(rb * P, rb * P + P)
                for nh in range(2):
                    s = slice(nh * 512, nh * 512 + 512)
                    three(lst, ps[DN[rb][nh]][:, :], ah[kt][:, a], al[kt][:, a], h[:, 0, s], l[:, 0, s],
                          n == 0, n == nk - 1)
                return emit(lst, at[kt])

            tail = []
            for n in range(nk):
                if n in mids:
                    mids[n]()
                i, _, _, h, l = use((name, 0))
                t0 = part(n, 0, h, l)
                if n < nk - TAIL:
                    release(i, part(n, 1, h, l))
                else:
                    tail.append((i, n, h, l))
            for i, n, h, l in tail:
                t1 = part(n, 1, h, l)
                release(i, t1, True)
            return [t0, t1]

        def split_evac(src, hi, lo, *after):
            t = act.do(lambda e: e.activation(hi, src, ACT.Copy), *after)
            return dve.do(lambda e: e.tensor_tensor(lo, src, hi.bitcast(F32), ALU.subtract), t)

        def turn(src, rb, hi, lo, after, banks, between=None):
            toks = []
            for g in range(2):
                b = banks[g]
                pe.wait(bf[b], after[g])
                for k in range(4):
                    f = lambda e: e.transpose(ps[b][:, k * P:k * P + P], src[:, rb, (4 * g + k) * P:(4 * g + k + 1) * P], ident)
                    t = pe.do(f) if k == 3 else pe.go(f)
                v = ps[b][:, :].rearrange("p (k t) -> p k t", k=4)
                d = slice(rb * P, rb * P + P)
                toks.append(split_evac(v, hi[:, 4 * g:4 * g + 4, d], lo[:, 4 * g:4 * g + 4, d], t))
                bf[b] = [toks[-1]]
                if g == 0 and between is not None:
                    between()
            return toks

        def to_T(src, hi, lo, after, banks=((2, 3), (4, 5))):
            return [turn(src, rb, hi, lo, [after[rb]] * 2, banks[rb]) for rb in range(2)]

        def turn_to(src, banks=((4, 5), (6, 7))):
            toks = {}

            def mid(rb, after, between=None):
                toks[rb] = turn(src, rb, xh, xl, after, banks[rb], between)

            return toks, mid

        gn = [0]
        gfree = {}
        s_gain = [Dmas(sem(f"s_gain{i}")) for i in range(2)]

        def gain(vec):
            g = gn[0] % 2
            gn[0] += 1
            t = s_gain[g].start(pool, gb[:, g, :], vec.partition_broadcast(P), gfree.get(g))
            return gb[:, g, :], t, g

        def rstd_of(var, rs, after, eps, scale):
            t = dve.do(lambda e: e.tensor_scalar(var, var, scale, eps, ALU.mult, ALU.add), after)
            n = var.free_size()
            return pool.do(lambda e: e.tensor_tensor(rs, var, mhalf[:, 0:n], ALU.pow), t, half_tok)

        def rms_row(rb, src, after, g, dst):
            gt, gtok, gi = g
            t = square_sum(src[:, rb, :], st[:, rb:rb + 1], D, after, st_free[0])
            t = rstd_of(st[:, rb:rb + 1], st[:, 2 + rb:3 + rb], t, EPS, 1.0 / D)

            def scaled():
                gfree[gi] = dve.do(lambda e: e.scalar_tensor_tensor(
                    out=dst[:, rb, :], in0=src[:, rb, :], scalar=st[:, 2 + rb:3 + rb], in1=gt,
                    op0=ALU.mult, op1=ALU.mult), t, gtok, dst_free[0])
                st_free[0] = gfree[gi]
                return gfree[gi]

            return scaled

        def rms_rows(src, after, g, dst):
            return [rms_row(rb, src, after[rb], g, dst)() for rb in range(2)]

        st_free, dst_free = [None], [None]
        junk_by = [None]

        def square_sum(src, dst, width, *after):
            junk_by[0] = act.do(lambda e: e.activation(junk[:, 0:width], src, ACT.Square, accum_out=dst), junk_by[0], *after)
            return junk_by[0]

        def rms_add(toks, g, tmp, tmp_free, mid, pre=None, part=False):
            gt, gtok, gi = g
            done, rs, scaled, normed = {}, {}, {}, {}

            def head(rb):
                for nh in range(2):
                    c = 8 + 2 * rb + nh
                    t = square_sum(ps[DN[rb][nh]][:, :], st[:, c:c + 1], 512, toks[rb], st_free[0])
                t = dve.do(lambda e: e.tensor_tensor(st[:, 12 + rb:13 + rb], st[:, 8 + 2 * rb:9 + 2 * rb],
                                                     st[:, 9 + 2 * rb:10 + 2 * rb], ALU.add), t)
                rs[rb] = rstd_of(st[:, 12 + rb:13 + rb], st[:, 14 + rb:15 + rb], t, EPS, 1.0 / D)

            def scale(rb):
                for nh in range(2):
                    b, s = DN[rb][nh], slice(nh * 512, nh * 512 + 512)
                    scaled[rb, nh] = dve.do(lambda e: e.scalar_tensor_tensor(
                        out=tmp[:, rb, s], in0=ps[b][:, :], scalar=st[:, 14 + rb:15 + rb], in1=gt[:, s],
                        op0=ALU.mult, op1=ALU.mult), rs[rb], gtok, list(tmp_free))
                    bf[b] = [scaled[rb, nh]]
                gfree[gi] = scaled[rb, 1]

            def add(rb):
                done[rb] = []
                for nh in range(2):
                    s = slice(nh * 512, nh * 512 + 512)
                    done[rb].append(dve.do(lambda e: e.tensor_tensor(x[:, rb, s], x[:, rb, s], tmp[:, rb, s], ALU.add),
                                           scaled[rb, nh]))

            def norm(rb):
                if pre is not None:
                    normed[rb] = rms_row(rb, x, done[rb], *pre)

            def norm_end(rb):
                if pre is not None:
                    done[rb] = [normed[rb]()] * 2

            head(0)
            scale(0)
            add(0)
            if pre is None:
                mid(0, done[0])
                head(1)
                scale(1)
                add(1)
                pay(1)
            elif part:
                pay(1)
                norm(0)
                pay(1)
                head(1)
                norm_end(0)
                mid(0, done[0])
                scale(1)
                add(1)
                norm(1)
                norm_end(1)
                pay(1)
            else:
                pay(1)
                head(1)
                norm(0)
                scale(1)
                norm_end(0)
                add(1)
                mid(0, done[0])
                norm(1)
                norm_end(1)
                pay(1)

            def rest():
                mid(1, done[1])
                pay()
                st_free[0] = done[1][1]

            return rest

        def ln_add(toks, scale, xtok, g, b_, mid):
            (gt, gtok, gi), (bt, btok, bi) = g, b_

            s_ = [slice(nh * 512, nh * 512 + 512) for nh in range(2)]
            summed = {}

            def add(rb, nh):
                b, s = DN[rb][nh], s_[nh]
                summed[rb, nh] = dve.do(lambda e: e.scalar_tensor_tensor(
                    out=x[:, rb, s], in0=ps[b][:, :], scalar=scale, in1=x[:, rb, s],
                    op0=ALU.mult, op1=ALU.add), toks[rb], xtok)
                bf[b] = [summed[rb, nh]]

            def stats(rb):
                t = []
                for nh in range(2):
                    c = 32 + 6 * nh + 12 * rb
                    t.append(dve.do(lambda e: e.bn_stats(st[:, c:c + 6], x[:, rb, s_[nh]]), summed[rb, nh], st_free[0]))
                m, v, r = st[:, 16 + 2 * rb:17 + 2 * rb], st[:, 17 + 2 * rb:18 + 2 * rb], st[:, 20 + rb:21 + rb]
                t = dve.do(lambda e: e.bn_aggr(st[:, 16 + 2 * rb:18 + 2 * rb], st[:, 32 + 12 * rb:44 + 12 * rb]), t)
                tr = rstd_of(v, r, t, LN_EPS, 1.0)
                n = [dve.do(lambda e, s=s: e.scalar_tensor_tensor(out=x[:, rb, s], in0=x[:, rb, s], scalar=m, in1=gt[:, s],
                                                                  op0=ALU.subtract, op1=ALU.mult), t, gtok) for s in s_]
                d = [dve.do(lambda e, s=s: e.scalar_tensor_tensor(out=x[:, rb, s], in0=x[:, rb, s], scalar=r, in1=bt[:, s],
                                                                  op0=ALU.mult, op1=ALU.add), n[i], tr, btok)
                     for i, s in enumerate(s_)]
                gfree[gi] = gfree[bi] = st_free[0] = d[1]
                return d

            add(0, 0)
            add(0, 1)
            d0 = stats(0)
            add(1, 0)
            mid(0, d0, lambda: add(1, 1))
            d1 = stats(1)
            pay(1)

            def rest():
                mid(1, d1)
                pay()

            return rest

        def ffn(nm, xt, hb, hh, hl, rest):
            ht = []
            waiting = []
            hb_free = {}

            def back():
                n0, w, slot, toks = waiting.pop()
                for q in range(w // T):
                    b = 4 + q
                    pe.wait(bf[b])
                    for k in range(2):
                        for rb in range(2):
                            o = ps[b][:, k * T + rb * P:k * T + rb * P + P]
                            i_ = hb[:, slot, rb, (2 * q + k) * P:(2 * q + k + 1) * P]
                            pe.wait(toks[rb])
                            f = lambda e, o=o, i_=i_: e.transpose(o, i_, ident)
                            t = pe.do(f) if (k, rb) == (1, 1) else pe.go(f)
                    f0 = n0 // P + 2 * q
                    v = ps[b][:, :].rearrange("p (k t) -> p k t", k=2)
                    t2 = split_evac(v, hh[:, f0:f0 + 2, :], hl[:, f0:f0 + 2, :], t)
                    bf[b] = [t2]
                    ht.extend([t2, t2])
                hb_free[slot] = t

            w = min(512, FF)
            tg = mm_x(nm + "g", 0, xh, xl, xt, (2, 3), lead=3, mid=rest)
            sg = []
            for rb in range(2):
                t = act.do(lambda e: e.activation(hb[:, 0, rb, 0:w], ps[2 + rb][:, 0:w], ACT.Silu), tg[rb])
                bf[2 + rb] = [t]
                sg.append(t)
            tu = mm_x(nm + "u", 0, xh, xl, xt, (6, 7))
            toks = []
            for rb in range(2):
                t = dve.do(lambda e: e.tensor_tensor(hb[:, 0, rb, 0:w], hb[:, 0, rb, 0:w], ps[6 + rb][:, 0:w], ALU.mult),
                           tu[rb], sg[rb])
                bf[6 + rb] = [t]
                toks.append(t)
            waiting.append((0, w, 0, toks))

            for c, n0 in enumerate(range(512, FF, 512)):
                nq, slot = min(512, FF - n0) // T, (c + 1) % 2
                tg = mm_w(nm + "g", n0, xh, xl, xt, (0, 1))
                sg = []
                for q in range(nq):
                    t = act.do(lambda e: e.activation(hb[:, slot, q, :], ps[q][:, :], ACT.Silu), tg, hb_free.get(slot))
                    bf[q] = [t]
                    sg.append(t)
                if waiting:
                    back()
                tu = mm_w(nm + "u", n0, xh, xl, xt, (2, 3))
                for q in range(nq):
                    h, f0 = hb[:, slot, q, :], n0 // P + 2 * q
                    t = dve.do(lambda e: e.tensor_tensor(h, h, ps[2 + q][:, :], ALU.mult), tu, sg[q])
                    bf[2 + q] = [t]
                    t = split_evac(h.rearrange("p (k t) -> p k t", k=2), hh[:, f0:f0 + 2, :], hl[:, f0:f0 + 2, :], t)
                    ht.extend([t, t])
                hb_free[slot] = t
            return mm_d(nm + "d", each(hh, NF), each(hl, NF), ht, NF)

        def probe(name, ap, *after):
            if dbg is not None and name in dbg:
                d = Dmas(sem("s_dbg" + name))
                t = d.start(sp, dbg[name], ap, *after)
                sp.wait(t)

        s_i, s_c, s_v, s_l = (Dmas(sem(n)) for n in ("s_i", "s_c", "s_v", "s_l"))
        s_x = [Dmas(sem(f"s_x{rb}")) for rb in range(2)]
        x_in = I["x"][0].rearrange("(b p) d -> p b d", p=P)
        half_tok = pool.do(lambda e: e.memset(mhalf[:, :], -0.5))
        x_tok = [s_x[0].start(sp, x[:, 0, :], x_in[:, 0, :])]
        g_pre = gain(I["g_mix_pre"])
        id_tok = s_i.start(sp, cst[:, 0:P], cst_in[:, 0:P])
        load(0)
        x_tok.append(s_x[1].start(sp, x[:, 1, :], x_in[:, 1, :]))
        for i in range(1, NR):
            load(i)
        vplace, r0 = {}, 0
        for name, n in VROWS:
            vplace[name] = r0
            r0 += n
        V = lambda name, i=0, n=1: vcol[:, vplace[name] + i:vplace[name] + i + n]

        ms = ExitStack()
        mh = ms.enter_context(nc.sbuf_tensor("mh", [P, 8, T], F32R))
        ml = ms.enter_context(nc.sbuf_tensor("ml", [P, 8, T], F32R))
        ph = ExitStack()
        pb = lambda n, s, d=F32: ph.enter_context(nc.sbuf_tensor(n, s, d))
        kxT = pb("kxT", [P, 8, T])
        vx = pb("vx", [P, 2, D])
        tmp = pb("tmp0", [P, 2, D])
        qkT = pb("qkT", [P, 8, T])
        inner = ExitStack()
        ib = lambda n, s, d=F32: inner.enter_context(nc.sbuf_tensor(n, s, d))
        xn = ib("xn", [P, 2, D])
        v_sb = ib("v_sb", [P, 2, 512])
        u_sb = ib("u_sb", [P, 2, 512])
        band = ib("band", [P, 8 * T])
        wpool = ib("wpool", [P, 4, P])
        lam_in = ib("lam_in", [P, 4, 64])
        rope = ib("rope", [P, 16 * 16])
        qk = tmp

        xt = {}
        normed = [rms_row(0, x, x_tok[0], g_pre, xn)]

        def first(rb):
            t = normed.pop()()
            split(3 * rb)
            xt[rb] = turn(xn, rb, xh, xl, [[t, id_tok]] * 2, ((2, 3), (4, 5))[rb])

        first(0)
        normed.append(rms_row(1, x, x_tok[1], g_pre, xn))
        for i in range(1, 3):
            split(i)
        cst_tok = s_c.start(pool, cst[:, P:NCST], cst_in[:, P:NCST])
        s_mem = Dmas(sem("s_mem"))
        mem_tok = s_mem.start(pool, vx[:, :, :], I["mem"][0].rearrange("(b p) d -> p b d", p=P))
        g_mem = gain(I["g_mem"])
        for name, n in VROWS:
            src = I[name]
            if len(src.shape) == 3:
                src = src.rearrange("a h d -> (a h d)")
            elif len(src.shape) == 2:
                src = src.rearrange("a d -> (a d)")
            v_tok = s_v.start(pool, vrow[vplace[name]:vplace[name] + n, :], src.rearrange("(r p) -> r p", p=P))
        for j, name in enumerate(("lambda_q1", "lambda_q2", "lambda_k1", "lambda_k2")):
            l_tok = s_l.start(pool, lam_in[:, j, :], I[name].partition_broadcast(P))
        s_pos, s_band, s_wp = (Dmas(sem(n)) for n in ("s_pos", "s_band", "s_wp"))
        pos_tok = s_pos.start(pool, pos_i[:, :], I["positions"].rearrange("a (b p) -> p (a b)", p=P),
                          allow_slow_non_contiguous=True)

        def second():
            first(1)
            for i in range(4, NH):
                split(i)

        R = lambda k: rope[:, 16 * k:16 * k + 16]
        R3 = lambda k: R(k).rearrange("p (b f) -> p b f", b=2)
        COS, SIN = R3(2), R3(3)
        nlam = st[:, 66:67]
        S0 = {}

        def vectors():
            pe.wait(bf[6])
            t = pe.do(lambda e: e.transpose(ps[6][:, 0:NV], vrow[0:NV, :], cst[0:NV, 0:NV]), v_tok, id_tok)
            S0["v"] = act.do(lambda e: e.activation(vcol[:, :], ps[6][:, 0:NV], ACT.Copy), t)
            bf[6] = [S0["v"]]
            S0["gs"] = dve.do(lambda e: e.tensor_scalar(V("g_subln"), V("g_subln"), 1.0 - LAM0, None, ALU.mult), S0["v"])

        def angles():
            t = dve.do(lambda e: e.tensor_tensor(lam_in[:, 0:2, :], lam_in[:, 0:2, :], lam_in[:, 2:4, :], ALU.mult), l_tok)
            S0["l"] = dve.do(lambda e: e.tensor_reduce(st[:, 64:66], lam_in[:, 0:2, :], AX.X, ALU.add), t)
            t = dve.do(lambda e: e.tensor_copy(st[:, 68:70], pos_i[:, :]), pos_tok)
            t = dve.do(lambda e: e.tensor_tensor(R3(0), st[:, 68:70].unsqueeze(2).to_broadcast([P, 2, 8]),
                                                 C(K_FREQ, 8).unsqueeze(1).to_broadcast([P, 2, 8]), ALU.mult), t, cst_tok)
            t = dve.do(lambda e: e.tensor_scalar(R(1), R(0), 1.0 / (2 * math.pi), 12582912.0, ALU.mult, ALU.add), t)
            t = dve.do(lambda e: e.tensor_scalar(R(1), R(1), -12582912.0, None, ALU.add), t)
            c1 = 6.28125
            c2 = float(np.float32(np.round((2 * math.pi - c1) * 2 ** 20) / 2 ** 20))
            c3 = 2 * math.pi - c1 - c2
            for c in (c1, c2, c3):
                t = dve.do(lambda e: e.scalar_tensor_tensor(out=R(0), in0=R(1), scalar=-c, in1=R(0),
                                                            op0=ALU.mult, op1=ALU.add), t)
            lim = float(np.nextafter(np.float32(math.pi), np.float32(0)))
            S0["s"] = t = dve.do(lambda e: e.tensor_scalar(R(0), R(0), lim, -lim, ALU.min, ALU.max), t)
            t = dve.do(lambda e: e.scalar_tensor_tensor(out=R(2), in0=R(0), scalar=-1.0, in1=R(0),
                                                        op0=ALU.mult, op1=ALU.min), t)
            S0["c"] = dve.do(lambda e: e.tensor_scalar(R(2), R(2), math.pi / 2, None, ALU.add), t)

        def tables():
            t = act.do(lambda e: e.activation(st[:, 64:66], st[:, 64:66], ACT.Exp), S0["l"])
            t = dve.do(lambda e: e.tensor_tensor(st[:, 66:67], st[:, 65:66], st[:, 64:65], ALU.subtract), t)
            S0["lam"] = dve.do(lambda e: e.tensor_scalar(nlam, nlam, -LAM0, None, ALU.add), t)
            act.do(lambda e: e.activation(R(3), R(0), ACT.Sin), S0["s"])
            S0["rope"] = act.do(lambda e: e.activation(R(2), R(2), ACT.Sin), S0["c"])

        rot = []
        for c in range(2):
            banks = (0, 1) if c == 0 else (2, 3)
            tq = mm_x("w_in", 512 * c, xh, xl, xt, banks,
                      **(dict(side=[lambda: None, vectors, angles, tables]) if c else dict(lead=3, mid=second)))
            for rb in range(2):
                b = banks[rb]
                t = act.do(lambda e, b=b, rb=rb, c=c: e.activation(qk[:, rb, 512 * c:512 * c + 512], ps[b][:, :],
                                                                   ACT.Copy), tq[rb])
                bf[b] = [t]
                rot.append(t)
            if c == 0:
                dst_free[0] = [xt[0], xt[1]]
                mem_n = rms_rows(vx, [mem_tok] * 2, g_mem, xn)
        v_ok, gs_ok, lam_ok, rope_ok = (S0[n] for n in ("v", "gs", "lam", "rope"))
        band_tok = s_band.start(pool, band[:, :], band_in, rot)
        wp_tok = s_wp.start(pool, wpool[:, :, :], I["w_pool"].rearrange("g c d -> c g d"))

        rt = {}
        for rb in range(2):
            v = qk[:, rb, :].rearrange("p (h d) -> p h d", d=64)
            t1, t2 = v[:, :, 0:8], v[:, :, 8:16]
            cs, sn = (z[:, rb, :].unsqueeze(1).to_broadcast([P, 16, 8]) for z in (COS, SIN))
            w4 = [junk[:, 128 * j + 512 * rb:128 * j + 512 * rb + 128].rearrange("p (h d) -> p h d", d=8) for j in range(4)]
            tt = lambda o, a, b, op, *w: dve.do(lambda e: e.tensor_tensor(o, a, b, op), *w)
            a1 = tt(w4[0], t1, cs, ALU.mult, rot, rope_ok, junk_by[0])
            a2 = tt(w4[1], t2, sn, ALU.mult)
            a3 = tt(w4[2], t2, cs, ALU.mult)
            a4 = tt(w4[3], t1, sn, ALU.mult)
            tt(t1, w4[0], w4[1], ALU.subtract, a4)
            rt[rb] = tt(t2, w4[2], w4[3], ALU.add)

        mt = []
        tv = mm_x("w_in", 1024, xh, xl, xt, (0, 1), side=[lambda: None] + [
            lambda rb=rb: mt.append(turn(xn, rb, mh, ml, [mem_n[rb]] * 2, ((6, 7), (4, 5))[rb])) for rb in range(2)])
        v_tok2 = []
        for rb in range(2):
            t = act.do(lambda e, rb=rb: e.activation(v_sb[:, rb, :], ps[rb][:, :], ACT.Copy), tv[rb])
            bf[rb] = [t]
            v_tok2.append(t)

        qk_tok = []

        def turn_qk(g):
            b = 4 + g % 2
            pe.wait(bf[b])
            for k in range(2):
                for rb in range(2):
                    pe.wait(rt[rb])
                    o = ps[b][:, k * T + rb * P:k * T + rb * P + P]
                    i_ = qk[:, rb, (2 * g + k) * P:(2 * g + k + 1) * P]
                    f = lambda e, o=o, i_=i_: e.transpose(o, i_, ident)
                    t = pe.do(f) if (k, rb) == (1, 1) else pe.go(f)
            t = act.do(lambda e: e.activation(
                qkT[:, 2 * g:2 * g + 2, :], ps[b][:, :].rearrange("p (k t) -> p k t", k=2), ACT.Copy), t)
            bf[b] = [t]
            qk_tok.append(t)

        tu = mm_x("w_in", 1536, xh, xl, xt, (2, 3), side=[lambda g=g: turn_qk(g) for g in range(4)])
        u_tok = []
        for rb in range(2):
            t = act.do(lambda e, rb=rb: e.activation(u_sb[:, rb, :], ps[2 + rb][:, :], ACT.Copy), tu[rb])
            bf[2 + rb] = [t]
            u_tok.append(t)
        mixed_ready = tu

        pl = xn.rearrange("p b d -> p (b d)")[:, 0:1024].rearrange("p (g t) -> p g t", g=4)
        bandv = band[:, :].rearrange("p (s g t) -> p s g t", s=2, g=4)
        pl_tok = []

        def pooled(q):
            b = 6 + q
            lst = []
            for k in range(2):
                g = 2 * q + k
                for s in range(2):
                    lst.append((ps[b][:, k * T:k * T + T], u_sb[:, s, g * P:g * P + P], bandv[:, s, g, :], s == 0, s == 1))
            t = emit(lst, bf[b], u_tok, band_tok)
            t = act.do(lambda e: e.activation(
                pl[:, 2 * q:2 * q + 2, :], ps[b][:, :].rearrange("p (k t) -> p k t", k=2), ACT.Copy), t, mt)
            bf[b] = [t]
            pl_tok.append(t)

        mix_tok = {}

        def mixed(q):
            b = 6 + q
            lst = [(ps[b][:, k * T:k * T + T], wpool[:, 2 * q + k, :], pl[:, 2 * q + k, :], True, True) for k in range(2)]
            t = emit(lst, bf[b], pl_tok, wp_tok)
            half = [ps[b][:, k * T:k * T + T] for k in range(2)]
            for k in range(2):
                g = 2 * q + k
                t1 = act.do(lambda e: e.activation(xh[:, 4 + g, :], half[k], ACT.Copy,
                                                   scale=V("pool_scale", g)), t, v_ok, mixed_ready)
            for k in range(2):
                g = 2 * q + k
                t2 = dve.do(lambda e: e.scalar_tensor_tensor(
                    out=xl[:, 4 + g, :], in0=half[k], scalar=V("pool_scale", g), in1=xh[:, 4 + g, :].bitcast(F32),
                    op0=ALU.mult, op1=ALU.subtract), t1)
                mix_tok[4 + g] = t2
            bf[b] = [t2]

        kx_tok, vx_tok = [], []

        def kx_chunk(c, side):
            banks = (0, 1) if c == 0 else (2, 3)

            def end(t):
                for q in range(2):
                    b = banks[q]
                    t2 = act.do(lambda e, j=4 * c + 2 * q: e.activation(
                        kxT[:, j:j + 2, :], ps[b][:, :].rearrange("p (k t) -> p k t", k=2), ACT.Copy), t)
                    bf[b] = [t2]
                    kx_tok.append(t2)

            mm_w("w_xkv", 512 * c, mh, ml, mt, banks, side=side, end=end)

        def vx_evac(c, banks, t):
            for rb in range(2):
                b = banks[rb]
                t2 = act.do(lambda e: e.activation(vx[:, rb, 512 * c:512 * c + 512], ps[b][:, :], ACT.Copy), t[rb])
                bf[b] = [t2]
                vx_tok.append(t2)

        pbuf = qk[:, 0:2, :].rearrange("p b d -> p (b d)")[:, 0:1536].rearrange("p (s m k) -> p s m k", s=2, m=2)
        pT = inner.enter_context(nc.sbuf_tensor("aT", [P, 4, 3, P], F32))
        p_free = {}
        a_tok = {}
        sc8 = 64 ** -0.5
        KEYS = (slice(0, P), slice(P, 3 * P))

        def scores(h):
            s = h % 2
            banks = (4, 5) if s == 0 else (6, 7)
            c = 72 + 16 * s
            S = lambda k, i, m=0, n=2: st[:, c + 4 * k + 2 * i + m:c + 4 * k + 2 * i + m + n]
            tm = []
            for m in range(2):
                d = slice(64 * m, 64 * m + 64)
                t = emit([(ps[banks[m]][:, KEYS[i]], qkT[d, h, i * P:i * P + P], qkT[d, 4 + h, 0:(i + 1) * P], i == 0, i == 1)
                          for i in range(2)], bf[banks[m]], qk_tok)
                t = dve.do(lambda e, m=m: e.tensor_tensor(pbuf[:, s, m, :], ps[banks[m]][:, 0:384], C(K_AM, 384), ALU.add),
                           t, p_free.get(s), rt[0], rt[1])
                bf[banks[m]] = [t]
                tm.append(t)
            for i in range(2):
                t = dve.do(lambda e, i=i: e.tensor_reduce(S(0, i), pbuf[:, s, :, KEYS[i]], AX.X, ALU.max), tm)
            t = dve.do(lambda e: e.tensor_scalar(st[:, c + 4:c + 8], st[:, c:c + 4], -sc8, None, ALU.mult), t)
            for i in range(2):
                for m in range(2):
                    te = act.do(lambda e, i=i, m=m: e.activation(
                        pbuf[:, s, m, KEYS[i]], pbuf[:, s, m, KEYS[i]], ACT.Exp, scale=sc8, bias=S(1, i, m, 1),
                        accum_out=S(2, i, m, 1)), t)
            t = dve.do(lambda e: e.reciprocal(st[:, c + 12:c + 16], st[:, c + 8:c + 12]), te)
            o2 = st[:, c + 12:c + 16].rearrange("p (i m) -> p i m", i=2)[:, :, 1]
            t = dve.do(lambda e: e.tensor_tensor(o2, o2, nlam.to_broadcast([P, 2]), ALU.mult), t, lam_ok)
            for i in range(2):
                p0, p1 = pbuf[:, s, 0, KEYS[i]], pbuf[:, s, 1, KEYS[i]]
                t2 = dve.do(lambda e, p0=p0, i=i: e.tensor_scalar(p0, p0, S(3, i, 0, 1), None, ALU.mult), t)
                a_tok[h, i] = dve.do(lambda e, p0=p0, p1=p1, i=i: e.scalar_tensor_tensor(
                    out=p0, in0=p1, scalar=S(3, i, 1, 1), in1=p0, op0=ALU.mult, op1=ALU.add), t2)

        aT_tok = {}

        def turn_a(h):
            s = h % 2
            b = 4 + h
            pe.wait(bf[b], a_tok[h, 0], a_tok[h, 1])
            for k in range(3):
                f = lambda e, k=k: e.transpose(ps[b][:, k * P:k * P + P], pbuf[:, s, 0, k * P:k * P + P], ident)
                t = pe.do(f) if k == 2 else pe.go(f)
            p_free[s] = t
            aT_tok[h] = act.do(lambda e: e.activation(
                pT[:, h, :, :], ps[b][:, 0:384].rearrange("p (k t) -> p k t", k=3), ACT.Copy), t)
            bf[b] = [aT_tok[h]]

        kx_chunk(0, [lambda: scores(0), lambda: pooled(0), lambda: pooled(1), lambda: (mixed(0), mixed(1))])
        kx_chunk(1, [lambda: scores(1), lambda: turn_a(0), lambda: scores(2), lambda: turn_a(1)])
        vx_evac(0, (0, 1), mm_x("w_xkv", 1024, mh, ml, mt, (0, 1), side=[
            lambda: scores(3), lambda: turn_a(2), lambda: None, lambda: turn_a(3)]))

        dan = u_sb
        for i in range(2):
            b = 4 + i
            lst = []
            for h in range(4):
                for k in range(i + 1):
                    lst.append((ps[b][:, h * P:h * P + P], pT[:, h, i + k, :], v_sb[:, k, h * P:h * P + P],
                                k == 0, k == i))
            t = emit(lst, bf[b], list(aT_tok.values()), v_tok2)
            sq = junk[:, 512 * i:512 * i + 512]
            t = act.do(lambda e, b=b, sq=sq: e.activation(sq, ps[b][:, :], ACT.Square), t)
            t = dve.do(lambda e, i=i, sq=sq: e.tensor_reduce(st[:, 104 + 4 * i:108 + 4 * i],
                                                      sq.rearrange("p (h d) -> p h d", h=4), AX.X, ALU.add), t)
            t = rstd_of(st[:, 104 + 4 * i:108 + 4 * i], st[:, 112 + 4 * i:116 + 4 * i], t, EPS, 1.0 / P)
            t = dve.do(lambda e, b=b, i=i: e.tensor_tensor(
                dan[:, i, :].rearrange("p (h d) -> p h d", h=4), ps[b][:, :].rearrange("p (h d) -> p h d", h=4),
                st[:, 112 + 4 * i:116 + 4 * i].unsqueeze(2).to_broadcast([P, 4, P]), ALU.mult), t, pl_tok)
            bf[b] = [t]
            if i == 0:
                d0 = t
        d1 = t
        probe("dan", dan[:, :, :], d1)
        vx_take, vx_half = put_x("w_xkv", 1536, mh, ml, mt, (2, 3), True)

        def turn_dan():
            for q in range(2):
                b = 4 + q
                pe.wait(bf[b])
                for k in range(2):
                    for rb in range(2):
                        pe.wait(d0, d1)
                        o = ps[b][:, k * T + rb * P:k * T + rb * P + P]
                        i_ = dan[:, rb, (2 * q + k) * P:(2 * q + k + 1) * P]
                        f = lambda e, o=o, i_=i_: e.transpose(o, i_, ident)
                        t = pe.do(f) if (k, rb) == (1, 1) else pe.go(f)
                v = ps[b][:, :].rearrange("p (k t) -> p k t", k=2)
                t1 = act.do(lambda e: e.activation(xh[:, 2 * q:2 * q + 2, :], v, ACT.Copy,
                                                   scale=V("g_subln")), t, gs_ok, mixed_ready)
                t2 = dve.do(lambda e: e.scalar_tensor_tensor(
                    out=xl[:, 2 * q:2 * q + 2, :], in0=v, scalar=V("g_subln"), in1=xh[:, 2 * q:2 * q + 2, :].bitcast(F32),
                    op0=ALU.mult, op1=ALU.subtract), t1)
                bf[b] = [t2]
                mix_tok[2 * q] = mix_tok[2 * q + 1] = t2

        g_post = gain(I["g_mix_post"])
        g_pre = gain(I["g_x_pre"])
        t = mm_d("w_out", each(xh), each(xl), mix_tok, 8, {3: turn_dan}, POOLED)
        probe("mixT", xh[:, :, :].bitcast(F32), list(mix_tok.values()))
        inner.close()
        xn = pb("xn2", [P, 2, D])
        pbx = pb("pbx", [P, 4, 2, T])
        pTx = pb("pTx", [P, 2, 2, T])
        m2 = pb("m2", [P, 2, D])
        for _ in range(3):
            vx_take()
            vx_half(0)
            vx_half(1)
        dst_free[0] = t
        m2_free = t
        xt, turn_x = turn_to(xn)
        tv = []

        def mid(rb, after):
            turn_x(rb, after)
            if rb == 0:
                vx_take()
                tv.extend([vx_half(0), vx_half(1)])

        rest = rms_add(t, g_post, tmp, list(p_free.values()) + qk_tok, mid, pre=(g_pre, xn))
        vx_evac(1, (2, 3), tv)
        rest()
        m2_tok = s_mem.start(pool, m2[:, :, :], I["mem_2"][0].rearrange("(b p) d -> p b d", p=P), m2_free)
        probe("x1", x[:, :, :], xt[1])

        xqT = qkT
        xq_tok = []

        def soft_attn(nh, qk_pairs, scale, pbuf, pTb, vtile, finish, ktok, vtok, sbanks, tbanks, obanks, at=128):
            free_t, tk, tp = {}, {}, {}

            def one(h):
                s, b, c = h, sbanks[h % len(sbanks)], at + 8 * h
                pw = ps[b][:, :].rearrange("p (b m) -> p b m", b=2)
                lst = []
                for tb in range(2):
                    prs = qk_pairs(h, tb)
                    for j, (l, r) in enumerate(prs):
                        lst.append((pw[:, tb, :], l, r, j == 0, j == len(prs) - 1))
                t = emit(lst, bf[b], ktok)
                t = dve.do(lambda e: e.tensor_reduce(st[:, c:c + 2], pw, AX.X, ALU.max), t, st_att[0])
                t = dve.do(lambda e: e.tensor_scalar(st[:, c + 2:c + 4], st[:, c:c + 2], -scale, None, ALU.mult), t)
                for tb in range(2):
                    t = act.do(lambda e, tb=tb: e.activation(pbuf[:, s, tb, :], pw[:, tb, :], ACT.Exp, scale=scale,
                                                             bias=st[:, c + 2 + tb:c + 3 + tb],
                                                             accum_out=st[:, c + 4 + tb:c + 5 + tb]), t)
                bf[b] = [t]
                t = dve.do(lambda e: e.reciprocal(st[:, c + 6:c + 8], st[:, c + 4:c + 6]), t)
                for tb in range(2):
                    t2 = dve.do(lambda e, tb=tb: e.tensor_scalar(pbuf[:, s, tb, :], pbuf[:, s, tb, :],
                                                                 st[:, c + 6 + tb:c + 7 + tb], None, ALU.mult), t)
                tk[h] = t2

            def turned_p(h):
                s, b = h % 2, tbanks[h % len(tbanks)]
                pe.wait(bf[b], tk[h])
                for mb in range(2):
                    for tb in range(2):
                        o = ps[b][:, mb * T + tb * P:mb * T + tb * P + P]
                        f = lambda e, o=o, tb=tb, mb=mb: e.transpose(o, pbuf[:, h, tb, mb * P:mb * P + P], ident)
                        t = pe.do(f) if (mb, tb) == (1, 1) else pe.go(f)
                t = act.do(lambda e: e.activation(pTb[:, s, :, :], ps[b][:, :].rearrange("p (m t) -> p m t", m=2),
                                                  ACT.Copy), t, free_t.get(s))
                bf[b] = [t]
                tp[h] = t

            def two(h):
                s, ob = h % 2, obanks[h % len(obanks)]
                lst = []
                lts = vtile(h)
                for j, lt in enumerate(lts):
                    for mb in range(2):
                        lst.append((ps[ob][:, j * T:j * T + T], lt(mb), pTb[:, s, mb, :], mb == 0, mb == 1))
                t = emit(lst, bf[ob], tp[h], vtok)
                free_t[s] = t
                bf[ob] = [finish(h, ps[ob], t)]

            st2 = [lambda: turned_p(0)]
            for h in range(1, nh):
                st2 += [lambda h=h: turned_p(h), lambda h=h: two(h - 1)]
            return [lambda h=h: one(h) for h in range(nh)] + st2 + [lambda: two(nh - 1)]

        st_att = [None]

        xo_tok, xq_done = {}, []

        def fin_x(h, bank, t):
            r = split_evac(bank[:, :].rearrange("p (k t) -> p k t", k=2), xh[:, 2 * h:2 * h + 2, :],
                           xl[:, 2 * h:2 * h + 2, :], t, xq_done)
            xo_tok[2 * h] = xo_tok[2 * h + 1] = r
            return r

        steps = soft_attn(4, lambda h, tb: [(xqT[:, 2 * h + j, tb * P:tb * P + P], kxT[:, 2 * h + j, :]) for j in range(2)],
                  256 ** -0.5, pbx, pTx, lambda h: [lambda mb, j=j: vx[:, mb, (2 * h + j) * P:(2 * h + j + 1) * P]
                                                    for j in range(2)],
                  fin_x, xq_tok, vx_tok, (4, 5), (4, 5), (2, 3))
        for c in range(2):
            banks = (0, 1) if c == 0 else (2, 3)
            t = mm_w("w_xq", 512 * c, xh, xl, xt, banks, side=[lambda: None] + steps[:2] if c else None)
            for q in range(2):
                b = banks[q]
                t2 = act.do(lambda e, b=b, j=4 * c + 2 * q: e.activation(
                    xqT[:, j:j + 2, :], ps[b][:, :].rearrange("p (k t) -> p k t", k=2), ACT.Copy), t, list(a_tok.values()),
                    kx_tok)
                bf[b] = [t2]
                xq_tok.append(t2)
        xq_done.append(t)
        turn_m = [lambda rb=rb: turn(m2, rb, mh, ml, [m2_tok] * 2, ((0, 1), (6, 7))[rb]) for rb in range(2)]
        mt = [turn_m[0]()]
        steps[2]()
        mt.append(turn_m[1]())
        for step in steps[3:9]:
            step()
        g_post = gain(I["g_x_post"])
        g_pre = gain(I["g_ffn_pre"])
        t = mm_d("w_xo", each(xh), each(xl), xo_tok, 8, {1: steps[9], 2: steps[10], 4: steps[11]})
        tk = mm_w("mkv", 0, mh, ml, mt, (2,), hold=True)
        dst_free[0] = t
        xt, turn_x = turn_to(xn)

        def mid(rb, after):
            turn_x(rb, after)
            if rb == 0:
                bf[2] = [act.do(lambda e: e.activation(mk2[:, :, :], ps[2][:, :].rearrange("p (k t) -> p k t", k=2),
                                                       ACT.Copy), tk)]

        rest = rms_add(t, g_post, tmp, [], mid, pre=(g_pre, xn), part=True)
        mk_tok = bf[2][0]
        probe("x2", x[:, :, :], xt[0])
        ph.close()

        def open_ffn(n):
            s = ExitStack()
            a = lambda nm, sh, d=F32: s.enter_context(nc.sbuf_tensor(nm + n, sh, d))
            return s, a("fhb", [P, 2, 2, 512]), a("fhh", [P, NF, T], F32R), a("fhl", [P, NF, T], F32R)

        fs, hb, hh, hl = open_ffn("0")
        t = ffn("f0", xt, hb, hh, hl, rest)
        g_post = gain(I["g_ffn_post"])
        xt, mid = turn_to(x)
        rest = rms_add(t, g_post, hb[:, :, :, :].rearrange("p s b n -> p (s b n)").rearrange("p (b n) -> p b n", b=2), [],
                       mid)
        fs.close()

        def scale_x(*after):
            return pool.do(lambda e: e.tensor_scalar(x[:, :, :], x[:, :, :], ALPHA, None, ALU.mult), *after)

        def norm_of(i, j):
            return gain(I["ln_g_2"][i, j]), gain(I["ln_b_2"][i, j])

        def half_ffn(nm, i, j, rest, xt, mid_of=None, side=None):
            fs, hb, hh, hl = open_ffn(nm)
            xa = []

            def start():
                rest()
                xa.append(scale_x(xt[0], xt[1]))

            g, b = norm_of(i, j)
            t = ffn(nm, xt, hb, hh, hl, start)
            xt2, turn_x = turn_to(x) if mid_of is None else (None, mid_of)

            def mid(rb, *a):
                turn_x(rb, *a)
                aside(side)

            aside(side)
            rest2 = ln_add(t, 0.5, xa, g, b, mid)
            fs.close()
            return rest2, xt2

        def mem_attn(mqT, mq_tok, dst, pbm, pTm, sbanks, tbanks, obanks):
            toks = []
            st_att[0] = mq_tok

            def fin(h, bank, t):
                o = slice(64 * (h % 2), 64 * (h % 2) + 64)
                r = act.do(lambda e: e.activation(dst[o, h // 2, :], bank[o, 0:T], ACT.Copy), t)
                toks.append(r)
                return r

            def pairs(h, tb):
                o = slice(64 * (h % 2), 64 * (h % 2) + 64)
                return [(mqT[o, h // 2, tb * P:tb * P + P], mk2[o, h // 2, :])]

            return toks, soft_attn(4, pairs, 0.125, pbm, pTm,
                                   lambda h: [lambda mb: mv2[:, mb, (h // 2) * P:(h // 2) * P + P]],
                                   fin, [mk_tok, mq_tok], mv_tok, sbanks, tbanks, obanks)

        mv_done = []

        mv_take, mv_half = put_x("mkv", 256, mh, ml, mt, (2, 3), True)

        def mv():
            mv_take()
            mv_done[:] = [mv_half(0), mv_half(1)]

        rest, xt = half_ffn("f1", 0, 0, rest, xt, side=[mv, mv])
        mv_tok = []
        for rb in range(2):
            t = act.do(lambda e: e.activation(mv2[:, rb, :], ps[2 + rb][:, 0:T], ACT.Copy), mv_done[rb])
            bf[2 + rb] = [t]
            mv_tok.append(t)
        ms.close()

        tt = lambda o, a, b, op, *w: dve.do(lambda e: e.tensor_tensor(o, a, b, op), *w)
        ts = lambda o, a, s1, s2, o1, o2, *w: dve.do(lambda e: e.tensor_scalar(o, a, s1, s2, o1, o2), *w)
        stt = lambda o, a, s_, b, o1, o2, *w: dve.do(
            lambda e: e.scalar_tensor_tensor(out=o, in0=a, scalar=s_, in1=b, op0=o1, op1=o2), *w)
        fn = lambda o, i_, f, *w, **k: act.do(lambda e: e.activation(o, i_, f, **k), *w)
        VB = lambda name: V(name, 0, 6).unsqueeze(2).to_broadcast([P, 6, T])
        flat = lambda a: a.rearrange("p c t -> p (c t)")

        rs = ExitStack()
        ra = lambda nm, sh, d=F32: rs.enter_context(nc.sbuf_tensor("r" + nm, sh, d))
        Rr, Kk, Vv, KK, AA, BV = (ra(n, [P, 6, T]) for n in ("R", "K", "V", "KK", "AA", "BV"))
        Vtm = ra("Vtm", [P, 2, C7])
        mqT = ra("mq", [P, 2, T])
        mo = ra("mo", [P, 2, T])
        DD = ra("DD", [P, 2, T])
        gup = ra("gup", [P, C7])
        zsc = ra("zsc", [P, 6])
        i24, iT = ra("i24", [P, 24]), ra("iT", [12, T])
        s1 = ExitStack()
        at1 = nc.sbuf_base
        rc = lambda nm, n: s1.enter_context(nc.sbuf_tensor("r" + nm, [P, n], F32))
        ga = rc("ga", 3080)
        at2 = nc.sbuf_base
        gb2 = rc("gb2", 3072)
        at3 = nc.sbuf_base
        gc = rc("gc", 3840)
        six = lambda a: a.rearrange("p (c t) -> p c t", t=T)
        LD, w1, w2 = six(ga[:, 0:1536]), six(gb2[:, 0:1536]), six(gb2[:, 1536:3072])
        zs = ga[:, 1536:1536 + 6 * (T + 1)].rearrange("p (s k t) -> p s k t", s=3, k=2)
        wab = gc[:, 0:C7]
        pbm = gc[:, 768:2816].rearrange("p (h b t) -> p h b t", h=4, b=2)
        pTm = gc[:, 2816:3840].rearrange("p (h b t) -> p h b t", h=2, b=2)

        rest()
        xk = [xt[0], xt[1]]
        s_up = Dmas(sem("s_up"))
        s_up.start(pool, wab[0:64, :], I["rwkv_w_up_2"][0], xk)
        s_up.start(pool, wab[64:128, :], I["rwkv_a_up_2"][0])
        up_tok = s_up.start(pool, gup[:, :], I["rwkv_g_up_2"][0])
        z0_tok = pool.do(lambda e: e.memset(zs[:, :, :, 0:1], 0.0), xk)
        xa = scale_x(xk)

        tiles = {0: Rr, 1: Kk, 2: Vv, 3: DD}
        zfree, z_tok = {}, {}
        n_z = [0]

        def shift(j, b, t):
            sl = n_z[0] % 3
            n_z[0] += 1
            dst = tiles[j // 6][:, j % 6:j % 6 + 2, :]
            cur, prev = zs[:, sl, :, 1:T + 1], zs[:, sl, :, 0:T]
            t1 = fn(cur, ps[b][:, :].rearrange("p (k t) -> p k t", k=2), ACT.Copy, t, zfree.get(sl), z0_tok)
            bf[b] = [t1]

            lane = pool if 12 <= j < 18 else dve
            t2 = lane.do(lambda e: e.tensor_tensor(dst, prev, cur, ALU.subtract), t1)
            if lane is pool:
                mu = V("rwkv_mu_2", j, 2).unsqueeze(2).to_broadcast([P, 2, T])
                t2 = pool.do(lambda e: e.tensor_tensor(dst, dst, mu, ALU.mult), t2)
                t2 = pool.do(lambda e: e.tensor_tensor(dst, dst, cur, ALU.add), t2)
            else:
                for k in range(2):
                    t2 = stt(dst[:, k, :], dst[:, k, :], V("rwkv_mu_2", j + k), cur[:, k, :], ALU.mult, ALU.add, t2)
            zfree[sl] = z_tok[j] = t2

        K = {}
        DEC = -math.exp(-0.5)
        hf = [slice(k * T, k * T + T) for k in range(2)]
        pair = lambda b: ps[b][:, :].rearrange("p (k t) -> p k t", k=2)

        def f_small():
            K["td"] = fn(DD[0:64, 0, :], DD[0:64, 0, :], ACT.Tanh, z_tok[18])
            K["dg"] = fn(DD[:, 1, :], DD[:, 1, :], ACT.Sigmoid, z_tok[18])

        def f_w(q):
            b = 4 + q % 2
            t = emit([(ps[b][:, hf[k]], wab[0:64, (2 * q + k) * P:(2 * q + k + 1) * P], DD[0:64, 0, :], True, True)
                      for k in range(2)], bf[b], K["td"], up_tok)
            for k in range(2):
                c = 2 * q + k
                t2 = fn(LD[:, c, :], ps[b][:, hf[k]], ACT.Sigmoid, t, bias=V("rwkv_w0_2", c))
                bf[b] = [t2]
                for n in range(2):
                    u = slice(n * P, n * P + P)
                    K["scan"] = dve.do(lambda e: e.tensor_tensor_scan(w1[:, c, u], C(K_ONE, P), LD[:, c, u], 0.0,
                                                                      ALU.mult, ALU.add), t2)

        def f_a(q):
            b = 6 + q % 2
            t = emit([(ps[b][:, hf[k]], wab[64:128, (2 * q + k) * P:(2 * q + k + 1) * P], DD[64:128, 0, :], True, True)
                      for k in range(2)], bf[b], z_tok[18], up_tok)
            for k in range(2):
                K["a"] = fn(AA[:, 2 * q + k, :], ps[b][:, hf[k]], ACT.Sigmoid, t, bias=V("rwkv_a0_2", 2 * q + k))
            bf[b] = [K["a"]]

        def f_ka():
            K["ka"] = stt(BV[:, :, :], AA[:, :, :], -1.0, VB("rwkv_k_a_2"), ALU.add, ALU.mult, K["a"], K["n2"])

        def f_mid():
            L4 = w1.rearrange("p c (n t) -> p c n t", t=P)
            t = tt(zsc[:, :], L4[:, :, 0, P - 1], L4[:, :, 0, 63], ALU.subtract, K["scan"])
            K["zsc"] = tt(zsc[:, :], zsc[:, :], L4[:, :, 1, 63], ALU.add, t)
            f3 = lambda a: flat(a).rearrange("p (n t) -> p n t", t=P)
            K["lr"] = pool.do(lambda e: e.tensor_tensor(f3(w2), f3(w1), f3(w1)[:, :, 63:64].to_broadcast([P, 12, P]), ALU.subtract),
                              K["scan"])

        def f_lp():
            K["lp"] = pool.do(lambda e: e.tensor_tensor(LD, w2, LD, ALU.subtract), K["lr"])

        def f_exp1():
            K["e3"] = fn(w1, w2, ACT.Exp, K["lr"], K["zsc"], scale=-DEC)

        def f_exp2():
            K["e2"] = fn(LD, LD, ACT.Exp, K["lp"], scale=DEC)

        def f_exp3():
            K["e1"] = fn(w2, w2, ACT.Exp, K["lp"], K["e3"], scale=DEC)
            K["zs"] = fn(zsc[:, :], zsc[:, :], ACT.Exp, K["zsc"], scale=DEC)

        def f_kk():
            K["kk"] = pool.do(lambda e: e.tensor_tensor(KK[:, :, :], Kk[:, :, :], VB("rwkv_k_k_2"), ALU.mult), z_tok[10])

        def f_sq():
            K["sq"] = fn(BV[:, :, :], KK[:, :, :], ACT.Square, K["kk"])

        def f_norm():
            t = emit([(ps[4][:, 12 * tb + 2 * c:12 * tb + 2 * c + 2], BV[:, c, tb * P:tb * P + P], C(K_SEL2, 2), True, True)
                      for tb in range(2) for c in range(6)], bf[4], K["sq"])
            K["n2"] = t
            t = ts(i24[:, :], ps[4][:, 0:24], 1e-24, None, ALU.max, ALU.bypass, t)
            bf[4] = [t]
            t = dve.do(lambda e: e.reciprocal(i24[:, :], i24[:, :]), t)
            K["i24"] = fn(i24[:, :], i24[:, :], ACT.Sqrt, t)

        def f_normT():
            pe.wait(bf[5], K["i24"])
            for tb in range(2):
                t = pe.do(lambda e: e.transpose(ps[5][0:12, tb * P:tb * P + P], i24[:, 12 * tb:12 * tb + 12], ident))
            K["iT"] = fn(iT[:, :], ps[5][0:12, 0:T], ACT.Copy, t)
            bf[5] = [K["iT"]]

        def f_nb():
            K["nb"] = stt(AA[:, :, :], KK[:, :, :], -1.0, AA[:, :, :], ALU.mult, ALU.mult, K["kk"], K["ka"])

        def f_kp():
            K["kp"] = tt(KK[:, :, :], KK[:, :, :], LD, ALU.mult, K["e2"], K["nb"], K["sq"])

        def f_b():
            K["b"] = tt(AA[:, :, :], AA[:, :, :], w1, ALU.mult, K["e3"], K["nb"])

        def f_unit(q):
            b = (4, 6, 7)[q]
            t = emit([(ps[b][:, hf[k]], C(K_SELH + (2 * q + k) * P, P, 12), iT[:, :], True, True)
                      for k in range(2)], bf[b], K["iT"])
            two_ = slice(2 * q, 2 * q + 2)
            tt(KK[:, two_, :], KK[:, two_, :], pair(b), ALU.mult, t, K["kp"])
            K["u"] = K["u", q] = tt(AA[:, two_, :], AA[:, two_, :], pair(b), ALU.mult, K["b"])
            bf[b] = [K["u"]]

        nop = lambda: None
        steps1 = [f_small, nop, lambda: f_w(0), lambda: f_w(1), lambda: (f_w(2), f_a(0), f_a(1)), lambda: (f_a(2), f_mid(), f_lp())]
        steps2 = [f_kk, lambda: (f_exp1(), f_exp2()), nop, f_sq, f_exp3, f_norm, f_ka, lambda: (f_nb(), f_normT()), f_kp, f_b,
                  lambda: f_unit(0), lambda: (f_unit(1), f_unit(2))]
        side = []
        for c, (n0, w) in enumerate(RW):
            banks = ((0, 1), (2, 3))[c % 2]
            t = mm_w("rw", n0, xh, xl, xt, banks, side=side)
            if n0 == 2560:
                mq_tok = fn(mqT[:, :, :], pair(banks[0]), ACT.Copy, t)
                bf[banks[0]] = [mq_tok]
            else:
                for q in range(w // T):
                    shift(n0 // P + 2 * q, banks[q], t)
            if n0 == 2304:
                side += steps1
            if n0 == 1280:
                side += steps2
        in_done = t

        def turned(src, tb, dst, banks, after):
            def part(q):
                b, n = banks[q], (4, 2)[q]
                pe.wait(bf[b], after, z_tok[16], K.get("kh"), K["u"])
                for k in range(n):
                    f = lambda e: e.transpose(ps[b][:, k * P:k * P + P], src[:, 4 * q + k, tb * P:tb * P + P], ident)
                    t = pe.do(f) if k == n - 1 else pe.go(f)
                t = fn(dst[:, 512 * q:512 * q + n * P], ps[b][:, 0:n * P], ACT.Copy, t)
                bf[b] = [t]
                return t
            return part

        mo_tok, steps = mem_attn(mqT, mq_tok, mo, pbm, pTm, (6, 7), (6,), (7,))
        while side:
            side.pop(0)()

        XI = ga[:, 0:3072].rearrange("p (m t) -> p m t", t=P)
        XIg = lambda g: XI[:, 4 * g:4 * g + 4, :]
        APg = lambda g: xf[:, g // 4, 512 * (g % 4):512 * (g % 4) + 512].rearrange("p (m t) -> p m t", t=P)
        places = (gb[:, 0, :], gb[:, 1, :], junk)
        TI = [a[:, 0:512].rearrange("p (m t) -> p m t", t=P) for a in places]
        Qm = [a[:, 512:768].rearrange("p (m t) -> p m t", t=64) for a in places]
        slot = {0: gfree[0], 1: gfree[1], 2: junk_by[0]}
        flat2 = gb[:, :, :].rearrange("p a n -> p (a n)")
        MR = [a.rearrange("p (m t) -> p m t", t=P) for a in (gc[:, 0:1536], flat2[:, 0:1536])]
        BM = [a.rearrange("p (m t) -> p m t", t=2 * P) for a in (gb2[:, :], xf[:, :, :].rearrange("p a n -> p (a n)")[:, 0:3072])]
        M_ = lambda k, n=P: C(k, n).bitcast(I32)
        H = lambda h, ck: (slice(64 * (h % 2), 64 * (h % 2) + 64), h // 2, slice(ck * P, ck * P + P))
        cp = lambda o, m, d, *w: dve.do(lambda e: e.copy_predicated(o, m, d), *w)
        gram = {}

        def gram_a(g):
            ck, h0 = g // 3, 4 * (g % 3)
            xi = fn(XIg(g), ident.unsqueeze(1).to_broadcast([P, 4, P]), ACT.Copy, K["kp"], in_done, [z_tok[16]] if g > 2 else None)
            for par in range(2):
                b = 4 + 2 * (g % 2) + par
                lst = []
                for k in range(2):
                    h = h0 + 2 * k + par
                    lst.append((ps[b][:, k * P:k * P + P], KK[H(h, ck)], AA[H(h, ck)], True, True))
                    lst.append((ps[b][:, T + k * P:T + k * P + P], AA[H(h, ck)], KK[H(h, ck)], True, True))
                t = emit(lst, bf[b], K["u", g % 3])
                pv = ps[b][:, :].rearrange("p (a k t) -> p a k t", a=2, k=2)
                tt(APg(g)[:, par::2, :], pv[:, 0, :, :], C(K_SL, P).unsqueeze(1).to_broadcast([P, 2, P]), ALU.mult, t, in_done)
                gram[g] = cp(XIg(g)[:, par::2, :], M_(K_M1).unsqueeze(1).to_broadcast([P, 2, P]), pv[:, 1, :, :], xi)
                bf[b] = [gram[g]]

        cut_ = lambda a, bl, w: a.rearrange("p (n two b) -> p n two b", two=2, b=bl)[:, :, w, :]
        xi_tok, ti_tok, qm_tok, inv_end = {}, {}, {}, []

        def inv_a(i):
            lv, g = divmod(i, 6)
            bl, k3, bT, bQ = 2 << lv, i % 3, i % 2, 2 + i % 2
            pe.wait(bf[bT], xi_tok.get(g, gram[g]))
            for k in range(4):
                f = lambda e: e.transpose(ps[bT][:, k * P:k * P + P], XI[:, 4 * g + k, :], ident)
                t = pe.do(f) if k == 3 else pe.go(f)
            ti_tok[i] = fn(TI[k3], ps[bT][:, :].rearrange("p (k t) -> p k t", k=4), ACT.Copy, t, slot.get(k3))
            bf[bT] = [ti_tok[i]]
            t = emit([(ps[bQ][:, 64 * k:64 * k + 64], APg(g)[:, k, :], cut_(XI[:, 4 * g + k, :], bl, 1), True, True)
                      for k in range(4)], bf[bQ])
            inv_end.append(t)
            qm_tok[i] = tt(Qm[k3], ps[bQ][:, 0:256].rearrange("p (k t) -> p k t", k=4),
                           C(K_LV + 64 * lv, 64).unsqueeze(1).to_broadcast([P, 4, 64]), ALU.mult, t, slot.get(k3))
            bf[bQ] = [qm_tok[i]]

        def inv_b(i):
            lv, g = divmod(i, 6)
            bl, k3, b = 2 << lv, i % 3, 4 + i % 2
            t = emit([(ps[b][:, 64 * k:64 * k + 64], TI[k3][:, k, :], Qm[k3][:, k, :], True, True) for k in range(4)],
                     bf[b], ti_tok[i], qm_tok[i])
            slot[k3] = t
            xo = cut_(XIg(g).rearrange("p m t -> p (m t)"), bl, 1)
            xi_tok[g] = tt(xo, xo, ps[b][:, 0:256].rearrange("p (n b) -> p n b", b=bl), ALU.add, t)
            bf[b] = [xi_tok[g]]

        khT, nbT, Xs = gc[:, 1536:2304], gc[:, 2304:3072], gc[:, 3072:3840]
        Us = [xf[:, 1, 1024:1024 + C7], ga[:, 0:C7]]
        NB = (4, 2)
        heads = lambda q: range(8 * q, 8 * q + 2 * NB[q])
        hcol = lambda h: slice(64 * (h % 8), 64 * (h % 8) + 64)
        wide = lambda a, q: a[:, 512 * q:512 * q + P * NB[q]]

        def g_bonus():
            K["k1"] = stt(Kk[:, :, :], BV[:, :, :], 1.0, Kk[:, :, :], ALU.add, ALU.mult, K["ka"], K["kk"])
            t = pool.do(lambda e: e.tensor_tensor(BV[:, :, :], Rr[:, :, :], VB("rwkv_r_k_2"), ALU.mult), K["k1"], z_tok[4])
            K["bo"] = pool.do(lambda e: e.tensor_tensor(BV[:, :, :], BV[:, :, :], Kk[:, :, :], ALU.mult), t)

        def g_hats():
            K["r"] = tt(Rr[:, :, :], Rr[:, :, :], w2, ALU.mult, K["e1"], K["bo"])
            K["kh"] = tt(Kk[:, :, :], Kk[:, :, :], w1, ALU.mult, K["bo"])
            free = [K["r"], K["kh"], K["u"], mo_tok]
            pool.do(lambda e: e.memset(BM[0][:, :, :], 0.0), free)
            K["zero0"] = pool.do(lambda e: e.memset(MR[0][:, :, :], 0.0), free)

        def g_bv(q):
            b = 6 + q % 2
            two_ = slice(2 * q, 2 * q + 2)
            t = emit([(ps[b][:, :], C(K_BO, P), BV[:, two_, :], True, True)], bf[b], K["bo"])
            t = tt(BV[:, two_, :], Vv[:, two_, :], pair(b), ALU.mult, t, z_tok[16])
            bf[b] = [t]
            for k in range(2):
                c = 2 * q + k
                K["bv"] = pool.do(lambda e: e.tensor_scalar(BV[:, c, :], BV[:, c, :], V("rwkv_lnx_b_2", c), None, ALU.add), t)

        def keep(name, f, *a):
            K.setdefault(name, []).append(f(*a))

        v_t = [turned(Vv, tb, Vtm[:, tb, :], (6, 7), None) for tb in range(2)]
        k_t = [turned(Kk, 0, khT, (6, 7), mo_tok), turned(AA, 0, nbT, (6, 7), mo_tok)]
        def gram_b(ck, g, par, b0=6):
            hs = (4 * g + par, 4 * g + 2 + par)
            la = [(ps[b0][:, (2 * k + j) * P:(2 * k + j + 1) * P], Kk[H(h, ck)], r[H(h, ck)], True, True)
                  for k, h in enumerate(hs) for j, r in enumerate((KK, Rr))]
            lb = [(ps[b0 + 1][:, k * P:k * P + P], AA[H(h, ck)], Rr[H(h, ck)], True, True) for k, h in enumerate(hs)]
            ta = emit(la, bf[b0], K["r"], K["kh"])
            tb_ = emit(lb, bf[b0 + 1])
            of = lambda a: a[:, hs[0]:hs[1] + 1:2, :]
            t = cp(of(BM[ck]), M_(K_SU, 2 * P).unsqueeze(1).to_broadcast([P, 2, 2 * P]),
                   ps[b0][:, :].rearrange("p (k t) -> p k t", k=2), ta, K["zero"][g] if ck else K["zero0"])
            bf[b0] = [t]
            t = cp(of(MR[ck]), M_(K_IU).unsqueeze(1).to_broadcast([P, 2, P]),
                   ps[b0 + 1][:, 0:T].rearrange("p (k t) -> p k t", k=2), tb_)
            bf[b0 + 1] = [t]
            K["bm"] = t

        def x_start(q):
            b = 6 + q
            t = emit([(ps[b][:, hcol(h)], BM[0][:, h, 0:P], Vtm[:, 0, 64 * h:64 * h + 64], True, True) for h in heads(q)],
                     bf[b], K["v"], K["bm"])
            t = fn(wide(Xs, q), ps[b][:, 0:P * NB[q]], ACT.Copy, t, mo_tok)
            bf[b] = [t]
            keep("x", lambda: t)

        fill = [g_bonus] + steps + [lambda: keep("v", v_t[0], 0), lambda: keep("v", v_t[0], 1), lambda: keep("v", v_t[1], 0),
                lambda: keep("v", v_t[1], 1), lambda: keep("nb_t", k_t[1], 0), lambda: keep("nb_t", k_t[1], 1), g_hats]
        fill += [lambda q=q: g_bv(q) for q in range(3)]
        fill += [lambda: keep("kh_t", k_t[0], 0), lambda: keep("kh_t", k_t[0], 1)]
        fill += [lambda g=g, par=par: gram_b(0, g, par) for g in range(3) for par in range(2)]
        fill += [lambda par=par: x_start(par) for par in range(2)]

        Z0 = junk[:, 0:C7].rearrange("p (c d) -> p c d", d=P)
        sqs = ga[:, C7:2 * C7]
        oc = Vv[:, :, :].rearrange("p c t -> p (c t)").rearrange("p (b n) -> p b n", b=2)
        x_t, u_t, y_tok, z_ok = {1: {}}, {0: {}, 1: {}}, [], []

        def state_of(b, q, k, side):
            c = 4 * q + k
            return ps[b][:, k * P:k * P + P], side[:, c, P:2 * P], Z0[:, c, :], True, False

        def x_of(q):
            b, lst = 2 + q, []
            for k in range(NB[q]):
                lst.append(state_of(b, q, k, KK))
                lst += [(ps[b][:, hcol(h)], BM[1][:, h, 0:P], Vtm[:, 1, 64 * h:64 * h + 64], False, h % 2 == 1)
                        for h in (8 * q + 2 * k, 8 * q + 2 * k + 1)]
            t = emit(lst, bf[b], K["bm"], z_ok)
            x_t[1][q] = fn(wide(Xs, q), ps[b][:, 0:P * NB[q]], ACT.Copy, t, K["u0"])
            bf[b] = [x_t[1][q]]

        def u_of(ck, q):
            b = (2 if ck else 6) + q
            t = emit([(ps[b][:, hcol(h)], XI[:, 12 * ck + h, :], Xs[:, 64 * h:64 * h + 64], True, True) for h in heads(q)],
                     bf[b], x_t[1][q] if ck else K["x"], [xi_tok[3 * ck + k] for k in range(3)])
            K[f"u{ck}"] = t
            u_t[ck][q] = fn(wide(Us[ck], q), ps[b][:, 0:P * NB[q]], ACT.Copy, t, inv_end[-1], K.get("u0"))
            bf[b] = [u_t[ck][q]]

        def z_of(q):
            b, n = 4 + q, NB[q]
            lst = []
            for k in range(n):
                s_ = slice((4 * q + k) * P, (4 * q + k + 1) * P)
                lst += [(ps[b][:, k * P:k * P + P], khT[:, s_], Vtm[:, 0, s_], True, False),
                        (ps[b][:, k * P:k * P + P], nbT[:, s_], Us[0][:, s_], False, True)]
            t = emit(lst, bf[b], K["kh_t"], K["nb_t"], u_t[0][q])
            for k in range(n):
                c = 4 * q + k
                z_ok.append(stt(Z0[:, c, :], ps[b][:, k * P:k * P + P], zsc[:, c:c + 1], C(K_BO, P), ALU.mult, ALU.mult, t,
                                K["zs"], slot[2]))
            K["z"] = t
            bf[b] = [z_ok[-1]]

        def o_of(ck, q, b):
            lst = []
            for h in heads(q):
                if ck and h % 2 == 0:
                    lst.append(state_of(b, q, h // 2 - 4 * q, Rr))
                v_ = Vtm[:, ck, 64 * h:64 * h + 64]
                lst.append((ps[b][:, hcol(h)], BM[ck][:, h, P:2 * P], v_, ck == 0, False))
                lst.append((ps[b][:, hcol(h)], MR[ck][:, h, :], Us[ck][:, 64 * h:64 * h + 64], False, True))
            K["o"] = K["o", ck, q] = emit(lst, bf[b], u_t[ck][q], K["bm"])

        def y_of(ck):
            hd = lambda a: a.rearrange("p (h d) -> p h d", d=64)
            N = lambda q: 2 * NB[q]
            bc = lambda a, q: a.unsqueeze(2).to_broadcast([P, N(q), 64])
            S = lambda k, q: st[:, 144 + 12 * k + 8 * q:144 + 12 * k + 8 * q + N(q)]
            oc3 = [hd(wide(oc[:, ck, :], q)) for q in range(2)]
            sq = [hd(wide(sqs, q)) for q in range(2)]
            t = {}
            for q in range(2):
                o3 = hd(ps[4 + q][:, 0:64 * N(q)])
                a = dve.do(lambda e: e.tensor_reduce(S(0, q), o3, AX.X, ALU.add), K["o", ck, q], K["bv"], K["v"])
                a = ts(S(0, q), S(0, q), 1.0 / 64, None, ALU.mult, ALU.bypass, a)
                a = tt(oc3[q], o3, bc(S(0, q), q), ALU.subtract, a)
                bf[4 + q] = [a]
                t[q] = fn(sq[q], oc3[q], ACT.Square, a, K["u0"])
            for q in range(2):
                a = dve.do(lambda e: e.tensor_reduce(S(1, q), sq[q], AX.X, ALU.add), t[q])
                t[q] = rstd_of(S(1, q), S(2, q), a, LNX_EPS, 1.0 / 64)
            for q in range(2):
                y_tok.append(tt(oc3[q], oc3[q], bc(S(2, q), q), ALU.mult, t[q]))

        gram_a(0)
        gram_a(1)
        NI = 36
        for i in range(NI + 2):
            if i < NI:
                inv_a(i)
            if i < 4:
                gram_a(i + 2)
            if i >= 2:
                inv_b(i - 2)
            if i >= 4 and fill:
                fill.pop(0)()
            if i >= NI:
                u_of(0, i - NI)
        for f in fill:
            f()
        used_up = [slot[0], slot[1], slot[2]]
        K["zero"] = {}
        for g in range(3):
            if g == 0:
                pool.do(lambda e: e.memset(MR[1][:, :, :], 0.0), used_up)
            K["zero"][g] = pool.do(lambda e: e.memset(BM[1][:, 4 * g:4 * g + 4, :], 0.0), used_up)

        gram_b(1, 0, 0, 0)
        gram_b(1, 0, 1, 2)
        z_of(0)
        gram_b(1, 1, 0, 0)
        z_of(1)
        gram_b(1, 1, 1, 2)
        gram_b(1, 2, 0, 6)
        gram_b(1, 2, 1, 2)
        gate = {}

        def gate_of(q):
            b = (2, 3, 2)[q]
            gate[q] = emit([(ps[b][:, hf[k]], gup[:, (2 * q + k) * P:(2 * q + k + 1) * P], DD[:, 1, :], True, True)
                            for k in range(2)], bf[b], K["dg"], up_tok)

        yh = nc.alloc_sbuf_tensor_at("ryh", [P, 6, T], F32R, offset=at1)
        yl = nc.alloc_sbuf_tensor_at("ryl", [P, 6, T], F32R, offset=at2)
        ym = nc.alloc_sbuf_tensor_at("rym", [P, 4, T], F32R, offset=at3 + 4 * 1536)
        yT = {}
        yT[6] = yT[7] = split_evac(mo[:, :, :], ym[:, 0:2, :], ym[:, 2:4, :], mo_tok, K["z"])

        def second_half():
            o_of(0, 0, 4)
            x_of(0)
            x_of(1)
            o_of(0, 1, 5)
            u_of(1, 0)
            u_of(1, 1)
            y_of(0)
            gate_of(0)
            o_of(1, 0, 4)
            o_of(1, 1, 5)
            y_of(1)
            probe("oc", oc, y_tok)
            gfree[0] = gfree[1] = K["o"]

        def y_turned():
            for q in range(3):
                b, bg = (4, 5, 4)[q], (2, 3, 2)[q]
                if q == 1:
                    gate_of(q)
                pe.wait(bf[b], y_tok)
                for k in range(2):
                    for ck in range(2):
                        f = lambda e: e.transpose(ps[b][:, k * T + ck * P:k * T + ck * P + P],
                                                  oc[:, ck, (2 * q + k) * P:(2 * q + k + 1) * P], ident)
                        t = pe.do(f) if (k, ck) == (1, 1) else pe.go(f)
                if q == 2:
                    gate_of(q)
                two_ = slice(2 * q, 2 * q + 2)
                d = [stt(Kk[:, 2 * q + k, :], ps[b][:, hf[k]], V("rwkv_lnx_g_2", 2 * q + k), BV[:, 2 * q + k, :],
                         ALU.mult, ALU.add, t) for k in range(2)]
                bf[b] = d
                t = tt(Kk[:, two_, :], Kk[:, two_, :], pair(bg), ALU.mult, d, gate[q])
                bf[bg] = [t]
                yT[2 * q] = yT[2 * q + 1] = split_evac(Kk[:, two_, :], yh[:, two_, :], yl[:, two_, :], t)

        t = mm_d("wo0", each(yh, 6) + each(ym, 2), each(yl, 6) + each(ym, 4)[2:], yT, 8, {1: second_half, 2: y_turned}, LATE)
        xt, mid = turn_to(x)
        rest = ln_add(t, 1.0, xa, *norm_of(0, 1), mid)
        s1.close()
        rs.close()

        rest, xt = half_ffn("f2", 0, 2, rest, xt)
        rest, xt = half_ffn("f3", 1, 0, rest, xt)

        rs = ExitStack()
        ra = lambda nm, sh, d=F32: rs.enter_context(nc.sbuf_tensor("b" + nm, sh, d))
        yh, yl = ra("yh", [P, 8, T], F32R), ra("yl", [P, 8, T], F32R)
        qT, kT = ra("qT", [P, 6, T]), ra("kT", [P, 6, T])
        mqT, mo = ra("mq", [P, 2, T]), ra("mo", [P, 2, T])
        vt = ra("vt", [P, 2, C7])
        m3, m3n = ra("m3", [P, 384]), ra("m3n", [P, 384])
        NS, FIRST = 8, 5
        sa, sw = (ra(n, [P, NS, 384]) for n in ("sa", "sw"))
        pbm, pTm = ra("pbm", [P, 4, 2, T]), ra("pTm", [P, 2, 2, T])
        xa = []

        def start():
            rest()
            xa.append(scale_x(xt[0], xt[1]))

        xk = xt[0]
        gb_ = norm_of(1, 1)
        m_tok = [pool.do(lambda e, o=o, k=k: e.tensor_copy(m3[:, o:o + P], C(k, P)), xk)
                 for o, k in ((0, K_SU), (P, K_ONE), (2 * P, K_SU))]
        m_tok = [pool.do(lambda e: e.tensor_scalar(m3n[:, :], m3[:, :], -1.0, None, ALU.mult), m_tok)]
        q_tok, k_tok, v_tok3, mq_tok = {}, {}, [], []

        free_s = {}
        att_tok, w_tok2, lk_tok = {}, {}, {}

        def sb_scores(h):
            s, b = h % NS, 4 + h % 2
            o, c = slice(64 * (h % 2), 64 * (h % 2) + 64), h // 2
            z = ps[b][:, 0:384]
            t = emit([(ps[b][:, 0:T], kT[o, c, 0:P], qT[o, c, :], True, True),
                      (ps[b][:, T:384], kT[o, c, P:T], qT[o, c, P:T], True, True)], bf[b], q_tok[c // 2], k_tok[c // 2])
            t = fn(sa[:, s, :], z, ACT.Abs, t, free_s.get(s))
            t = fn(sa[:, s, :], sa[:, s, :], ACT.Exp, t, scale=-1.0)
            t = fn(sa[:, s, :], sa[:, s, :], ACT.Ln, t, bias=1.0)
            t = stt(sa[:, s, :], z, 0.0, sa[:, s, :], ALU.max, ALU.add, t)
            w_tok2[h] = tt(sw[:, s, :], z, sa[:, s, :], ALU.subtract, t, free_s.get(s))
            bf[b] = [w_tok2[h]]
            lk_tok[h] = pool.do(lambda e: e.tensor_tensor(sa[:, s, :], sa[:, s, :], m3n[:, :], ALU.mult), w_tok2[h], m_tok)

        def sb_later(h):
            s, b = h % NS, 6 + h % 2 if h < FIRST else 2
            tri, one = C(K_SL, P), C(K_ONE, P)
            t = emit([(ps[b][:, 0:T], tri, sa[:, s, 0:T], True, False),
                      (ps[b][:, P:T], one, sa[:, s, T:384], False, True),
                      (ps[b][:, T:384], tri, sa[:, s, T:384], True, True)], bf[b], lk_tok[h])
            t = tt(sw[:, s, :], sw[:, s, :], ps[b][:, 0:384], ALU.add, t, w_tok2[h])
            bf[b] = [t]
            t = fn(sw[:, s, :], sw[:, s, :], ACT.Exp, t)
            att_tok[h] = pool.do(lambda e: e.tensor_tensor(sw[:, s, :], sw[:, s, :], m3[:, :], ALU.mult), t)

        yT = {}

        def sb_out(c):
            b = 3
            lst = []
            for k in range(2):
                s = (2 * c + k) % NS
                lst += [(ps[b][:, k * T:k * T + T], vt[:, 0, c * P:c * P + P], sw[:, s, 0:T], True, False),
                        (ps[b][:, k * T + P:k * T + T], vt[:, 1, c * P:c * P + P], sw[:, s, T:384], False, True)]
            t = emit(lst, bf[b], att_tok[2 * c], att_tok[2 * c + 1], v_tok3)
            for k in range(2):
                free_s[(2 * c + k) % NS] = t
            for k in range(2):
                o = slice(64 * k, 64 * k + 64)
                yT[c] = split_evac(ps[b][o, k * T:k * T + T], yh[o, c, :], yl[o, c, :], t)
            bf[b] = [yT[c]]

        def v_chunk(c, n0, w, banks, **how):
            t = mm_x("sb", n0, xh, xl, xt, banks, **how)
            for rb in range(2):
                b = banks[rb]
                t2 = fn(vt[:, rb, 512 * c:512 * c + w], ps[b][:, 0:w], ACT.Copy, t[rb])
                bf[b] = [t2]
                v_tok3.append(t2)

        v_chunk(0, 1536, 512, (0, 1), lead=3, mid=start)
        def qk_chunk(n0, b, side=None):
            src, j = ps[b][:, :].rearrange("p (k t) -> p k t", k=2), n0 // P

            def end(t):
                if j < 6:
                    t2 = q_tok[j // 2] = fn(qT[:, j:j + 2, :], src, ACT.Copy, t, scale=0.125)
                else:
                    t2 = k_tok[j // 2 - 3] = fn(kT[:, j - 6:j - 4, :], src, ACT.Copy, t)
                bf[b] = [t2]

            mm_w("sb", n0, xh, xl, xt, (b,), side=side, end=end)

        def run(*todo):
            return lambda: [f(*a) for f, *a in todo]

        S, L, O = sb_scores, sb_later, sb_out
        qk_chunk(0, 2)
        qk_chunk(768, 3)
        act.go(lambda e: e.preload_act_table_set("natural_log_exp_and_others"))
        side = [run(), run((S, 0)), run((S, 1)), run((S, 2))]
        t = mm_w("sb", 2304, xh, xl, xt, (0,), side=side)
        mq_tok.append(fn(mqT[:, :, :], ps[0][:, :].rearrange("p (k t) -> p k t", k=2), ACT.Copy, t))
        bf[0] = mq_tok[:]
        mo_tok, M = mem_attn(mqT, mq_tok, mo, pbm, pTm, (6, 7), (0, 1), (0, 1))
        side += [run((S, 3)), run((M[0],)), run((S, 4), (L, 0)), run((S, 5), (L, 1)), run((M[1],), (L, 2)),
                 run((M[2],), (L, 3)), run((S, 6), (M[3],)), run((S, 7), (O, 0))]
        qk_chunk(256, 1, side)
        qk_chunk(1024, 2, side)
        qk_chunk(512, 3, side)
        qk_chunk(1280, 0, side)
        v_chunk(1, 2048, 256, (1, 2), side=side)
        run((M[4],), (L, 4), (M[5],), (M[6],), (O, 1), (M[7],), (M[8],), (M[9],), (M[10],), (M[11],))()
        yT[6] = yT[7] = split_evac(mo[:, :, :], yh[:, 6:8, :], yl[:, 6:8, :], mo_tok)
        t = mm_d("wo1", each(yh), each(yl), yT, 8, {
            0: run((S, 8), (L, 5), (S, 9)), 1: run((L, 6), (S, 10)), 2: run((O, 2), (L, 7), (S, 11)),
            3: run((L, 8), (O, 3), (L, 9)), 4: run((L, 10), (O, 4), (L, 11)), 6: run((O, 5))}, LATE)
        probe("headsT1", yh[:, :, :].bitcast(F32), yT[6], yT[5])
        xt, mid = turn_to(x)
        rest = ln_add(t, 1.0, xa, *gb_, mid)
        rs.close()

        s_out = Dmas(sem("s_out"))
        gone = []

        def store(rb, toks, between=None):
            if between is not None:
                between()
            gone.append(s_out.start(sp, out[0, rb * P:rb * P + P, :], x[:, rb, :], toks))

        rest, _ = half_ffn("f4", 1, 2, rest, xt, store)
        rest()
        sp.wait(gone)
        assert used[0] == NU, (used[0], NU)


def constants():
    c = np.zeros((P, NCST), np.float32)
    i, j = np.arange(P)[:, None], np.arange(P)[None, :]
    c[:, K_ID:K_ID + P] = i == j
    c[:, K_AM:K_AM + P] = c[:, K_AM + 2 * P:K_AM + 3 * P] = np.where(j > i, np.float32(NEG), np.float32(0))
    c[:, K_SU:K_SU + P] = i < j
    c[:, K_IU:K_IU + P] = i <= j
    c[:, K_M1:K_M1 + P] = (j == i + 1) & (i % 2 == 0)
    c[:, K_SL:K_SL + P] = i > j
    for lv in range(6):
        b = 2 << lv
        odd = (np.arange(64) // b) * 2 * b + b + np.arange(64) % b
        row = np.arange(P)[:, None]
        c[:, K_LV + 64 * lv:K_LV + 64 * lv + 64] = (row // (2 * b) == odd[None, :] // (2 * b)) & (row // b % 2 == 0)
    c[:, K_ONE:K_ONE + P] = 1
    c[:, K_SEL2:K_SEL2 + 2] = i // 64 == np.arange(2)[None, :]
    c[:, K_FREQ:K_FREQ + 8] = np.float32(500000.0) ** (-np.arange(0, 16, 2, dtype=np.float32) / np.float32(16))
    c[:, K_BO:K_BO + P] = i // 64 == j // 64
    f = np.arange(C7)[None, :]
    c[0:12, K_SELH:K_SELH + C7] = np.arange(12)[:, None] == f // 64
    s = np.arange(T)[:, None, None]
    w = np.array([2, 4, 8, 16])[None, :, None]
    t = np.arange(T)[None, None, :]
    band = np.where((s <= t) & (s > t - w), np.float32(1) / np.minimum(t + 1, w).astype(np.float32), np.float32(0))
    band = (band - (s == t)).astype(np.float32)
    band = band.reshape(2, P, 4, T).transpose(1, 0, 2, 3).reshape(P, 8 * T)
    return c, np.ascontiguousarray(band)


NAMES = [
    "x", "mem", "positions", "g_mix_pre", "w_in", "lambda_q1", "lambda_k1", "lambda_q2", "lambda_k2", "g_subln",
    "w_pool", "pool_scale", "w_out", "g_mix_post", "g_x_pre", "g_mem", "w_xq", "w_xkv", "w_xo", "g_x_post",
    "g_ffn_pre", "w_gate", "w_up", "w_down", "g_ffn_post", "mem_2", "ffn1_w_gate_2", "ffn1_w_up_2",
    "ffn1_w_down_2", "ffn2_w_gate_2", "ffn2_w_up_2", "ffn2_w_down_2", "ln_g_2", "ln_b_2", "w_out_2",
    "w_mem_kv_2", "rwkv_w_in_2", "rwkv_mu_2", "rwkv_w0_2", "rwkv_w_up_2", "rwkv_a0_2", "rwkv_a_up_2",
    "rwkv_g_up_2", "rwkv_k_k_2", "rwkv_k_a_2", "rwkv_r_k_2", "rwkv_lnx_g_2", "rwkv_lnx_b_2", "sb_w_in_2",
]


def kernel(**inputs):
    import concourse.bacc as bacc
    from concourse.bass_utils import run_bass_kernel_spmd

    nc = bacc.Bacc("TRN2", target_bir_lowering=False, num_devices=1)
    arrays, args = {}, {}
    for name in NAMES:
        a = np.ascontiguousarray(inputs[name])
        arrays["in_" + name] = a
        args[name] = nc.dram_tensor("in_" + name, a.shape, mybir.dt.from_np(a.dtype), kind="ExternalInput").ap()
    consts = []
    for name, a in zip(("c_tables", "c_band"), constants()):
        arrays[name] = a
        consts.append(nc.dram_tensor(name, a.shape, F32, kind="ExternalInput").ap())
    out = nc.dram_tensor("out_x", (1, T, D), F32, kind="ExternalOutput").ap()
    build_program(nc, args, consts[0], consts[1], out)
    r = run_bass_kernel_spmd(nc, [arrays], core_ids=[0])
    return r.results[0]["out_x"]
```
